# Optimizing a Trainium2 kernel written in Bass

```python
import jax, jax.numpy as jnp
from jax import lax
import numpy as np
import math

D_MODEL = 1024
BATCH = 1
SEQ = 256
DEPTH = 2

HEAD_DIM = 64
GROUP_WIDTH = D_MODEL // 2
GROUP_HEADS = GROUP_WIDTH // HEAD_DIM
RW_HEADS = GROUP_HEADS
RW_DIM = GROUP_WIDTH
DECAY_LORA = 64
AAA_LORA = 64
GATE_LORA = 128
RW_GN_EPS = 64e-5
MLA_HEADS = GROUP_HEADS
MLA_NOPE = HEAD_DIM
MLA_ROPE = HEAD_DIM // 2
MLA_V = HEAD_DIM
MLA_Q_RANK = D_MODEL // 4
MLA_KV_RANK = D_MODEL // 8
FOX_HEADS = GROUP_HEADS
FOX_DIM = GROUP_WIDTH
MOBA_HEADS = GROUP_HEADS
MOBA_DIM = GROUP_WIDTH
MOBA_BLOCK = 256
MOBA_TOPK = 3
MOBA_Q_CHUNK = 32
Q_BLOCK = 128
ROPE_THETA = 10000.0
NORM_EPS = 1e-6
D_FF = 256 * ((8 * D_MODEL // 3 + 255) // 256)
N_EXPERTS = 8
TOP_K = 2
D_EXPERT = 7 * D_MODEL // 2

RW_SIZES = (RW_DIM, RW_DIM, RW_DIM, DECAY_LORA, AAA_LORA, GATE_LORA)
RW_COLS = sum(RW_SIZES)
MLA_SIZES = (MLA_Q_RANK, MLA_KV_RANK, MLA_ROPE)
IN0_COLS = RW_COLS + sum(MLA_SIZES)
FOX_SIZES = (FOX_DIM, FOX_DIM, FOX_DIM, FOX_HEADS)
FOX_COLS = sum(FOX_SIZES)
MOBA_SIZES = (MOBA_DIM, MOBA_DIM, MOBA_DIM)
IN1_COLS = FOX_COLS + sum(MOBA_SIZES)
MIX0_OUT = RW_DIM + MLA_HEADS * MLA_V
MIX1_OUT = FOX_DIM + MOBA_DIM


def split_cols(t, sizes):
    return jnp.split(t, [int(i) for i in np.cumsum(sizes)[:-1]], axis=-1)

def to_heads(t, n_heads):
    b, s, _ = t.shape
    return t.reshape(b, s, n_heads, -1)

def rmsnorm(x, g, eps=NORM_EPS):
    xf = x.astype(jnp.float32)
    xf = xf * lax.rsqrt(jnp.mean(xf * xf, axis=-1, keepdims=True) + eps)
    return (xf * g.astype(jnp.float32)).astype(x.dtype)

def rope_tables(seq_len, dim):
    inv_freq = ROPE_THETA ** (-jnp.arange(0, dim, 2, dtype=jnp.float32) / dim)
    ang = jnp.arange(seq_len, dtype=jnp.float32)[:, None] * inv_freq[None, :]
    return jnp.cos(ang), jnp.sin(ang)

def apply_rope(x, cos_r, sin_r):
    xf = x.astype(jnp.float32)
    x1, x2 = jnp.split(xf, 2, axis=-1)
    c, s = cos_r[:, None, :], sin_r[:, None, :]
    return jnp.concatenate([x1 * c - x2 * s, x2 * c + x1 * s], axis=-1).astype(x.dtype)

def swiglu(t, w_gate, w_up, w_down):
    return (jax.nn.silu(t @ w_gate) * (t @ w_up)) @ w_down

def block_causal_attention(q, k, v, scale, log_decay_cum=None):
    b, h, s, _ = q.shape
    k_pos = jnp.arange(s)

    def one_block(i):
        start = i * Q_BLOCK
        qb = lax.dynamic_slice_in_dim(q, start, Q_BLOCK, axis=2)
        logits = jnp.einsum('bhqd,bhkd->bhqk', qb, k).astype(jnp.float32) * scale
        q_pos = start + jnp.arange(Q_BLOCK)
        if log_decay_cum is not None:
            dq = lax.dynamic_slice_in_dim(log_decay_cum, start, Q_BLOCK, axis=2)
            logits = logits + dq[..., :, None] - log_decay_cum[..., None, :]
        logits = jnp.where(k_pos[None, :] <= q_pos[:, None], logits, -jnp.inf)
        p = jax.nn.softmax(logits, axis=-1).astype(v.dtype)
        return jnp.einsum('bhqk,bhkd->bhqd', p, v)

    out = lax.map(one_block, jnp.arange(s // Q_BLOCK))
    return out.transpose(1, 2, 0, 3, 4).reshape(b, h, s, -1)

def rwkv7_time_mix(r, k, v, w_down, a_down, g_down, w0, w2, a0, a2, g2,
                   k_k, k_a, r_k, lnx_g, lnx_b):
    out_dtype = r.dtype
    f32 = jnp.float32
    r, k, v, w_down, a_down, g_down = (t.astype(f32) for t in (r, k, v, w_down, a_down, g_down))
    b, s, c = r.shape
    h, n = RW_HEADS, HEAD_DIM
    log_w = -jax.nn.softplus(-(w0 + jnp.tanh(w_down) @ w2)) - 0.5
    decay = jnp.exp(-jnp.exp(log_w))
    a = jax.nn.sigmoid(a0 + a_down @ a2)
    g = jax.nn.sigmoid(g_down) @ g2
    kk = (k * k_k).reshape(b, s, h, n)
    kk = kk / jnp.maximum(jnp.linalg.norm(kk, axis=-1, keepdims=True), 1e-12)
    k = k * (1.0 + (a - 1.0) * k_a)
    r_h, w_h, k_h, v_h, a_h = (t.reshape(b, s, h, n) for t in (r, decay, k, v, a))
    b_h = kk * a_h
    xs = tuple(jnp.moveaxis(t, 1, 0) for t in (r_h, w_h, k_h, v_h, kk, b_h))

    def step(state, inp):
        r_t, w_t, k_t, v_t, kk_t, b_t = inp
        sa = jnp.einsum('bhvk,bhk->bhv', state, -kk_t)
        state = (state * w_t[:, :, None, :] + sa[..., None] * b_t[:, :, None, :]
                 + v_t[..., None] * k_t[:, :, None, :])
        return state, jnp.einsum('bhvk,bhk->bhv', state, r_t)

    state0 = jnp.zeros((b, h, n, n), f32)
    _, y = lax.scan(step, state0, xs)
    y = jnp.moveaxis(y, 0, 1)
    mu = jnp.mean(y, axis=-1, keepdims=True)
    var = jnp.mean(jnp.square(y - mu), axis=-1, keepdims=True)
    y = ((y - mu) * lax.rsqrt(var + RW_GN_EPS)).reshape(b, s, c) * lnx_g + lnx_b
    bonus = jnp.sum(r_h * k_h * r_k, axis=-1, keepdims=True) * v_h
    y = (y + bonus.reshape(b, s, c)) * g
    return y.astype(out_dtype)

def mla_attention(q_lat, kv_lat, k_rope, q_norm, w_uq, kv_norm, w_ukv, cos_r, sin_r):
    b, s, _ = q_lat.shape
    h = MLA_HEADS
    q = to_heads(rmsnorm(q_lat, q_norm) @ w_uq, h)
    q_nope, q_pe = q[..., :MLA_NOPE], apply_rope(q[..., MLA_NOPE:], cos_r, sin_r)
    kv = to_heads(rmsnorm(kv_lat, kv_norm) @ w_ukv, h)
    k_nope, v = kv[..., :MLA_NOPE], kv[..., MLA_NOPE:]
    k_pe = apply_rope(k_rope[:, :, None, :], cos_r, sin_r)
    q = jnp.concatenate([q_nope, q_pe], axis=-1)
    k = jnp.concatenate([k_nope, jnp.broadcast_to(k_pe, (b, s, h, MLA_ROPE))], axis=-1)
    out = block_causal_attention(q.transpose(0, 2, 1, 3), k.transpose(0, 2, 1, 3),
                                 v.transpose(0, 2, 1, 3), (MLA_NOPE + MLA_ROPE) ** -0.5)
    return out.transpose(0, 2, 1, 3).reshape(b, s, h * MLA_V)

def forgetting_attention(q, k, v, f_logit, b_f):
    b, s, _ = q.shape
    h = FOX_HEADS
    log_f = jax.nn.log_sigmoid(f_logit.astype(jnp.float32) + b_f.astype(jnp.float32))
    d_cum = jnp.cumsum(log_f, axis=1).transpose(0, 2, 1)
    qh, kh, vh = (to_heads(t, h).transpose(0, 2, 1, 3) for t in (q, k, v))
    out = block_causal_attention(qh, kh, vh, HEAD_DIM ** -0.5, d_cum)
    return out.transpose(0, 2, 1, 3).reshape(b, s, h * HEAD_DIM)

def moba_attention(q, k, v, cos_r, sin_r):
    b, s, _ = q.shape
    h, d = MOBA_HEADS, HEAD_DIM
    qh = apply_rope(to_heads(q, h), cos_r, sin_r).transpose(0, 2, 1, 3)
    kh = apply_rope(to_heads(k, h), cos_r, sin_r).transpose(0, 2, 1, 3)
    vh = to_heads(v, h).transpose(0, 2, 1, 3)
    nb = -(-s // MOBA_BLOCK)
    pad = nb * MOBA_BLOCK - s
    kp = jnp.pad(kh, ((0, 0), (0, 0), (0, pad), (0, 0)))
    vp = jnp.pad(vh, ((0, 0), (0, 0), (0, pad), (0, 0)))
    k_blocks = kp.reshape(b, h, nb, MOBA_BLOCK, d)
    v_blocks = vp.reshape(b, h, nb, MOBA_BLOCK, d)
    k_mean = jnp.mean(k_blocks.astype(jnp.float32), axis=3).astype(kh.dtype)
    n_sel = min(MOBA_TOPK, nb)
    n_sel_keys = n_sel * MOBA_BLOCK
    scale = d ** -0.5
    b_idx = jnp.arange(b)[:, None, None, None]
    h_idx = jnp.arange(h)[None, :, None, None]
    blk_ids = jnp.arange(nb)
    offs = jnp.arange(MOBA_BLOCK)

    def one_chunk(i):
        start = i * MOBA_Q_CHUNK
        qc = lax.dynamic_slice_in_dim(qh, start, MOBA_Q_CHUNK, axis=2)
        q_pos = start + jnp.arange(MOBA_Q_CHUNK)
        own = start // MOBA_BLOCK
        gate = jnp.einsum('bhqd,bhnd->bhqn', qc, k_mean).astype(jnp.float32)
        gate = jnp.where(blk_ids < own, gate, -jnp.inf)
        _, sel = lax.top_k(gate, n_sel)
        sel_valid = sel < own
        k_sel = k_blocks[b_idx, h_idx, sel]
        v_sel = v_blocks[b_idx, h_idx, sel]
        s_sel = jnp.einsum('bhqd,bhqjld->bhqjl', qc, k_sel).astype(jnp.float32) * scale
        s_sel = jnp.where(sel_valid[..., None], s_sel, -jnp.inf)
        k_own = lax.dynamic_slice_in_dim(kp, own * MOBA_BLOCK, MOBA_BLOCK, axis=2)
        v_own = lax.dynamic_slice_in_dim(vp, own * MOBA_BLOCK, MOBA_BLOCK, axis=2)
        s_own = jnp.einsum('bhqd,bhld->bhql', qc, k_own).astype(jnp.float32) * scale
        s_own = jnp.where((own * MOBA_BLOCK + offs)[None, :] <= q_pos[:, None], s_own, -jnp.inf)
        logits = jnp.concatenate([s_sel.reshape(b, h, MOBA_Q_CHUNK, n_sel_keys), s_own], axis=-1)
        p = jax.nn.softmax(logits, axis=-1).astype(vh.dtype)
        p_sel = p[..., :n_sel_keys].reshape(b, h, MOBA_Q_CHUNK, n_sel, MOBA_BLOCK)
        p_own = p[..., n_sel_keys:]
        return (jnp.einsum('bhqjl,bhqjld->bhqd', p_sel, v_sel)
                + jnp.einsum('bhql,bhld->bhqd', p_own, v_own))

    out = lax.map(one_chunk, jnp.arange(s // MOBA_Q_CHUNK))
    out = out.transpose(1, 2, 0, 3, 4).reshape(b, h, s, d)
    return out.transpose(0, 2, 1, 3).reshape(b, s, h * d)

def moe_swiglu(t, router, w_gate, w_up, w_down):
    logits = (t @ router).astype(jnp.float32)
    top_logits, top_idx = lax.top_k(logits, TOP_K)
    gates = jax.nn.softmax(top_logits, axis=-1)
    combine = jnp.sum(jax.nn.one_hot(top_idx, N_EXPERTS, dtype=jnp.float32) * gates[..., None], axis=1)
    out = jnp.zeros_like(t)
    for e in range(N_EXPERTS):
        out = out + combine[:, e:e + 1].astype(t.dtype) * swiglu(t, w_gate[e], w_up[e], w_down[e])
    return out

def even_layer(h, norm_mix, w_in, shift_mu, rw_w0, rw_w2, rw_a0, rw_a2, rw_g2, rw_kk, rw_ka,
               rw_rk, rw_lnx_g, rw_lnx_b, mla_qnorm, mla_wuq, mla_kvnorm, mla_wukv, w_out,
               norm_ffn, ffn_wg, ffn_wu, ffn_wd, cos_r, sin_r):
    u = rmsnorm(h, norm_mix)
    proj = u @ w_in
    rw_cols, mla_cols = proj[..., :RW_COLS], proj[..., RW_COLS:]
    rw_prev = jnp.pad(rw_cols[:, :-1], ((0, 0), (1, 0), (0, 0)))
    rw_cols = rw_cols + shift_mu * (rw_prev - rw_cols)
    y_a = rwkv7_time_mix(*split_cols(rw_cols, RW_SIZES), rw_w0, rw_w2, rw_a0, rw_a2, rw_g2,
                         rw_kk, rw_ka, rw_rk, rw_lnx_g, rw_lnx_b)
    y_b = mla_attention(*split_cols(mla_cols, MLA_SIZES), mla_qnorm, mla_wuq, mla_kvnorm,
                        mla_wukv, cos_r, sin_r)
    h = h + jnp.concatenate([y_a, y_b], axis=-1) @ w_out
    return h + swiglu(rmsnorm(h, norm_ffn), ffn_wg, ffn_wu, ffn_wd)

def odd_layer(h, norm_mix, w_in, fox_bf, w_out, norm_ffn, router, moe_wg, moe_wu, moe_wd,
              cos_r, sin_r):
    b, s, d = h.shape
    u = rmsnorm(h, norm_mix)
    proj = u @ w_in
    fox_cols, moba_cols = proj[..., :FOX_COLS], proj[..., FOX_COLS:]
    y_c = forgetting_attention(*split_cols(fox_cols, FOX_SIZES), fox_bf)
    y_d = moba_attention(*split_cols(moba_cols, MOBA_SIZES), cos_r, sin_r)
    h = h + jnp.concatenate([y_c, y_d], axis=-1) @ w_out
    t = rmsnorm(h, norm_ffn).reshape(b * s, d)
    return h + moe_swiglu(t, router, moe_wg, moe_wu, moe_wd).reshape(b, s, d)

def first_inputs(seed: int = 0) -> dict:
    key = jax.random.key(seed)
    ks = iter(jax.random.split(key, 40))
    D = D_MODEL

    def nrm(shape, scale):
        return scale * jax.random.normal(next(ks), shape, jnp.float32)

    def gain(n):
        return 1.0 + nrm((n,), 0.05)

    return {
        'x': nrm((BATCH, SEQ, D), 1.0),
        'norm_mix_0': gain(D),
        'w_in_0': nrm((D, IN0_COLS), D ** -0.5),
        'shift_mu_0': jax.random.uniform(next(ks), (RW_COLS,), jnp.float32, 0.2, 0.8),
        'rw_w0_0': jax.random.uniform(next(ks), (RW_DIM,), jnp.float32, -6.0, -1.0),
        'rw_w2_0': nrm((DECAY_LORA, RW_DIM), DECAY_LORA ** -0.5),
        'rw_a0_0': nrm((RW_DIM,), 0.1),
        'rw_a2_0': nrm((AAA_LORA, RW_DIM), AAA_LORA ** -0.5),
        'rw_g2_0': nrm((GATE_LORA, RW_DIM), GATE_LORA ** -0.5),
        'rw_kk_0': 0.85 + nrm((RW_DIM,), 0.05),
        'rw_ka_0': 1.0 + nrm((RW_DIM,), 0.05),
        'rw_rk_0': nrm((RW_HEADS, HEAD_DIM), 0.1),
        'rw_lnx_g_0': gain(RW_DIM),
        'rw_lnx_b_0': nrm((RW_DIM,), 0.02),
        'mla_qnorm_0': gain(MLA_Q_RANK),
        'mla_wuq_0': nrm((MLA_Q_RANK, MLA_HEADS * (MLA_NOPE + MLA_ROPE)), MLA_Q_RANK ** -0.5),
        'mla_kvnorm_0': gain(MLA_KV_RANK),
        'mla_wukv_0': nrm((MLA_KV_RANK, MLA_HEADS * (MLA_NOPE + MLA_V)), MLA_KV_RANK ** -0.5),
        'w_out_0': nrm((MIX0_OUT, D), MIX0_OUT ** -0.5),
        'norm_ffn_0': gain(D),
        'ffn_wg_0': nrm((D, D_FF), D ** -0.5),
        'ffn_wu_0': nrm((D, D_FF), D ** -0.5),
        'ffn_wd_0': nrm((D_FF, D), D_FF ** -0.5),
        'norm_mix_1': gain(D),
        'w_in_1': nrm((D, IN1_COLS), D ** -0.5),
        'fox_bf_1': 3.0 + nrm((FOX_HEADS,), 0.5),
        'w_out_1': nrm((MIX1_OUT, D), MIX1_OUT ** -0.5),
        'norm_ffn_1': gain(D),
        'router_1': nrm((D, N_EXPERTS), D ** -0.5),
        'moe_wg_1': nrm((N_EXPERTS, D, D_EXPERT), D ** -0.5),
        'moe_wu_1': nrm((N_EXPERTS, D, D_EXPERT), D ** -0.5),
        'moe_wd_1': nrm((N_EXPERTS, D_EXPERT, D), D_EXPERT ** -0.5),
        'final_norm': gain(D),
    }

def first_block(x, norm_mix_0, w_in_0, shift_mu_0, rw_w0_0, rw_w2_0, rw_a0_0, rw_a2_0, rw_g2_0,
              rw_kk_0, rw_ka_0, rw_rk_0, rw_lnx_g_0, rw_lnx_b_0, mla_qnorm_0, mla_wuq_0,
              mla_kvnorm_0, mla_wukv_0, w_out_0, norm_ffn_0, ffn_wg_0, ffn_wu_0, ffn_wd_0,
              norm_mix_1, w_in_1, fox_bf_1, w_out_1, norm_ffn_1, router_1, moe_wg_1, moe_wu_1,
              moe_wd_1, final_norm):
    seq_len = x.shape[1]
    rope_mla = rope_tables(seq_len, MLA_ROPE)
    rope_full = rope_tables(seq_len, HEAD_DIM)
    layer_params = (
        (norm_mix_0, w_in_0, shift_mu_0, rw_w0_0, rw_w2_0, rw_a0_0, rw_a2_0, rw_g2_0, rw_kk_0,
         rw_ka_0, rw_rk_0, rw_lnx_g_0, rw_lnx_b_0, mla_qnorm_0, mla_wuq_0, mla_kvnorm_0,
         mla_wukv_0, w_out_0, norm_ffn_0, ffn_wg_0, ffn_wu_0, ffn_wd_0),
        (norm_mix_1, w_in_1, fox_bf_1, w_out_1, norm_ffn_1, router_1, moe_wg_1, moe_wu_1,
         moe_wd_1),
    )
    h = x
    for layer in range(DEPTH):
        if layer % 2 == 0:
            h = even_layer(h, *layer_params[layer], *rope_mla)
        else:
            h = odd_layer(h, *layer_params[layer], *rope_full)
    return rmsnorm(h, final_norm)


D_MIX = D_MODEL
N_HEADS_TOTAL = D_MIX // HEAD_DIM
N_HEADS_DIL = N_HEADS_TOTAL // 2
N_LRU_BLOCKS = N_HEADS_TOTAL // 4
N_HEADS_SB = N_HEADS_TOTAL // 4
W_DIL = N_HEADS_DIL * HEAD_DIM
W_LRU = N_LRU_BLOCKS * HEAD_DIM
W_SB = N_HEADS_SB * HEAD_DIM
D_IN = 4 * W_DIL + 2 * W_LRU + 4 * W_SB
ROPE_DIM = HEAD_DIM // 4
ROPE_THETA_2 = 500000.0
DILATED_PATTERNS = ((128, 1), (512, 4), (2048, 16))
CONV_WIDTH = 4
LRU_C = 8.0
EPS = 1e-6


def _in_split_points():
    sizes = [W_DIL] * 4 + [W_LRU] * 2 + [W_SB] * 4
    points, acc = [], 0
    for s in sizes[:-1]:
        acc += s
        points.append(acc)
    return points

def rms_norm(x, gain):
    xf = x.astype(jnp.float32)
    xf = xf * lax.rsqrt(jnp.mean(xf * xf, axis=-1, keepdims=True) + EPS)
    return (xf * gain.astype(jnp.float32)).astype(x.dtype)

def rope_tables_2(seq_len):
    pos = jnp.arange(seq_len, dtype=jnp.float32)
    inv_freq = ROPE_THETA_2 ** (-jnp.arange(0, ROPE_DIM, 2, dtype=jnp.float32) / ROPE_DIM)
    ang = pos[:, None] * inv_freq[None, :]
    return jnp.cos(ang), jnp.sin(ang)

def apply_partial_rope(x, cos, sin):
    half = ROPE_DIM // 2
    xf = x.astype(jnp.float32)
    x1 = xf[..., :half]
    x2 = xf[..., half:ROPE_DIM]
    c = cos[None, :, None, :]
    s = sin[None, :, None, :]
    out = jnp.concatenate([x1 * c - x2 * s, x2 * c + x1 * s, xf[..., ROPE_DIM:]], axis=-1)
    return out.astype(x.dtype)

def dilated_attention(q, k, v):
    b, h, seq, _ = q.shape
    scale = 1.0 / math.sqrt(HEAD_DIM)
    offs = jnp.arange(Q_BLOCK)

    def block(blk):
        t = blk * Q_BLOCK + offs
        q_blk = lax.dynamic_slice_in_dim(q, blk * Q_BLOCK, Q_BLOCK, axis=2).astype(jnp.float32) * scale
        lses, outs = [], []
        for window, dilation in DILATED_PATTERNS:
            n_keys = window // dilation + 1
            idx = t[:, None] - dilation * jnp.arange(n_keys)[None, :]
            valid = idx >= 0
            idx = jnp.maximum(idx, 0)
            k_g = jnp.take(k, idx, axis=2).astype(jnp.float32)
            v_g = jnp.take(v, idx, axis=2).astype(jnp.float32)
            s = jnp.einsum('bhqd,bhqjd->bhqj', q_blk, k_g)
            s = jnp.where(valid[None, None], s, -jnp.inf)
            lse = jax.nn.logsumexp(s, axis=-1)
            p = jnp.exp(s - lse[..., None])
            outs.append(jnp.einsum('bhqj,bhqjd->bhqd', p, v_g))
            lses.append(lse)
        mix = jax.nn.softmax(jnp.stack(lses), axis=0)
        return jnp.sum(mix[..., None] * jnp.stack(outs), axis=0)

    out = lax.map(block, jnp.arange(seq // Q_BLOCK))
    return out.transpose(1, 2, 0, 3, 4).reshape(b, h, seq, HEAD_DIM).astype(q.dtype)

def stick_breaking_attention(q, k, v):
    b, h, seq, _ = q.shape
    scale = 1.0 / math.sqrt(HEAD_DIM)
    offs = jnp.arange(Q_BLOCK)
    key_pos = jnp.arange(seq)
    kf = k.astype(jnp.float32)
    vf = v.astype(jnp.float32)

    def block(blk):
        t = blk * Q_BLOCK + offs
        q_blk = lax.dynamic_slice_in_dim(q, blk * Q_BLOCK, Q_BLOCK, axis=2).astype(jnp.float32)
        z = jnp.einsum('bhqd,bhkd->bhqk', q_blk, kf) * scale
        causal = key_pos[None, :] < t[:, None]
        log_keep = jnp.where(causal, jax.nn.log_sigmoid(-z), 0.0)
        tail = lax.cumsum(log_keep, axis=3, reverse=True)
        between = jnp.concatenate([tail[..., 1:], jnp.zeros_like(tail[..., :1])], axis=-1)
        weights = jnp.where(causal, jnp.exp(jax.nn.log_sigmoid(z) + between), 0.0)
        return jnp.einsum('bhqk,bhkd->bhqd', weights, vf)

    out = lax.map(block, jnp.arange(seq // Q_BLOCK))
    return out.transpose(1, 2, 0, 3, 4).reshape(b, h, seq, HEAD_DIM).astype(q.dtype)

def _linear_recurrence_combine(left, right):
    a1, b1 = left
    a2, b2 = right
    return a1 * a2, a2 * b1 + b2

def rg_lru_branch(x, conv_w, conv_b, gate_a_w, gate_a_b, gate_x_w, gate_x_b, lru_lambda):
    b, s, w = x.shape
    xc = lax.conv_general_dilated(
        x, conv_w[:, None, :].astype(x.dtype), window_strides=(1,), padding=[(CONV_WIDTH - 1, 0)],
        dimension_numbers=('NWC', 'WIO', 'NWC'), feature_group_count=w) + conv_b
    xg = xc.reshape(b, s, N_LRU_BLOCKS, HEAD_DIM)
    r = jax.nn.sigmoid(jnp.einsum('bsnd,nde->bsne', xg, gate_a_w) + gate_a_b).reshape(b, s, w)
    i = jax.nn.sigmoid(jnp.einsum('bsnd,nde->bsne', xg, gate_x_w) + gate_x_b).reshape(b, s, w)
    log_a = LRU_C * r.astype(jnp.float32) * jax.nn.log_sigmoid(lru_lambda.astype(jnp.float32))
    a = jnp.exp(log_a)
    u = jnp.sqrt(-jnp.expm1(2.0 * log_a)) * (i * xc).astype(jnp.float32)
    _, h = lax.associative_scan(_linear_recurrence_combine, (a, u), axis=1)
    return h.astype(x.dtype)

def hybrid_layer(x, cos, sin, norm_gain, w_in, conv_w, conv_b, gate_a_w, gate_a_b,
                 gate_x_w, gate_x_b, lru_lambda, w_out):
    b, s, _ = x.shape
    hn = rms_norm(x, norm_gain)
    proj = jnp.einsum('bsd,de->bse', hn, w_in)
    a_q, a_k, a_v, a_g, b_x, b_g, c_q, c_k, c_v, c_g = jnp.split(proj, _in_split_points(), axis=-1)

    qa = apply_partial_rope(a_q.reshape(b, s, N_HEADS_DIL, HEAD_DIM), cos, sin).transpose(0, 2, 1, 3)
    ka = apply_partial_rope(a_k.reshape(b, s, N_HEADS_DIL, HEAD_DIM), cos, sin).transpose(0, 2, 1, 3)
    va = a_v.reshape(b, s, N_HEADS_DIL, HEAD_DIM).transpose(0, 2, 1, 3)
    y_a = dilated_attention(qa, ka, va).transpose(0, 2, 1, 3).reshape(b, s, W_DIL) * jax.nn.silu(a_g)

    y_b = rg_lru_branch(b_x, conv_w, conv_b, gate_a_w, gate_a_b, gate_x_w, gate_x_b, lru_lambda) * jax.nn.silu(b_g)

    qc = c_q.reshape(b, s, N_HEADS_SB, HEAD_DIM).transpose(0, 2, 1, 3)
    kc = c_k.reshape(b, s, N_HEADS_SB, HEAD_DIM).transpose(0, 2, 1, 3)
    vc = c_v.reshape(b, s, N_HEADS_SB, HEAD_DIM).transpose(0, 2, 1, 3)
    y_c = stick_breaking_attention(qc, kc, vc).transpose(0, 2, 1, 3).reshape(b, s, W_SB) * jax.nn.silu(c_g)

    y = jnp.concatenate([y_a, y_b, y_c], axis=-1)
    return x + jnp.einsum('bse,ed->bsd', y, w_out)

def second_inputs(seed: int = 0) -> dict:
    key = jax.random.key(seed)
    ks = jax.random.split(key, 13)
    f32 = jnp.float32
    x = jax.random.normal(ks[0], (BATCH, SEQ, D_MODEL), f32)
    norm_gain = 1.0 + 0.02 * jax.random.normal(ks[1], (DEPTH, D_MODEL), f32)
    w_in = jax.random.normal(ks[2], (DEPTH, D_MODEL, D_IN), f32) * D_MODEL ** -0.5
    conv_w = jax.random.normal(ks[3], (DEPTH, CONV_WIDTH, W_LRU), f32) * CONV_WIDTH ** -0.5
    conv_b = 0.01 * jax.random.normal(ks[4], (DEPTH, W_LRU), f32)
    gate_a_w = jax.random.normal(ks[5], (DEPTH, N_LRU_BLOCKS, HEAD_DIM, HEAD_DIM), f32) * HEAD_DIM ** -0.5
    gate_a_b = 0.01 * jax.random.normal(ks[6], (DEPTH, N_LRU_BLOCKS, HEAD_DIM), f32)
    gate_x_w = jax.random.normal(ks[7], (DEPTH, N_LRU_BLOCKS, HEAD_DIM, HEAD_DIM), f32) * HEAD_DIM ** -0.5
    gate_x_b = 0.01 * jax.random.normal(ks[8], (DEPTH, N_LRU_BLOCKS, HEAD_DIM), f32)
    u = jax.random.uniform(ks[9], (DEPTH, W_LRU), f32, minval=0.9, maxval=0.999)
    a0 = u ** (1.0 / LRU_C)
    lru_lambda = jnp.log(a0) - jnp.log1p(-a0)
    w_out = jax.random.normal(ks[10], (DEPTH, D_MIX, D_MODEL), f32) * D_MIX ** -0.5
    final_gain = 1.0 + 0.02 * jax.random.normal(ks[11], (D_MODEL,), f32)
    return {'x': x, 'norm_gain': norm_gain, 'w_in': w_in, 'conv_w': conv_w, 'conv_b': conv_b,
            'gate_a_w': gate_a_w, 'gate_a_b': gate_a_b, 'gate_x_w': gate_x_w, 'gate_x_b': gate_x_b,
            'lru_lambda': lru_lambda, 'w_out': w_out, 'final_gain': final_gain}

def second_block(x, norm_gain, w_in, conv_w, conv_b, gate_a_w, gate_a_b, gate_x_w, gate_x_b,
              lru_lambda, w_out, final_gain):
    cos, sin = rope_tables_2(x.shape[1])
    h = x
    for l in range(DEPTH):
        h = hybrid_layer(h, cos, sin, norm_gain[l], w_in[l], conv_w[l], conv_b[l], gate_a_w[l],
                         gate_a_b[l], gate_x_w[l], gate_x_b[l], lru_lambda[l], w_out[l])
    return rms_norm(h, final_gain)


def setup_inputs(seed=0):
    out = dict(first_inputs(seed))
    for name, value in second_inputs(seed + 1).items():
        if name != "x":
            out[name + "_2"] = value
    return out


def reference(
    x, norm_mix_0, w_in_0, shift_mu_0, rw_w0_0, rw_w2_0, rw_a0_0, rw_a2_0, rw_g2_0, rw_kk_0,
    rw_ka_0, rw_rk_0, rw_lnx_g_0, rw_lnx_b_0, mla_qnorm_0, mla_wuq_0, mla_kvnorm_0, mla_wukv_0,
    w_out_0, norm_ffn_0, ffn_wg_0, ffn_wu_0, ffn_wd_0, norm_mix_1, w_in_1, fox_bf_1, w_out_1,
    norm_ffn_1, router_1, moe_wg_1, moe_wu_1, moe_wd_1, final_norm, norm_gain_2, w_in_2,
    conv_w_2, conv_b_2, gate_a_w_2, gate_a_b_2, gate_x_w_2, gate_x_b_2, lru_lambda_2, w_out_2,
    final_gain_2,
):
    x = first_block(
        x, norm_mix_0, w_in_0, shift_mu_0, rw_w0_0, rw_w2_0, rw_a0_0, rw_a2_0, rw_g2_0, rw_kk_0,
        rw_ka_0, rw_rk_0, rw_lnx_g_0, rw_lnx_b_0, mla_qnorm_0, mla_wuq_0, mla_kvnorm_0,
        mla_wukv_0, w_out_0, norm_ffn_0, ffn_wg_0, ffn_wu_0, ffn_wd_0, norm_mix_1, w_in_1,
        fox_bf_1, w_out_1, norm_ffn_1, router_1, moe_wg_1, moe_wu_1, moe_wd_1, final_norm,
    )
    return second_block(
        x, norm_gain_2, w_in_2, conv_w_2, conv_b_2, gate_a_w_2, gate_a_b_2, gate_x_w_2,
        gate_x_b_2, lru_lambda_2, w_out_2, final_gain_2,
    )


_drawn_inputs = setup_inputs


def setup_inputs(seed=0):
    import zlib

    import numpy as np

    out = dict(_drawn_inputs(seed))
    spreads = {}
    factors = {'rw_lnx_b_0': 2.743,
     'mla_qnorm_0': 2.702,
     'norm_gain_2': 4.323,
     'conv_b_2': 3.519,
     'gate_a_b_2': 35.868,
     'gate_x_b_2': 26.529}
    for name, (base, spread) in spreads.items():
        noise = np.random.default_rng([zlib.crc32(name.encode()), seed]).standard_normal(out[name].shape)
        drawn = base * np.exp(spread * noise) if base else spread * noise
        out[name] = __import__('jax').numpy.asarray(drawn.astype(out[name].dtype))
    for name, factor in factors.items():
        out[name] = (out[name] * factor).astype(out[name].dtype)
    return out
```

```python
from contextlib import ExitStack

import numpy as np
import concourse.bass as bass
from concourse import mybir

F32 = mybir.dt.float32
BF16 = mybir.dt.bfloat16
I32 = mybir.dt.int32
ALU = mybir.AluOpType
ACT = mybir.ActivationFunctionType
AX_X = mybir.AxisListType.X

P = 128
T = 256
TT = T // P
D = 1024
DC = D // P
HD = 64
NH = 8
GW = NH * HD
GC = GW // P
E = 8
RING = 6
SLOT = 2048
SLOT_COLS = SLOT // DC

N_IN0, N_OUT, N_FFN, N_IN1 = 9, 4, 33, 12
FFN_STEPS = 11
MOE_STEPS = 14
MOE_SLOTS = 3 * MOE_STEPS
N_EARLY = N_IN0 + N_OUT + N_FFN + N_IN1 + N_OUT
N_MOE = E * MOE_SLOTS
N_IN2 = 14
N_LATE = 2 * (N_IN2 + N_OUT)
W_MOE = N_EARLY
W_LATE = N_EARLY + N_MOE
EPS = 1e-6
GN_EPS = 64e-5
NEG = -1e30
LEVELS = (2, 4, 8, 16, 32, 64)



def rope_table(n_rot, theta, period):
    half = n_rot // 2
    inv = np.float32(theta) ** (-np.arange(0, n_rot, 2, dtype=np.float32) / np.float32(n_rot))
    ang = np.arange(T, dtype=np.float32)[None, :] * inv[:, None].astype(np.float32)
    cos, sin = np.ones((P, T), np.float32), np.zeros((P, T), np.float32)
    for f in range(P):
        if f % period < n_rot:
            cos[f], sin[f] = np.cos(ang[f % period % half]), np.sin(ang[f % period % half])
    return cos, sin


def rope_partner(n_rot, period):
    perm, half = np.zeros((P, P), np.float32), n_rot // 2
    for o in range(P):
        r = o % period
        if r < half:
            perm[o + half, o] = -1.0
        elif r < n_rot:
            perm[o - half, o] = 1.0
    return perm


def shape_constants():
    i, j = np.arange(P)[:, None], np.arange(P)[None, :]
    c = {}
    c["ident"] = (i == j)
    c["ones"] = np.ones((P, P))
    c["same_head"] = (i // HD == j // HD)
    strict, incl = (i < j), (i <= j)
    c["mask4"] = np.concatenate([strict, incl, strict, incl], 1)
    c["level1"] = (i == j + 1) & (i % 2 == 1)
    for m in (1,) + LEVELS:
        c[f"levelT{m}"] = (i // (2 * m) == j // (2 * m)) & (i // m < j // m)
    t, s = np.arange(T)[:, None], np.arange(T)[None, :]
    causal = np.where(s <= t, 0.0, NEG)
    gap = t - s
    count = ((gap >= 0) & (gap <= 128)) * 1.0 + ((gap >= 0) & (gap % 4 == 0)) + ((gap >= 0) & (gap % 16 == 0))
    dil = np.where(count > 0, np.log(np.maximum(count, 1)), NEG)
    for name, m in (("causal", causal), ("dilated", dil)):
        c[name] = np.concatenate([m[:P, :P], m[P:, :]], 1)
    stick = np.concatenate([strict, np.ones((P, P)), strict], 1)
    c["stick01"] = stick
    c["stick_add"] = np.where(stick > 0, 0.0, NEG)
    c["neg_tail"] = -1.0 * (i >= j)
    c["neg_ones"] = -np.ones((P, P))
    c["before"] = strict
    c["slot_iota"] = np.broadcast_to(np.arange(P), (P, P))
    lower = (np.arange(E)[None, :] < np.arange(E)[:, None]) * 1.0
    c["lower"] = np.broadcast_to(lower.reshape(1, E * E), (P, E * E))
    c["pick8"] = 8.0 * (np.arange(P)[:, None] == np.arange(NH)[None, :])
    for name, rot, theta, period in (("mla", 32, 1e4, 32), ("full", 64, 1e4, 64), ("part", 16, 5e5, 64)):
        c[f"cos_{name}"], c[f"sin_{name}"] = rope_table(rot, theta, period)
        c[f"partner_{name}"] = rope_partner(rot, period)
    return {k: np.asarray(v, np.float32) for k, v in c.items()}


PARAMS = dict(
    gains=8 * DC, mu=14, w0=GC, a0=GC, kkp=GC, kap=GC, rkp=GC, lnxg=GC, lnxb=GC,
    qnorm=2, kvnorm=1, w2z=GW, a2z=GW, g2=GW, wuq=2 * 768, wukv=1024,
    foxbf=1, wf=DC * NH, router=DC * E, convw=2 * 2 * 4, convb=4, gab=4, gxb=4, lam=4,
    gaw=2 * 2 * P, gxw=2 * 2 * P)


def program(nc, x_dram, const_dram, param_dram, w_dram, out_dram, const_at):
    ctx = ExitStack()
    with ctx:
        def sb(name, cols, dt=F32):
            return ctx.enter_context(nc.sbuf_tensor(name, [P, cols], dt))

        def sem(name):
            return ctx.enter_context(nc.semaphore(name))

        ring = sb("weight_ring", RING * SLOT)
        hT_ = sb("hT", DC * T)
        uT_ = sb("uT", DC * T)
        yc_ = sb("ycat", DC * T)
        sq_ = sb("squares", DC * T)
        cst = sb("constants", const_dram.shape[1])
        par = sb("parameters", param_dram.shape[1])
        ARENA = 20480
        arena = sb("arena", ARENA)
        tiny = sb("tiny", 512)
        zero16 = sb("zero16", 512, BF16)
        hT = hT_[:, :].rearrange("p (c t) -> p c t", c=DC)
        uT = uT_[:, :].rearrange("p (c t) -> p c t", c=DC)
        ycat = yc_[:, :].rearrange("p (c t) -> p c t", c=DC)
        sq = sq_[:, :].rearrange("p (c t) -> p c t", c=DC)

        def C(name):
            a, n = const_at[name]
            return cst[:, a:a + n]

        par_at, at = {}, 0
        for k, n in PARAMS.items():
            par_at[k] = (at, n)
            at += n

        def Pm(name):
            a, n = par_at[name]
            return par[:, a:a + n]

        def col(name, i):
            a, _ = par_at[name]
            return par[:, a + i:a + i + 1]

        class Arena:
            def __init__(self, start=0):
                self.at = start

            def take(self, n):
                a = self.at
                self.at += n
                assert self.at <= ARENA, self.at
                return arena[:, a:a + n]

        def chunks(ap, c):
            return ap.rearrange("p (c t) -> p c t", c=c)

        banks = [ctx.enter_context(nc.psum_tensor(f"bank{i}", [P, 512], F32)) for i in range(8)]

        loaded = sem("inputs_loaded")
        stored = sem("output_stored")
        landed = [sem(f"weights_landed{i}") for i in range(RING)]
        late_landed = [sem(f"late_weights_landed{i}") for i in range(RING)]
        used = sem("weights_used")
        late_used = sem("late_weights_used")
        flag_ready = sem("expert_passes_known")
        names = ("squares_ready", "std_ready", "u_ready", "h_ready", "y_ready",
                 "zero_ready",
                 "lora_in", "kk_in", "decay_in", "exp_in", "exp_out", "keys_ready", "bonus_in",
                 "masked", "level_ct", "inv_update", "solve_x", "solve_u", "state_ready", "tok_ready",
                 "gn_in", "gn_sq", "gn_std", "gn_var", "kk_sq", "kk_std", "lru_arg",
                 "mla_sq", "mla_std", "mla_q", "mla_kv", "rope_in", "rope_done",
                 "nmax_ready", "exp_done", "rz_ready", "prob_ready",
                 "fox_z", "fox_e", "fox_d", "stick_z", "stick_l", "stick_n", "stick_arg", "stick_w",
                 "conv_done", "lru_gates", "lru_a", "lru_t", "lru_q", "lru_s", "lam_in", "lam_e", "lam_c",
                 "gate_raw", "gate_done",
                 "router_l", "router_e", "router_sel", "tok_major", "onehot", "onehot_g",
                 "moe_tab", "moe_gu", "moe_sig", "moe_hid", "moe_down", "moe_x", "moe_y", "moe_ytok",
                 "moe_gt", "moe_gtt", "moe_g", "moe_sc", "moe_add", "moe_end",
                 "ffn_mid", "moe_mid", "moe_act", "moe_vec", "ffn_gu", "ffn_sig", "ffn_hid", "ffn_down", "out_ready")
        S = {n: sem(n) for n in names}

        class Channel:
            def __init__(self, which, filled, freed):
                self.which, self.filled, self.freed, self.np, self.nc = which, filled, freed, 0, 0

            def claim(self, pe):
                n = self.np
                if n >= len(self.which):
                    pe.wait_ge(self.freed, n - len(self.which) + 1)
                return banks[self.which[n % len(self.which)]]

            def fill(self, ins):
                ins.then_inc(self.filled, 1)
                self.np += 1
                return self.np

            def take(self, eng):
                eng.wait_ge(self.filled, self.nc + 1)
                return banks[self.which[self.nc % len(self.which)]]

            def free(self, ins):
                ins.then_inc(self.freed, 1)
                self.nc += 1
                return self.nc

        A = Channel((0, 1), sem("psum_for_scalar"), sem("scalar_read_psum"))
        V = Channel((2, 3), sem("psum_for_vector"), sem("vector_read_psum"))

        class Step:
            def __init__(self, eng, chain):
                self.eng, self.chain, self.n, self.said = eng, chain, 0, {}

            def own(self, ins):
                self.n += 1
                ins.then_inc(self.chain, 1)
                self.eng.wait_ge(self.chain, self.n)

            def lone(self, ins):
                self.n += 1
                ins.then_inc(self.chain, 1)

            def settle(self):
                self.eng.wait_ge(self.chain, self.n)

            def say(self, ins, name):
                self.said[name] = self.said.get(name, 0) + 1
                ins.then_inc(S[name], 1)

            def wait_said(self, name):
                self.eng.wait_ge(S[name], self.said[name])

        ar = Arena()
        raw = chunks(ar.take(14 * T), 14)
        qlat = chunks(ar.take(2 * T), 2)
        kvl = ar.take(T)
        kpe = ar.take(T)
        ATT = ar.at
        qno = chunks(ar.take(GC * T), GC)
        qpe = chunks(ar.take(2 * T), 2)
        kno = chunks(ar.take(GC * T), GC)
        vml = ar.take(TT * GW).rearrange("p (a n) -> p a n", a=TT)
        qn = chunks(ar.take(2 * T), 2)
        kvn = ar.take(T)
        rt1 = ar.take(T)
        rt2 = ar.take(T)
        std_m = ar.take(T)
        att = Arena(ARENA - 3 * 384 - 4 * 384)
        Lg = [att.take(384) for _ in range(3)]
        PTs = [att.take(384) for _ in range(4)]
        assert ar.at <= ARENA - 7 * 384

        aw = Arena(14 * T)
        rw = chunks(aw.take(14 * T), 14)
        lw = aw.take(T)
        sg = aw.take(T)
        logd = chunks(aw.take(GC * T), GC)
        iclr = chunks(aw.take(GC * T), GC)
        g_ = chunks(aw.take(GC * T), GC)
        cs = chunks(aw.take(GC * T), GC)
        csx = chunks(aw.take(GC * T), GC)
        KR = aw.take(2 * GC * T).rearrange("p (c a k t) -> p c a k t", c=GC, a=TT, k=2)
        Bs = chunks(aw.take(GC * T), GC)
        Ks = chunks(aw.take(GC * T), GC)
        vtok = aw.take(TT * GW).rearrange("p (a n) -> p a n", a=TT)
        Btok = aw.take(GW)
        Ktok = aw.take(GW)
        Sbd = aw.take(GW).rearrange("p (c n) -> p c n", c=GC)
        Xn = aw.take(GW)
        Ut = aw.take(GW)
        yT = ycat[:, 0:GC, :]
        k2 = chunks(sq_[:, 0:GC * T], GC)
        bon = chunks(sq_[:, GC * T:2 * GC * T], GC)
        AT_A = arena[:, 0:14 * T]
        E1 = chunks(AT_A[:, 0:GC * T], GC)
        E2 = chunks(AT_A[:, GC * T:2 * GC * T], GC)
        E3 = chunks(AT_A[:, 2 * GC * T:3 * GC * T], GC)
        kk = chunks(uT_[:, 0:GC * T], GC)
        kkr = chunks(uT_[:, GC * T:2 * GC * T], GC)
        AT0 = arena[:, 14 * T:14 * T + NH * 512]
        AT = AT0.rearrange("p (h q s) -> p h q s", h=NH, q=4)
        Dm = chunks(AT_A[:, 0:NH * P], NH)
        DmT = chunks(AT_A[:, NH * P:2 * NH * P], NH)
        Gm = chunks(AT_A[:, 2 * NH * P:3 * NH * P], NH)
        CTm = chunks(uT_[:, 0:NH * P], NH)
        omka = tiny[:, 0:GC]
        fend = tiny[:, 8:8 + GC]

        a1 = Arena()
        fq = chunks(a1.take(GC * T), GC)
        fk = chunks(a1.take(GC * T), GC)
        fv = a1.take(TT * GW).rearrange("p (a n) -> p a n", a=TT)
        mq = chunks(a1.take(GC * T), GC)
        mk = chunks(a1.take(GC * T), GC)
        mv = a1.take(TT * GW).rearrange("p (a n) -> p a n", a=TT)
        fz, fe, fl, fd, fnd = [a1.take(T) for _ in range(5)]
        r1a, r1b = a1.take(T), a1.take(T)
        am = Arena()
        ttok = am.take(TT * D).rearrange("p (a n) -> p a n", a=TT)
        lg = am.take(TT * E)
        big = am.take(TT * E * E)
        big2 = am.take(TT * E * E)
        rank, selm, ex, comb, posm = [am.take(TT * E) for _ in range(5)]
        cnt = am.take(E)
        table = am.take(2 * E * 4).rearrange("p (e k) -> p e k", e=2 * E)
        cur = am.take(4)
        m0, den = am.take(TT), am.take(TT)
        mcnt = am.take(2)
        oh = am.take(TT * P).rearrange("p (a s) -> p a s", a=TT)
        ohg = am.take(TT * P).rearrange("p (a s) -> p a s", a=TT)
        ohgT = am.take(T)
        xg = am.take(DC * P).rearrange("p (c s) -> p c s", c=DC)
        ysl = am.take(D)
        sigb = [am.take(2 * T) for _ in range(2)]
        gtmp = [am.take(2 * T) for _ in range(2)]
        hid = [am.take(2 * T) for _ in range(2)]
        ah = Arena()
        hq = chunks(ah.take(GC * T), GC)
        hk = chunks(ah.take(GC * T), GC)
        hv = ah.take(TT * GW).rearrange("p (a n) -> p a n", a=TT)
        gate = chunks(ah.take(DC * T), DC)
        bx = chunks(ah.take(2 * T), 2)
        xc = chunks(ah.take(2 * T), 2)
        lr, li, la, lt, lq, lu = [chunks(ah.take(2 * T), 2) for _ in range(6)]
        cq = chunks(ah.take(2 * T), 2)
        ck = chunks(ah.take(2 * T), 2)
        cv = ah.take(TT * T).rearrange("p (a n) -> p a n", a=TT)
        hra, hrb = ah.take(T), ah.take(T)
        zb = ah.take(4 * 384).rearrange("p (h n) -> p h n", h=4)
        gsig = chunks(arena[:, ah.at - 4 * 384:ah.at - 4 * 384 + DC * T], DC)
        zl = ah.take(4 * 384).rearrange("p (h n) -> p h n", h=4)
        zw = ah.take(4 * 384).rearrange("p (h n) -> p h n", h=4)
        assert max(ah.at, a1.at) <= ARENA - 7 * 384
        lam_t = tiny[:, 16:80]
        nmx = tiny[:, 80:96].rearrange("p (n k) -> p n k", k=2)
        zsum = tiny[:, 96:112].rearrange("p (n k) -> p n k", k=2)
        rz = tiny[:, 112:128].rearrange("p (n k) -> p n k", k=2)
        passes_i = ctx.enter_context(nc.sbuf_tensor("passes_i", [P, 1], I32))

        done = {}

        def slot(i):
            return ring[:, (i % RING) * SLOT:(i % RING + 1) * SLOT]

        block = ctx.enter_context(nc.Block())

        @block.sync
        def _(sp):
            sp.dma_start(hT_[:, :], x_dram).then_inc(loaded, 16)
            sp.dma_start(cst[:, :], const_dram).then_inc(loaded, 16)
            sp.dma_start(par[:, :], param_dram).then_inc(loaded, 16)

            for k in range(RING):
                sp.dma_start(slot(k), w_dram[k]).then_inc(landed[k], 16)
            with sp.Fori(1, N_EARLY // RING) as turn:
                for k in range(RING):
                    sp.wait_ge(used, turn * RING + (k + 1 - RING))
                    sp.dma_start(slot(k), w_dram[bass.ds(turn * RING + k, 1)].rearrange("o p n -> (o p) n"))\
                      .then_inc(landed[k], 16)
            for n in range(N_EARLY // RING * RING, N_EARLY):
                sp.wait_ge(used, n + 1 - RING)
                sp.dma_start(slot(n), w_dram[n]).then_inc(landed[n % RING], 16)
            sp.wait_ge(flag_ready, 1)
            passes = sp.value_load(passes_i[0:1, 0:1], min_val=1, max_val=2)
            with sp.Fori(0, passes) as ps:
                with sp.Fori(0, N_MOE // RING) as turn:
                    for k in range(RING):
                        n = N_EARLY + k
                        sp.wait_ge(used, ps * N_MOE + turn * RING + (n + 1 - RING))
                        sp.dma_start(slot(n), w_dram[bass.ds(turn * RING + n, 1)].rearrange("o p n -> (o p) n"))\
                          .then_inc(landed[n % RING], 16)
            sp.wait_ge(S["moe_end"], 1)
            for n in range(N_LATE):
                if n >= RING:
                    sp.wait_ge(late_used, n + 1 - RING)
                sp.dma_start(slot(n), w_dram[W_LATE + n]).then_inc(late_landed[n % RING], 16)
            sp.wait_ge(S["out_ready"], 1)
            sp.dma_start(out_dram, uT_[:, :]).then_inc(stored, 16)
            sp.wait_ge(stored, 16)

        @block.tensor
        def _(pe):
            wn = [0, 0]
            job = {}

            def next_slot(late):
                n = wn[late]
                pe.wait_ge((late_landed if late else landed)[n % RING], 16 * (n // RING + 1))
                return slot(n)

            owed = []

            def mm(out, lhsT, rhs, start=True, stop=True, tells=False):
                ins = pe.matmul(out, lhsT, rhs, start=start, stop=stop, skip_group_check=True)
                if owed and not tells:
                    ins.then_inc(owed.pop(), 1)
                return ins

            def tr(out, in_):
                return pe.transpose(out, in_, C("ident"))

            def project(ch, rhs, late=0):
                w = next_slot(late).rearrange("p (c n) -> p c n", c=DC)
                bank = ch.claim(pe)[:, :].rearrange("p (j t) -> p j t", j=2)
                for j in range(2):
                    for c in range(DC):
                        last = mm(bank[:, j, :], w[:, c, j * P:(j + 1) * P], rhs[:, c, :], start=(c == 0), stop=(c == DC - 1))
                ch.fill(last)
                free_slot(late)
                return ch.np

            def free_slot(late):
                owed.append(late_used if late else used)
                wn[late] += 1

            def project_tok(ch, lhs, late=0):
                w = next_slot(late).rearrange("p (c n) -> p c n", c=DC)
                bank = ch.claim(pe)[:, :].rearrange("p (a n) -> p a n", a=TT)
                for a in range(TT):
                    for c in range(DC):
                        last = mm(bank[:, a, :], lhs[:, c, a * P:(a + 1) * P], w[:, c, :], start=(c == 0), stop=(c == DC - 1))
                ch.fill(last)
                free_slot(late)

            def norm(k):
                bank = A.claim(pe)
                for c in range(DC):
                    if c % 4 == 0:
                        pe.wait_ge(S["squares_ready"], 2 * k + c // 4 + 1)
                    last = mm(bank[:, 0:T], C("ones"), sq[:, c, :], start=(c == 0), stop=(c == DC - 1))
                A.fill(last)

            def attention(scores, v, n0, v_done):
                prob = {}
                for i in range(NH + 3):
                    if i < NH:
                        bank = V.claim(pe)
                        V.fill(scores(i, bank))
                    if 1 <= i <= NH:
                        h = i - 1
                        pe.wait_ge(S["prob_ready"], n0 + h + 1)
                        bank = A.claim(pe)
                        for b, (lo, sp_) in enumerate(((0, 0), (P, 0), (2 * P, 0))):
                            last = tr(bank[:, lo:lo + P], Lg[h % 3][:, lo:lo + P])
                        prob[h] = A.fill(last)
                    if i >= 3 and (i - 2) % 2 == 1:
                        bank = V.claim(pe)
                        pe.wait_ge(A.freed, prob[i - 2])
                        for h in (i - 3, i - 2):
                            o = bank[HD * (h % 2):HD * (h % 2) + HD, :]
                            mm(o[:, 0:T], v[:, 0, h * HD:(h + 1) * HD], PTs[h % 4][:, 0:T], stop=False)
                            last = mm(o[:, P:T], v[:, 1, h * HD:(h + 1) * HD], PTs[h % 4][:, T:T + P], start=False)
                        V.fill(last)

            def head_scores(q, k):
                def go(h, bank):
                    c, b = h // 2, HD * (h % 2)
                    mm(bank[:, 0:P], q[b:b + HD, c, 0:P], k[b:b + HD, c, 0:P])
                    return mm(bank[:, P:P + T], q[b:b + HD, c, P:T], k[b:b + HD, c, :])
                return go

            def rope(x, n, which, cnt0):
                for c in range(n):
                    bank = V.claim(pe)
                    V.fill(mm(bank[:, 0:T], C(f"partner_{which}"), x[:, c, :], tells=True))

            pe.wait_ge(loaded, 48)
            norm(0)
            pe.wait_ge(S["u_ready"], 1)
            for _ in range(N_IN0):
                project(A, uT)

            bank = A.claim(pe)
            pe.wait_ge(S["mla_sq"], 1)
            for c in range(2):
                mm(bank[:, 0:T], C("ones"), sq[:, c, :], start=(c == 0), stop=(c == 1))
            A.fill(mm(bank[:, T:2 * T], C("ones"), sq[:, 2, :], tells=True))
            pe.wait_ge(S["mla_q"], 1)
            wuq = Pm("wuq").rearrange("p (k n) -> p k n", k=2)
            for j2 in range(3):
                bank = A.claim(pe)
                for j in range(2):
                    for c in range(2):
                        cc = (2 * j2 + j) * P
                        last = mm(bank[:, j * T:(j + 1) * T], wuq[:, c, cc:cc + P], qn[:, c, :], start=(c == 0), stop=(c == 1))
                A.fill(last)
            wukv = Pm("wukv")
            pe.wait_ge(S["mla_kv"], 1)
            for j2 in range(2):
                bank = A.claim(pe)
                for j in range(2):
                    cc = (2 * j2 + j) * P
                    last = mm(bank[:, j * T:(j + 1) * T], wukv[:, cc:cc + P], kvn)
                A.fill(last)
            for a in range(TT):
                bank = A.claim(pe)
                A.fill(mm(bank[:, :], kvn[:, a * P:(a + 1) * P], wukv[:, GW:2 * GW], tells=True))
            pe.wait_ge(A.freed, A.np)
            rope(qpe, 2, "mla", 0)
            bank = V.claim(pe)
            V.fill(mm(bank[:, 0:T], C("partner_mla"), kpe, tells=True))
            pe.wait_ge(S["rope_done"], 3)

            def mla_scores(h, bank):
                c, b = h // 2, HD * (h % 2)
                c4, b4 = h // 4, 32 * (h % 4)
                mm(bank[:, 0:P], qno[b:b + HD, c, 0:P], kno[b:b + HD, c, 0:P], stop=False)
                mm(bank[:, 0:P], qpe[b4:b4 + 32, c4, 0:P], kpe[b4:b4 + 32, 0:P], start=False)
                mm(bank[:, P:P + T], qno[b:b + HD, c, P:T], kno[b:b + HD, c, :], stop=False)
                return mm(bank[:, P:P + T], qpe[b4:b4 + 32, c4, P:T], kpe[b4:b4 + 32, :], start=False)

            attention(mla_scores, vml, 0, None)

            pe.wait_ge(S["lora_in"], 2)
            for w, x in ((Pm("w2z"), lw), (Pm("a2z"), lw), (Pm("g2"), sg)):
                for j2 in range(2):
                    bank = A.claim(pe)
                    for j in range(2):
                        cc = (2 * j2 + j) * P
                        last = mm(bank[:, j * T:(j + 1) * T], w[:, cc:cc + P], x)
                    A.fill(last)
            pe.wait_ge(S["kk_sq"], 1)
            for j2 in range(2):
                bank = A.claim(pe)
                A.fill(mm(bank[:, 0:512], C("same_head"), sq_[:, j2 * 512:(j2 + 1) * 512], tells=True))
            pe.wait_ge(S["bonus_in"], 1)
            for j2 in range(2):
                bank = V.claim(pe)
                V.fill(mm(bank[:, 0:512], C("same_head"), sq_[:, 1024 + j2 * 512:1024 + (j2 + 1) * 512], tells=True))
            for a in range(TT):
                bank = A.claim(pe)
                for c in range(GC):
                    last = tr(bank[:, c * P:(c + 1) * P], rw[:, 8 + c, a * P:(a + 1) * P])
                A.fill(last)
            pe.wait_ge(S["keys_ready"], 1)
            for src in (Bs, Ks):
                bank = A.claim(pe)
                for c in range(GC):
                    last = tr(bank[:, c * P:(c + 1) * P], src[:, c, 0:P])
                A.fill(last)

            for a in range(TT):
                lo, hi = a * P, (a + 1) * P
                for h in range(NH):
                    c, b = h // 2, HD * (h % 2)
                    bank = V.claim(pe)
                    kr = KR[b:b + HD, c, a].rearrange("p k t -> p (k t)")
                    mm(bank[:, 0:T], Bs[b:b + HD, c, lo:hi], kr)
                    V.fill(mm(bank[:, T:2 * T], Ks[b:b + HD, c, lo:hi], kr, tells=True))
                for par_ in range(2):
                    bank = V.claim(pe)
                    for h in range(par_, NH, 2):
                        c, b = h // 2, HD * par_
                        last = mm(bank[:, c * P:(c + 1) * P], KR[b:b + HD, c, a, 0, :], Bs[b:b + HD, c, lo:hi])
                    V.fill(last)
                for n, m in enumerate(LEVELS):
                    pe.wait_ge(S["level_ct"], a * len(LEVELS) + n + 1)
                    pe.wait_ge(V.freed, V.np)
                    gj = []
                    for h4 in range(2):
                        bank = A.claim(pe)
                        for h in range(4 * h4, 4 * h4 + 4):
                            last = mm(bank[:, (h % 4) * P:(h % 4 + 1) * P], CTm[:, h, :], Dm[:, h, :])
                        gj.append(A.fill(last))
                    for h4 in range(2):
                        pe.wait_ge(A.freed, gj[h4])
                        if m != LEVELS[-1]:
                            bank = V.claim(pe)
                            for h in range(4 * h4, 4 * h4 + 4):
                                last = mm(bank[:, (h % 4) * P:(h % 4 + 1) * P], DmT[:, h, :], Gm[:, h, :])
                            V.fill(last)
                        bank = V.claim(pe)
                        for h in range(4 * h4, 4 * h4 + 4):
                            last = mm(bank[:, (h % 4) * P:(h % 4 + 1) * P], Gm[:, h, :], DmT[:, h, :])
                        V.fill(last)
                bank = A.claim(pe)
                for c in range(GC):
                    if a:
                        mm(bank[:, c * P:(c + 1) * P], KR[:, c, a, 0, :], Sbd[:, c, :], stop=False)
                    for h in (2 * c, 2 * c + 1):
                        last = mm(bank[:, h * HD:(h + 1) * HD], AT[:, h, 2, :], vtok[:, a, h * HD:(h + 1) * HD],
                                  start=not a)
                nx = A.fill(last)
                pe.wait_ge(A.freed, nx)
                pe.wait_ge(V.freed, V.np)
                bank = A.claim(pe)
                for h in range(NH):
                    last = mm(bank[:, h * HD:(h + 1) * HD], DmT[:, h, :], Xn[:, h * HD:(h + 1) * HD])
                nu = A.fill(last)
                pe.wait_ge(A.freed, nu)
                bank = A.claim(pe)
                for c in range(GC):
                    if a:
                        mm(bank[:, c * P:(c + 1) * P], Sbd[:, c, :], KR[:, c, a, 1, :], stop=False)
                    for h in (2 * c, 2 * c + 1):
                        o = bank[HD * (h % 2):HD * (h % 2) + HD, c * P:(c + 1) * P]
                        mm(o, Ut[:, h * HD:(h + 1) * HD], AT[:, h, 1, :], start=not a, stop=False)
                        last = mm(o, vtok[:, a, h * HD:(h + 1) * HD], AT[:, h, 3, :], start=False)
                A.fill(last)
                if a == 0:
                    bank = V.claim(pe)
                    for c in range(GC):
                        mm(bank[:, c * P:(c + 1) * P], Btok[:, c * P:(c + 1) * P], Ut[:, c * P:(c + 1) * P], stop=False)
                        last = mm(bank[:, c * P:(c + 1) * P], Ktok[:, c * P:(c + 1) * P], vtok[:, 0, c * P:(c + 1) * P], start=False)
                    V.fill(last)
                    pe.wait_ge(S["state_ready"], 1)
            pe.wait_ge(A.freed, A.np)
            for j2 in range(2):
                bank = V.claim(pe)
                V.fill(mm(bank[:, :], C("same_head"), yT[:, 2 * j2:2 * j2 + 2, :], tells=True))
            pe.wait_ge(S["gn_sq"], 1)
            for j2 in range(2):
                bank = A.claim(pe)
                A.fill(mm(bank[:, :], C("same_head"), sq_[:, j2 * 512:(j2 + 1) * 512], tells=True))

            def out_projection(k, late=0):
                pe.wait_ge(S["y_ready"], k + 1)
                for _ in range(N_OUT):
                    project(V, ycat, late)

            out_projection(0)

            norm(1)
            pe.wait_ge(S["u_ready"], 2)
            pe.wait_ge(A.freed, A.np)
            pe.wait_ge(V.freed, V.np)
            pe.wait_ge(S["zero_ready"], 1)
            for b in range(4, 8):
                mm(banks[b][:, :], zero16[:, 0:P], zero16[:, 0:512], stop=False)

            w0 = wn[0]

            def ffn_gu(k, turn, step, first):
                for g in range(2):
                    n = k + g
                    pe.wait_ge(landed[n % RING], turn * 16 + 16 * (n // RING + 1))
                    w = slot(n).rearrange("p (c n) -> p c n", c=DC)
                    bank = banks[2 * g + step % 2]
                    for j in range(2):
                        for c in range(DC):
                            last = mm(bank[:, j * T:(j + 1) * T], w[:, c, j * P:(j + 1) * P], uT[:, c, :],
                                      start=(c == 0), stop=(c == DC - 1))
                    if g == 0:
                        owed.append(used)
                last.then_inc(S["ffn_gu"], 1)
                owed.append(used)

            def ffn_down(k, turn, step):
                pe.wait_ge(landed[k % RING], turn * 16 + 16 * (k // RING + 1))
                w = slot(k).rearrange("p (f n) -> p f n", f=2)
                hm = chunks(hid[step % 2], 2)
                for f in range(2):
                    for c in range(DC):
                        last = mm(banks[4 + c // 2][:, (c % 2) * T:(c % 2 + 1) * T], w[:, f, c * P:(c + 1) * P],
                                  hm[:, f, :], start=False, stop=False)
                last.then_inc(S["ffn_down"], 1)
                owed.append(used)

            ffn_gu(w0, 0, 0, True)
            with pe.Fori(0, (FFN_STEPS - 1) // 2) as it:
                for s in range(2):
                    k = w0 + 2 + 3 * s
                    ffn_gu(k, it, 1 + s, False)
                    pe.wait_ge(S["ffn_hid"], it * 2 + (s + 1))
                    ffn_down(k + 2, it, s)
            wn[0] += N_FFN
            pe.wait_ge(S["ffn_hid"], FFN_STEPS)
            ffn_down(wn[0] - 1, 0, 0)

            norm(2)
            pe.wait_ge(S["u_ready"], 3)
            bank = V.claim(pe)
            wf = Pm("wf").rearrange("p (c n) -> p c n", c=DC)
            for c in range(DC):
                last = mm(bank[0:NH, 0:T], wf[:, c, :], uT[:, c, :], start=(c == 0), stop=(c == DC - 1))
            V.fill(last)
            for which in "qkvQKV":
                for _ in range(2):
                    if which in "vV":
                        project_tok(A, uT)
                    else:
                        project(A, uT)
            pe.wait_ge(A.freed, A.np)
            rope(mq, GC, "full", 0)
            rope(mk, GC, "full", 0)
            pe.wait_ge(S["fox_d"], 1)
            pick = C("pick8")

            def fox_scores(h, bank):
                c, b = h // 2, HD * (h % 2)
                for lo, q0, nk in ((0, 0, P), (P, P, T)):
                    o = bank[:, lo:lo + nk]
                    mm(o, fq[b:b + HD, c, q0:q0 + P], fk[b:b + HD, c, 0:nk], stop=False)
                    mm(o, fd[0:NH, q0:q0 + P], pick[0:NH, h:h + 1].broadcast_to([NH, nk]), start=False, stop=False)
                    last = mm(o, pick[0:NH, h:h + 1].broadcast_to([NH, P]), fnd[0:NH, 0:nk], start=False)
                return last

            attention(fox_scores, fv, NH, None)
            pe.wait_ge(S["rope_done"], 3 + 2 * GC)
            attention(head_scores(mq, mk), mv, 2 * NH, None)
            out_projection(1)

            norm(3)
            pe.wait_ge(S["u_ready"], 4)
            bank = V.claim(pe)
            rw_ = Pm("router").rearrange("p (c n) -> p c n", c=DC)
            for a in range(TT):
                for c in range(DC):
                    last = mm(bank[:, a * E:(a + 1) * E], uT[:, c, a * P:(a + 1) * P], rw_[:, c, :],
                              start=(c == 0), stop=(c == DC - 1))
            V.fill(last)
            for a in range(TT):
                for c4 in range(2):
                    bank = A.claim(pe)
                    for c in range(4):
                        last = tr(bank[:, c * P:(c + 1) * P], uT[:, 4 * c4 + c, a * P:(a + 1) * P])
                    A.fill(last)
            pe.wait_ge(S["router_sel"], 1)
            bank = V.claim(pe)
            mm(bank[:, 0:E], C("before"), selm[:, 0:E])
            mm(bank[:, E:2 * E], C("ones"), selm[:, 0:E], stop=False)
            mm(bank[:, E:2 * E], C("before"), selm[:, E:2 * E], start=False)
            mm(bank[:, 2 * E:3 * E], C("ones"), selm[:, 0:E], stop=False)
            V.fill(mm(bank[:, 2 * E:3 * E], C("ones"), selm[:, E:2 * E], start=False, tells=True))
            pe.wait_ge(A.freed, A.np)
            pe.wait_ge(V.freed, V.np)
            pe.wait_ge(flag_ready, 1)
            passes = pe.value_load(passes_i[0:1, 0:1], min_val=1, max_val=2)

            def moe_gu(k, turn, step, half):
                bank = banks[half]
                for g in range(2):
                    n = k + g
                    pe.wait_ge(landed[n % RING], turn * 16 + 16 * (n // RING + 1))
                    w = slot(n).rearrange("p (c n) -> p c n", c=DC)
                    for j in range(2):
                        for c in range(DC):
                            last = mm(bank[:, (2 * g + j) * P:(2 * g + j + 1) * P], w[:, c, j * P:(j + 1) * P], xg[:, c, :],
                                      start=(c == 0), stop=(c == DC - 1))
                    if g == 0:
                        owed.append(used)
                last.then_inc(S["moe_gu"], 1)
                owed.append(used)

            def moe_down(k, turn, half):
                pe.wait_ge(landed[k % RING], turn * 16 + 16 * (k // RING + 1))
                w = slot(k).rearrange("p (f n) -> p f n", f=2)
                for f in range(2):
                    for o in range(2):
                        last = mm(banks[4 + o][:, :], hid[half][:, f * P:(f + 1) * P], w[:, f, o * 512:(o + 1) * 512],
                                  start=False, stop=False)
                last.then_inc(S["moe_down"], 1)
                owed.append(used)

            with pe.Fori(0, passes) as ps:
                with pe.Fori(0, E) as e:
                    ex_n = pe.snap(ps * E + e)
                    pe.wait_ge(S["onehot"], ex_n + 1)
                    for c4 in range(2):
                        for c in range(4):
                            for a in range(TT):
                                cc = 4 * c4 + c
                                last = mm(banks[6 + c4][:, c * P:(c + 1) * P], ttok[:, a, cc * P:(cc + 1) * P], oh[:, a, :],
                                          start=(a == 0), stop=(a == 1))
                    last.then_inc(S["moe_g"], 1)
                    for o in range(2):
                        mm(banks[4 + o][:, :], zero16[:, 0:P], zero16[:, 0:512], stop=False)
                    pe.wait_ge(S["moe_x"], ex_n + 1)
                    tb = ex_n * (MOE_SLOTS // RING)
                    sb_ = ex_n * MOE_STEPS
                    k0 = N_EARLY
                    moe_gu(k0, tb, 0, 0)
                    with pe.Fori(0, (MOE_STEPS - 2) // 2) as it:
                        tn = pe.snap(tb + it)
                        sn = pe.snap(sb_ + it * 2)
                        for s in range(2):
                            k = k0 + 2 + 3 * s
                            moe_gu(k, tn, 1 + s, (1 + s) % 2)
                            pe.wait_ge(S["moe_hid"], sn + (s + 1))
                            moe_down(k + 2, tn, s % 2)
                    k = k0 + 2 + 3 * (MOE_STEPS - 2)
                    moe_gu(k, tb, 13, 1)
                    pe.wait_ge(S["moe_hid"], sb_ + (MOE_STEPS - 1))
                    moe_down(k + 2, tb, 0)
                    pe.wait_ge(S["moe_hid"], sb_ + MOE_STEPS)
                    moe_down(k + 3, tb, 1)
                    pe.wait_ge(S["onehot_g"], ex_n + 1)
                    for a in range(TT):
                        last = tr(banks[6][:, a * P:(a + 1) * P], ohg[:, a, :])
                    last.then_inc(S["moe_gt"], 1)
                    pe.wait_ge(S["moe_ytok"], ex_n + 1)
                    for c2 in range(4):
                        bank = banks[(7, 2, 3, 7)[c2]]
                        if c2 == 3:
                            pe.wait_ge(S["moe_add"], ex_n * 4 + 1)
                        for c in range(2):
                            cc = 2 * c2 + c
                            last = mm(bank[:, c * T:(c + 1) * T], ysl[:, cc * P:(cc + 1) * P], ohgT)
                        last.then_inc(S["moe_sc"], 1)
                    pe.wait_ge(S["moe_add"], ex_n * 4 + 4)

            norm(4)
            for l in range(2):
                norm(5 + l)
                pe.wait_ge(S["u_ready"], 6 + l)
                for kind in ("q", "q", "k", "k", "v", "v", "g", "g", "x", "g", "q", "k", "v", "g"):
                    if kind == "v":
                        project_tok(A, uT, 1)
                    else:
                        project(A, uT, 1)
                pe.wait_ge(A.freed, A.np)
                rope(hq, GC, "part", 0)
                rope(hk, GC, "part", 0)
                pe.wait_ge(S["conv_done"], l + 1)
                for w in (Pm("gaw"), Pm("gxw")):
                    bank = A.claim(pe)
                    for c in range(2):
                        last = mm(bank[:, c * T:(c + 1) * T], w[:, (2 * l + c) * P:(2 * l + c + 1) * P], xc[:, c, :])
                    A.fill(last)
                pe.wait_ge(S["rope_done"], 3 + 2 * GC * (2 + l))
                attention(head_scores(hq, hk), hv, (3 + l) * NH, None)
                for h in range(4):
                    c, b = h // 2, HD * (h % 2)
                    bank = V.claim(pe)
                    mm(bank[:, 0:T], ck[b:b + HD, c, 0:P], cq[b:b + HD, c, :])
                    V.fill(mm(bank[:, T:T + P], ck[b:b + HD, c, P:T], cq[b:b + HD, c, P:T], tells=True))
                pe.wait_ge(S["stick_n"], l + 1)
                for h in range(4):
                    bank = V.claim(pe)
                    mm(bank[:, 0:T], C("neg_tail"), zl[:, h, 0:T], stop=False)
                    mm(bank[:, P:T], C("neg_ones"), zl[:, h, T:T + P], start=False)
                    V.fill(mm(bank[:, T:T + P], C("neg_tail"), zl[:, h, T:T + P], tells=True))
                pe.wait_ge(S["stick_w"], l + 1)
                for c in range(2):
                    bank = V.claim(pe)
                    for h in (2 * c, 2 * c + 1):
                        o = bank[HD * (h % 2):HD * (h % 2) + HD, :]
                        mm(o[:, 0:T], cv[:, 0, h * HD:(h + 1) * HD], zw[:, h, 0:T], stop=False)
                        last = mm(o[:, P:T], cv[:, 1, h * HD:(h + 1) * HD], zw[:, h, T:T + P], start=False)
                    V.fill(last)
                out_projection(2 + l, 1)
            norm(7)

        @block.scalar
        def _(act):
            st = Step(act, sem("scalar_step"))

            def a_(out, in_, f, **kw):
                return act.activation(out, in_, f, **kw)

            def evac(dst, width=512):
                bank = A.take(act)
                A.free(a_(dst, bank[:, 0:width], ACT.Copy))

            def norm(k, h_done):
                if h_done:
                    act.wait_ge(S["h_ready"], h_done)
                for c4 in range(2):
                    st.say(a_(sq[:, 4 * c4:4 * c4 + 4, :], hT[:, 4 * c4:4 * c4 + 4, :], ACT.Square), "squares_ready")
                bank = A.take(act)
                A.free(a_(rstd(), bank[:, 0:T], ACT.Sqrt, scale=1.0 / D, bias=epscol))
                done["norm", k] = A.nc

            def rstd():
                return yc_[:, 0:T]

            epscol = tiny[:, 130:131]
            gncol = tiny[:, 131:132]
            onecol = tiny[:, 132:133]
            zcol = tiny[:, 133:134]
            act.wait_ge(S["zero_ready"], 1)

            def attention(n0):
                done["attention", n0] = A.nc
                for i in range(NH + 1):
                    if i < NH:
                        n = n0 + i
                        act.wait_ge(S["nmax_ready"], n + 1)
                        st.lone(a_(Lg[i % 3][:, 0:P], Lg[i % 3][:, 0:P], ACT.Exp, bias=nmx[:, i, 0:1], accum_out=zsum[:, i, 0:1]))
                        st.say(a_(Lg[i % 3][:, P:384], Lg[i % 3][:, P:384], ACT.Exp, bias=nmx[:, i, 1:2], accum_out=zsum[:, i, 1:2]), "exp_done")
                    if i >= 1:
                        evac(PTs[(i - 1) % 4], 384)

            act.wait_ge(loaded, 48)
            norm(0, 0)
            for n in range(7):
                evac(raw[:, 2 * n:2 * n + 2, :])
            evac(qlat)
            bank = A.take(act)
            st.lone(a_(kvl, bank[:, 0:T], ACT.Copy))
            A.free(a_(kpe, bank[:, T:2 * T], ACT.Copy))
            st.settle()
            act.wait_ge(A.freed, A.nc)
            st.lone(a_(sq[:, 0:2, :], qlat, ACT.Square))
            st.say(a_(sq[:, 2, :], kvl, ACT.Square), "mla_sq")
            bank = A.take(act)
            st.say(a_(std_m, bank[:, 0:T], ACT.Sqrt, scale=1.0 / 256, bias=epscol), "mla_std")
            A.free(a_(rt1, bank[:, T:2 * T], ACT.Sqrt, scale=1.0 / 128, bias=epscol))
            done["mla_std"] = A.nc
            for j2 in range(2):
                evac(qno[:, 2 * j2:2 * j2 + 2, :])
            evac(qpe)
            for j2 in range(2):
                evac(kno[:, 2 * j2:2 * j2 + 2, :])
            for a in range(TT):
                evac(vml[:, a, :])
            done["mla"] = A.nc
            attention(0)

            act.wait_ge(S["decay_in"], 1)
            st.say(a_(lw[0:HD], rw[0:HD, 12, :], ACT.Tanh), "lora_in")
            st.lone(a_(lw[HD:P], rw[HD:P, 12, :], ACT.Copy))
            st.settle()
            st.say(a_(sg, rw[:, 13, :], ACT.Sigmoid), "lora_in")
            for dst, bias in ((logd, "w0"), (iclr, "a0"), (g_, None)):
                for j2 in range(2):
                    bank = A.take(act)
                    for j in range(2):
                        c = 2 * j2 + j
                        if bias:
                            ins = a_(dst[:, c, :], bank[:, j * T:(j + 1) * T], ACT.Sigmoid, bias=col(bias, c))
                        else:
                            ins = a_(dst[:, c, :], bank[:, j * T:(j + 1) * T], ACT.Copy)
                        if j:
                            A.free(ins)
                        else:
                            st.lone(ins)
            st.settle()
            done["lora"] = A.nc
            act.wait_ge(S["kk_in"], 1)
            st.say(a_(sq_[:, 0:1024], kkr, ACT.Square), "kk_sq")
            for j2 in range(2):
                bank = A.take(act)
                A.free(a_(kk[:, 2 * j2:2 * j2 + 2, :], bank[:, :], ACT.Sqrt))
            done["kk"] = A.nc
            act.wait_ge(S["exp_in"], 1)
            st.lone(a_(E1, cs, ACT.Exp))
            st.lone(a_(E2, csx, ACT.Exp))
            st.lone(a_(E3, cs, ACT.Exp, scale=-1.0))
            st.settle()
            act.wait_ge(S["exp_in"], 2)
            st.say(a_(fend, tiny[:, 140:140 + GC], ACT.Exp), "exp_out")
            for a in range(TT):
                evac(vtok[:, a, :])
            evac(Btok)
            evac(Ktok)
            for a in range(TT):
                done["levels", a] = A.nc
                for m in LEVELS:
                    for h4 in range(2):
                        evac(Gm[:, 4 * h4:4 * h4 + 4, :])
                bank = A.take(act)
                A.free(a_(Xn, bank[:, :], ACT.Copy, scale=-1.0))
                evac(Ut)
                bank = A.take(act)
                A.free(a_(yT[:, :, a * P:(a + 1) * P], bank[:, :].rearrange("p (c t) -> p c t", c=GC), ACT.Copy))
                done["y", a] = A.nc
            act.wait_ge(S["gn_in"], 1)
            st.say(a_(sq_[:, 0:1024], yT, ACT.Square), "gn_sq")
            for j2 in range(2):
                bank = A.take(act)
                A.free(a_(cs[:, 2 * j2:2 * j2 + 2, :], bank[:, :], ACT.Sqrt, scale=1.0 / HD, bias=gncol))
            done["gn"] = A.nc

            norm(1, 1)
            with act.Fori(0, FFN_STEPS // 2) as it:
                for s in range(2):
                    act.wait_ge(S["ffn_gu"], it * 2 + (s + 1))
                    a_(sigb[s], banks[s][:, :], ACT.Sigmoid).then_inc(S["ffn_sig"], 1)
            act.wait_ge(S["ffn_gu"], FFN_STEPS)
            a_(sigb[0], banks[0][:, :], ACT.Sigmoid).then_inc(S["ffn_sig"], 1)

            norm(2, 2)
            for dst in (fq, fk, fv, mq, mk, mv):
                for n in range(2):
                    if dst is fv or dst is mv:
                        bank = A.take(act)
                        A.free(a_(dst[:, :, n * T:(n + 1) * T], bank[:, :].rearrange("p (a n) -> p a n", a=TT), ACT.Copy))
                    else:
                        evac(dst[:, 2 * n:2 * n + 2, :])
            done["l1"] = A.nc
            act.wait_ge(S["fox_z"], 1)
            st.own(a_(fe[0:NH], fl[0:NH], ACT.Exp, scale=-1.0))
            st.say(a_(fe[0:NH], fe[0:NH], ACT.Ln, bias=tiny[0:NH, 132:133]), "fox_e")
            attention(NH)
            attention(2 * NH)

            norm(3, 3)
            for a in range(TT):
                for c4 in range(2):
                    evac(ttok[:, a, c4 * 512:(c4 + 1) * 512])
            act.wait_ge(S["router_l"], 1)
            st.say(a_(ex, ex, ACT.Exp), "router_e")
            act.wait_ge(flag_ready, 1)
            passes = act.value_load(passes_i[0:1, 0:1], min_val=1, max_val=2)
            with act.Fori(0, passes) as ps:
                with act.Fori(0, E) as e:
                    ex_n = act.snap(ps * E + e)
                    act.wait_ge(S["moe_g"], ex_n + 1)
                    a_(xg[:, 0:4, :], banks[6][:, :], ACT.Copy).then_inc(S["moe_act"], 1)
                    a_(xg[:, 4:8, :], banks[7][:, :], ACT.Copy).then_inc(S["moe_x"], 1)
                    with act.Fori(0, MOE_STEPS // 2) as it:
                        for s in range(2):
                            act.wait_ge(S["moe_gu"], ex_n * MOE_STEPS + it * 2 + (s + 1))
                            a_(sigb[s][:, 0:T], banks[s][:, 0:T], ACT.Sigmoid).then_inc(S["moe_sig"], 1)
                    act.wait_ge(S["moe_gt"], ex_n + 1)
                    act.wait_ge(S["moe_down"], ex_n * MOE_STEPS + MOE_STEPS)
                    a_(ohgT, banks[6][:, 0:T], ACT.Copy).then_inc(S["moe_act"], 1)
                    a_(ysl[:, 0:512], banks[4][:, :], ACT.Copy).then_inc(S["moe_act"], 1)
                    a_(ysl[:, 512:1024], banks[5][:, :], ACT.Copy).then_inc(S["moe_ytok"], 1)

            norm(4, 4)
            for l in range(2):
                norm(5 + l, 5 + l)
                for dst, n in ((hq, 0), (hq, 2), (hk, 0), (hk, 2), (hv, 0), (hv, 1), (gate, 0), (gate, 2),
                               (bx, 0), (gate, 4), (cq, 0), (ck, 0), (cv, 0), (gate, 6)):
                    bank = A.take(act)
                    if dst is hv or dst is cv:
                        A.free(a_(dst[:, :, n * T:(n + 1) * T], bank[:, :].rearrange("p (a n) -> p a n", a=TT), ACT.Copy))
                    elif dst is gate:
                        st.lone(a_(gsig[:, n:n + 2, :], bank[:, :], ACT.Sigmoid))
                        A.free(a_(dst[:, n:n + 2, :], bank[:, :], ACT.Copy))
                    else:
                        A.free(a_(dst[:, n:n + 2, :], bank[:, :], ACT.Copy))
                st.settle()
                done["hybrid", l] = A.nc
                act.wait_ge(S["lam_in"], l + 1)
                st.say(a_(lam_t[:, 2:4], lam_t[:, 0:2], ACT.Exp, scale=-1.0), "lam_e")
                for dst, bias in ((lr, "gab"), (li, "gxb")):
                    bank = A.take(act)
                    st.lone(a_(dst[:, 0, :], bank[:, 0:T], ACT.Sigmoid, bias=col(bias, 2 * l)))
                    A.free(a_(dst[:, 1, :], bank[:, T:2 * T], ACT.Sigmoid, bias=col(bias, 2 * l + 1)))
                st.settle()
                act.wait_ge(A.freed, A.nc)
                act.wait_ge(S["lam_c"], l + 1)
                for c in range(2):
                    st.lone(a_(lt[:, c, :], lr[:, c, :], ACT.Tanh, scale=lam_t[:, 20 + c:21 + c]))
                for c in range(2):
                    ins = a_(la[:, c, :], lr[:, c, :], ACT.Exp, scale=lam_t[:, 20 + c:21 + c])
                    if c:
                        st.say(ins, "lru_a")
                    else:
                        st.lone(ins)
                act.wait_ge(S["lru_q"], l + 1)
                st.say(a_(lq, lq, ACT.Sqrt), "lru_s")
                attention((3 + l) * NH)
                act.wait_ge(S["stick_z"], l + 1)
                st.own(a_(zl, zb, ACT.Abs))
                st.own(a_(zl, zl, ACT.Exp, scale=-1.0))
                st.say(a_(zl, zl, ACT.Ln, bias=onecol), "stick_l")
                act.wait_ge(S["stick_arg"], l + 1)
                st.say(a_(zw, zw, ACT.Exp), "stick_w")
            norm(7, 7)

        @block.vector
        def _(dve):
            st = Step(dve, sem("vector_step"))
            tt, ts, stt, cp = dve.tensor_tensor, dve.tensor_scalar, dve.scalar_tensor_tensor, dve.tensor_copy
            rstd = yc_[:, 0:T]

            st.lone(dve.memset(tiny[:, 130:131], EPS))
            st.lone(dve.memset(tiny[:, 131:132], GN_EPS))
            st.lone(dve.memset(tiny[:, 132:133], 1.0))
            st.lone(dve.memset(tiny[:, 133:134], 0.0))
            st.lone(dve.memset(zero16[:, :], 0.0))
            st.settle()
            st.say(dve.memset(tiny[:, 134:135], 0.0), "zero_ready")

            def norm(k, a_count, dst=None, name="u_ready"):
                dst = uT if dst is None else dst
                dve.wait_ge(A.freed, a_count)
                st.own(dve.reciprocal(rstd, rstd))
                for c in range(DC):
                    ins = stt(dst[:, c, :], hT[:, c, :], col("gains", k * DC + c), rstd, ALU.mult, ALU.mult)
                    if c == DC - 1:
                        st.say(ins, name)
                    else:
                        st.lone(ins)
                st.settle()

            def attention(n0, scale, mask, y0, post=None):
                m384 = C(mask)
                for i in range(NH + 3):
                    if i < NH:
                        bank = V.take(dve)
                        if i >= 3:
                            pass
                        if i >= 3:
                            dve.wait_ge(A.filled, done["attention", n0] + i - 2)
                        V.free(stt(Lg[i % 3], bank[:, 0:384], scale, m384, ALU.mult, ALU.add))
                        dve.wait_ge(V.freed, V.nc)
                        st.lone(dve.tensor_reduce(nmx[:, i, 0:1], Lg[i % 3][:, 0:P], AX_X, ALU.max, negate=True))
                        st.say(dve.tensor_reduce(nmx[:, i, 1:2], Lg[i % 3][:, P:384], AX_X, ALU.max, negate=True), "nmax_ready")
                    if 1 <= i <= NH:
                        dve.wait_ge(S["exp_done"], n0 + i)
                        st.say(dve.reciprocal(rz[:, i - 1, :], zsum[:, i - 1, :]), "rz_ready")
                    if i >= 3 and (i - 2) % 2 == 1:
                        bank = V.take(dve)
                        V.free(cp(ycat[:, y0 + (i - 2) // 2, :], bank[:, 0:T]))

            def rope(x, n, which, cos, sin, ta, tb):
                for c in range(n):
                    bank = V.take(dve)
                    V.free(tt(ta, bank[:, 0:T], C(sin), ALU.mult))
                    st.own(tt(tb, x[:, c, :], C(cos), ALU.mult))
                    dve.wait_ge(V.freed, V.nc)
                    st.say(tt(x[:, c, :], ta, tb, ALU.add), "rope_done")
                    st.wait_said("rope_done")

            def residual():
                for n in range(N_OUT):
                    bank = V.take(dve)
                    ins = tt(hT[:, 2 * n:2 * n + 2, :], hT[:, 2 * n:2 * n + 2, :], bank[:, :], ALU.add)
                    V.free(ins)
                dve.wait_ge(V.freed, V.nc)
                st.say(dve.memset(tiny[:, 135:136], 0.0), "h_ready")

            dve.wait_ge(loaded, 48)
            norm(0, done["norm", 0])

            dve.wait_ge(A.freed, done["mla_std"])
            st.own(dve.reciprocal(std_m, std_m))
            st.own(dve.reciprocal(rt1, rt1))
            st.lone(stt(qn[:, 0, :], qlat[:, 0, :], col("qnorm", 0), std_m, ALU.mult, ALU.mult))
            st.say(stt(qn[:, 1, :], qlat[:, 1, :], col("qnorm", 1), std_m, ALU.mult, ALU.mult), "mla_q")
            st.say(stt(kvn, kvl, col("kvnorm", 0), rt1, ALU.mult, ALU.mult), "mla_kv")
            st.wait_said("mla_kv")
            dve.wait_ge(A.freed, done["mla"])
            rope(qpe, 2, "mla", "cos_mla", "sin_mla", rt1, rt2)
            bank = V.take(dve)
            V.free(tt(rt1, bank[:, 0:T], C("sin_mla"), ALU.mult))
            st.own(tt(rt2, kpe, C("cos_mla"), ALU.mult))
            dve.wait_ge(V.freed, V.nc)
            st.say(tt(kpe, rt1, rt2, ALU.add), "rope_done")
            attention(0, (HD + 32) ** -0.5, "causal", GC)
            dve.wait_ge(V.freed, V.nc)

            st.lone(tt(rw[:, :, 1:T], raw[:, :, 0:T - 1], raw[:, :, 1:T], ALU.subtract))
            st.lone(ts(rw[:, :, 0:1], raw[:, :, 0:1], -1.0, None, ALU.mult))
            st.settle()
            for c in (12, 13) + tuple(range(12)):
                st.lone(stt(rw[:, c, :], rw[:, c, :], col("mu", c), raw[:, c, :], ALU.mult, ALU.add))
            st.settle()
            st.say(dve.memset(tiny[:, 136:137], 0.0), "decay_in")
            r_, k_, v_ = rw[:, 0:4, :], rw[:, 4:8, :], rw[:, 8:12, :]
            for c in range(GC):
                ins = ts(kkr[:, c, :], rw[:, 4 + c, :], col("kkp", c), None, ALU.mult)
                if c == GC - 1:
                    st.say(ins, "kk_in")
                else:
                    st.lone(ins)
            st.lone(ts(omka, Pm("kap"), -1.0, 1.0, ALU.mult, ALU.add))
            st.settle()
            st.wait_said("kk_in")
            dve.wait_ge(A.freed, done["lora"])
            st.own(ts(logd, logd, -float(np.exp(-0.5)), None, ALU.mult))
            for c in range(GC):
                for a in range(TT):
                    st.lone(dve.tensor_tensor_scan(cs[:, c, a * P:(a + 1) * P], C("ones"), logd[:, c, a * P:(a + 1) * P],
                                                   0.0, ALU.mult, ALU.add))
            st.settle()
            cs8 = cs.rearrange("p c (a t) -> p (c a) t", a=TT)
            mid = tiny[:, 144:152]
            st.own(cp(mid, cs8[:, :, HD - 1:HD].rearrange("p n o -> p (n o)")))
            st.own(tt(cs8, cs8, mid.rearrange("p (n o) -> p n o", o=1).broadcast_to([P, 8, P]), ALU.subtract))
            st.say(tt(csx, cs, logd, ALU.subtract), "exp_in")
            st.own(tt(tiny[:, 140:144], cs[:, :, P - 1:P].rearrange("p c o -> p (c o)"),
                      mid.rearrange("p (c a) -> p c a", a=TT)[:, :, 1], ALU.add))
            st.say(dve.memset(tiny[:, 137:138], 0.0), "exp_in")
            for c in range(GC):
                st.lone(ts(bon[:, c, :], iclr[:, c, :], col("kap", c), omka[:, c:c + 1], ALU.mult, ALU.add))
            st.settle()
            dve.wait_ge(A.freed, done["kk"])
            st.own(tt(k2, k_, bon, ALU.mult))
            st.own(ts(kk, kk, 1e-12, None, ALU.max))
            st.own(dve.reciprocal(kk, kk))
            st.own(tt(kk, kk, kkr, ALU.mult))
            for c in range(GC):
                ins = stt(bon[:, c, :], rw[:, c, :], col("rkp", c), k2[:, c, :], ALU.mult, ALU.mult)
                if c == GC - 1:
                    st.say(ins, "bonus_in")
                else:
                    st.lone(ins)
            dve.wait_ge(S["exp_out"], 1)
            v4 = lambda x: x.rearrange("p c (a t) -> p c a t", a=TT)
            st.lone(tt(KR[:, :, :, 0, :], v4(kk), v4(E2), ALU.mult))
            st.lone(tt(KR[:, :, :, 1, :], v4(r_), v4(E1), ALU.mult))
            st.own(tt(Ks, k2, E3, ALU.mult))
            st.own(tt(Bs, kk, iclr, ALU.mult))
            st.own(tt(Bs, Bs, E3, ALU.mult))
            st.say(dve.memset(tiny[:, 138:139], 0.0), "keys_ready")
            for j2 in range(2):
                bank = V.take(dve)
                V.free(tt(csx[:, 2 * j2:2 * j2 + 2, :], v_[:, 2 * j2:2 * j2 + 2, :], bank[:, :], ALU.mult))

            idb = C("ident").rearrange("p (o s) -> p o s", o=1).broadcast_to([P, 4, P])
            for a in range(TT):
                if a:
                    dve.wait_ge(A.freed, done["y", 0])
                for h in range(NH):
                    bank = V.take(dve)
                    V.free(tt(AT[:, h].rearrange("p q s -> p (q s)"), bank[:, :], C("mask4"), ALU.mult))
                dve.wait_ge(V.freed, V.nc)
                for par_ in range(2):
                    hs = slice(par_, NH, 2)
                    bank = V.take(dve)
                    b3 = bank[:, :].rearrange("p (h s) -> p h s", h=4)
                    l1 = C("level1").rearrange("p (o s) -> p o s", o=1).broadcast_to([P, 4, P])
                    l1T = C("levelT1").rearrange("p (o s) -> p o s", o=1).broadcast_to([P, 4, P])
                    V.free(tt(Dm[:, hs, :], b3, l1, ALU.mult))
                    dve.wait_ge(V.freed, V.nc)
                    st.own(tt(Dm[:, hs, :], idb, Dm[:, hs, :], ALU.subtract))
                    st.own(tt(DmT[:, hs, :], AT[:, hs, 0, :], l1T, ALU.mult))
                    st.own(tt(DmT[:, hs, :], idb, DmT[:, hs, :], ALU.subtract))
                for n, m in enumerate(LEVELS):
                    lT = C(f"levelT{m}").rearrange("p (o s) -> p o s", o=1).broadcast_to([P, NH, P])
                    if n:
                        dve.wait_ge(A.freed, done["levels", a] + 2 * n)
                    st.say(tt(CTm, AT[:, :, 0, :], lT, ALU.mult), "level_ct")
                    for h4 in range(2):
                        hs = slice(4 * h4, 4 * h4 + 4)
                        if m != LEVELS[-1]:
                            b1 = V.take(dve)
                            V.free(tt(Dm[:, hs, :], Dm[:, hs, :], b1[:, :].rearrange("p (h s) -> p h s", h=4), ALU.subtract))
                        b2 = V.take(dve)
                        V.free(tt(DmT[:, hs, :], DmT[:, hs, :], b2[:, :].rearrange("p (h s) -> p h s", h=4), ALU.subtract))
                    dve.wait_ge(V.freed, V.nc)
                if a == 0:
                    bank = V.take(dve)
                    dve.wait_ge(S["exp_out"], 1)
                    for c in range(GC):
                        ins = stt(Sbd[:, c, :], bank[:, c * P:(c + 1) * P], fend[:, c:c + 1], C("same_head"), ALU.mult, ALU.mult)
                        if c == GC - 1:
                            V.free(ins)
                        else:
                            st.lone(ins)
                    st.settle()
                    dve.wait_ge(V.freed, V.nc)
                    st.say(dve.memset(tiny[:, 139:140], 0.0), "state_ready")
            dve.wait_ge(A.freed, done["y", 1])
            for j2 in range(2):
                bank = V.take(dve)
                y2 = yT[:, 2 * j2:2 * j2 + 2, :]
                V.free(stt(y2, bank[:, :].rearrange("p (j t) -> p j t", j=2), -1.0 / HD, y2, ALU.mult, ALU.add))
            dve.wait_ge(V.freed, V.nc)
            st.say(dve.memset(tiny[:, 152:153], 0.0), "gn_in")
            dve.wait_ge(A.freed, done["gn"])
            st.own(dve.reciprocal(cs, cs))
            st.own(tt(yT, yT, cs, ALU.mult))
            for c in range(GC):
                st.lone(ts(yT[:, c, :], yT[:, c, :], col("lnxg", c), col("lnxb", c), ALU.mult, ALU.add))
            st.settle()
            st.own(tt(yT, yT, csx, ALU.add))
            st.own(tt(ycat[:, 0:GC, :], yT, g_, ALU.mult))
            st.say(dve.memset(tiny[:, 153:154], 0.0), "y_ready")
            residual()

            norm(1, done["norm", 1])

            def ffn_step(s, n_sig, first):
                dve.wait_ge(S["ffn_sig"], n_sig)
                tt(gtmp[s], sigb[s], banks[s][:, :], ALU.mult).then_inc(S["ffn_mid"], 1)
                dve.wait_ge(S["ffn_mid"], n_sig)
                tt(hid[s], gtmp[s], banks[2 + s][:, :], ALU.mult).then_inc(S["ffn_hid"], 1)

            ffn_step(0, 1, True)
            ffn_step(1, 2, True)
            with dve.Fori(1, FFN_STEPS // 2) as it:
                for s in range(2):
                    dve.wait_ge(S["ffn_down"], it * 2 + (s - 1))
                    ffn_step(s, it * 2 + (s + 1), False)
            dve.wait_ge(S["ffn_down"], FFN_STEPS - 2)
            ffn_step(0, FFN_STEPS, False)
            dve.wait_ge(S["ffn_down"], FFN_STEPS)
            for n in range(4):
                st.lone(tt(hT[:, 2 * n:2 * n + 2, :], hT[:, 2 * n:2 * n + 2, :], banks[4 + n][:, :], ALU.add))
            st.settle()
            st.say(dve.memset(tiny[:, 154:155], 0.0), "h_ready")

            norm(2, done["norm", 2])
            bank = V.take(dve)
            z8 = fz[0:NH]
            V.free(ts(z8, bank[0:NH, 0:T], par[0:NH, par_at["foxbf"][0]:par_at["foxbf"][0] + 1], None, ALU.add))
            dve.wait_ge(V.freed, V.nc)
            st.own(ts(fe[0:NH], z8, -1.0, None, ALU.mult))
            st.say(tt(fl[0:NH], fe[0:NH], z8, ALU.max), "fox_z")
            st.own(ts(z8, z8, 0.0, None, ALU.min))
            dve.wait_ge(S["fox_e"], 1)
            st.own(tt(z8, z8, fe[0:NH], ALU.subtract))
            st.own(ts(fl[0:NH], z8, 0.0, 1.0, ALU.mult, ALU.add))
            st.own(dve.tensor_tensor_scan(fd[0:NH], fl[0:NH], z8, 0.0, ALU.mult, ALU.add))
            st.say(ts(fnd[0:NH], fd[0:NH], -1.0, None, ALU.mult), "fox_d")
            dve.wait_ge(A.freed, done["l1"])
            rope(mq, GC, "full", "cos_full", "sin_full", r1a, r1b)
            rope(mk, GC, "full", "cos_full", "sin_full", r1a, r1b)
            attention(NH, HD ** -0.5, "causal", 0)
            attention(2 * NH, HD ** -0.5, "causal", GC)
            dve.wait_ge(V.freed, V.nc)
            st.say(dve.memset(tiny[:, 155:156], 0.0), "y_ready")
            residual()

            norm(3, done["norm", 3])
            bank = V.take(dve)
            V.free(cp(lg, bank[:, 0:TT * E]))
            dve.wait_ge(V.freed, V.nc)
            l3 = lg.rearrange("p (a e) -> p a e", a=TT)
            m3 = lambda x: x.rearrange("p (a o) -> p a o", o=1).broadcast_to([P, TT, E])
            st.own(dve.tensor_reduce(m0, l3, AX_X, ALU.max))
            st.say(tt(ex.rearrange("p (a e) -> p a e", a=TT), l3, m3(m0), ALU.subtract), "router_l")
            low = C("lower").rearrange("p (e j) -> p e j", e=E)
            for a in range(TT):
                la_ = lg[:, a * E:(a + 1) * E]
                lj = la_.rearrange("p (o j) -> p o j", o=1).broadcast_to([P, E, E])
                le = la_.rearrange("p (e o) -> p e o", o=1).broadcast_to([P, E, E])
                b1 = big[:, a * E * E:(a + 1) * E * E].rearrange("p (e j) -> p e j", e=E)
                b2 = big2[:, a * E * E:(a + 1) * E * E].rearrange("p (e j) -> p e j", e=E)
                st.lone(tt(b1, lj, le, ALU.is_gt))
                st.own(tt(b2, lj, le, ALU.is_equal))
                st.own(tt(b2, b2, low, ALU.mult))
                st.own(tt(b1, b1, b2, ALU.add))
                st.own(dve.tensor_reduce(rank[:, a * E:(a + 1) * E], b1, AX_X, ALU.add))
            st.say(ts(selm, rank, 1.5, None, ALU.is_lt), "router_sel")
            st.wait_said("router_sel")
            dve.wait_ge(S["router_e"], 1)
            st.own(tt(comb, ex, selm, ALU.mult))
            c3 = comb.rearrange("p (a e) -> p a e", a=TT)
            st.own(dve.tensor_reduce(den, c3, AX_X, ALU.add))
            st.own(dve.reciprocal(den, den))
            st.own(tt(c3, c3, m3(den), ALU.mult))
            bank = V.take(dve)
            st.lone(cp(posm, bank[:, 0:2 * E]))
            V.free(cp(cnt, bank[:, 2 * E:3 * E]))
            st.settle()
            dve.wait_ge(V.freed, V.nc)
            st.own(ts(rank, selm, -1e4, 1e4, ALU.mult, ALU.add))
            st.own(tt(posm, posm, rank, ALU.add))
            for a in range(TT):
                st.lone(cp(table[:, 0:E, a], posm[:, a * E:(a + 1) * E]))
                st.lone(ts(table[:, E:2 * E, a], posm[:, a * E:(a + 1) * E], -float(P), None, ALU.add))
                st.lone(cp(table[:, 0:E, 2 + a], comb[:, a * E:(a + 1) * E]))
                st.lone(cp(table[:, E:2 * E, 2 + a], comb[:, a * E:(a + 1) * E]))
            st.own(dve.tensor_reduce(mcnt[:, 0:1], cnt, AX_X, ALU.max))
            st.own(ts(mcnt[:, 1:2], mcnt[:, 0:1], P + 0.5, 1.0, ALU.is_gt, ALU.add))
            cp(passes_i[:, :], mcnt[:, 1:2]).then_inc(flag_ready, 1)
            dve.wait_ge(flag_ready, 1)
            passes = dve.value_load(passes_i[0:1, 0:1], min_val=1, max_val=2)
            with dve.Fori(0, passes) as ps:
                with dve.Fori(0, E) as e:
                    ex_n = dve.snap(ps * E + e)
                    cp(cur, table[:, bass.ds(ex_n, 1), :].rearrange("p o k -> p (o k)")).then_inc(S["moe_tab"], 1)
                    dve.wait_ge(S["moe_tab"], ex_n + 1)
                    ts(oh[:, 0, :], C("slot_iota"), cur[:, 0:1], None, ALU.is_equal).then_inc(S["moe_vec"], 1)
                    ts(oh[:, 1, :], C("slot_iota"), cur[:, 1:2], None, ALU.is_equal).then_inc(S["onehot"], 1)
                    dve.wait_ge(S["onehot"], ex_n + 1)
                    ts(ohg[:, 0, :], oh[:, 0, :], cur[:, 2:3], None, ALU.mult).then_inc(S["moe_vec"], 1)
                    ts(ohg[:, 1, :], oh[:, 1, :], cur[:, 3:4], None, ALU.mult).then_inc(S["onehot_g"], 1)

                    def step(s, n):
                        dve.wait_ge(S["moe_sig"], n)
                        tt(gtmp[s][:, 0:T], sigb[s][:, 0:T], banks[s][:, 0:T], ALU.mult).then_inc(S["moe_mid"], 1)
                        dve.wait_ge(S["moe_mid"], n)
                        tt(hid[s][:, 0:T], gtmp[s][:, 0:T], banks[s][:, T:2 * T], ALU.mult).then_inc(S["moe_hid"], 1)

                    base = dve.snap(ex_n * MOE_STEPS)
                    step(0, base + 1)
                    step(1, base + 2)
                    with dve.Fori(1, MOE_STEPS // 2) as it:
                        for s in range(2):
                            dve.wait_ge(S["moe_down"], base + it * 2 + (s - 1))
                            step(s, base + it * 2 + (s + 1))
                    for c2 in range(4):
                        bank = banks[(7, 2, 3, 7)[c2]]
                        dve.wait_ge(S["moe_sc"], ex_n * 4 + (c2 + 1))
                        tt(hT[:, 2 * c2:2 * c2 + 2, :], hT[:, 2 * c2:2 * c2 + 2, :], bank[:, :], ALU.add).then_inc(S["moe_add"], 1)
            st.say(dve.memset(tiny[:, 160:161], 0.0), "moe_end")
            st.say(dve.memset(tiny[:, 156:157], 0.0), "h_ready")

            norm(4, done["norm", 4], dst=hT, name="u_ready")
            st.wait_said("u_ready")
            st.say(dve.memset(tiny[:, 157:158], 0.0), "h_ready")
            for l in range(2):
                norm(5 + l, done["norm", 5 + l])
                lam = Pm("lam")[:, 2 * l:2 * l + 2]
                L = lambda i: lam_t[:, 2 * i:2 * i + 2]
                st.own(ts(L(2), lam, -1.0, None, ALU.mult))
                st.say(tt(L(0), L(2), lam, ALU.max), "lam_in")
                dve.wait_ge(S["lam_e"], l + 1)
                st.own(ts(L(3), L(1), 2.0, None, ALU.add))
                st.own(dve.reciprocal(L(3), L(3)))
                st.own(tt(L(3), L(3), L(1), ALU.mult))
                st.own(tt(L(4), L(3), L(3), ALU.mult))
                st.own(ts(L(5), L(4), 1.0 / 17, 1.0 / 15, ALU.mult, ALU.add))
                for k in (13, 11, 9, 7, 5, 3, 1):
                    st.own(tt(L(5), L(5), L(4), ALU.mult))
                    st.own(ts(L(5), L(5), 1.0 / k, None, ALU.add))
                st.own(tt(L(5), L(5), L(3), ALU.mult))
                st.own(ts(L(6), lam, 0.0, None, ALU.min))
                st.own(stt(L(6), L(5), -2.0, L(6), ALU.mult, ALU.add))
                st.say(ts(L(10), L(6), 8.0, None, ALU.mult), "lam_c")

                dve.wait_ge(A.freed, done["hybrid", l])
                for c in range(2):
                    w = lambda j: col("convw", (2 * l + c) * 4 + j)
                    st.own(ts(xc[:, c, :], bx[:, c, :], w(3), col("convb", 2 * l + c), ALU.mult, ALU.add))
                    for j in range(3):
                        sh = 3 - j
                        st.own(stt(xc[:, c, sh:T], bx[:, c, 0:T - sh], w(j), xc[:, c, sh:T], ALU.mult, ALU.add))
                st.say(tt(gate, gate, gsig, ALU.mult), "conv_done")
                rope(hq, GC, "part", "cos_part", "sin_part", hra, hrb)
                rope(hk, GC, "part", "cos_part", "sin_part", hra, hrb)
                dve.wait_ge(S["lru_a"], l + 1)
                st.own(ts(lq, lt, -1.0, 1.0, ALU.mult, ALU.add))
                st.own(dve.reciprocal(lq, lq))
                st.say(stt(lq, lt, -2.0, lq, ALU.mult, ALU.mult), "lru_q")
                st.own(tt(lu, li, xc, ALU.mult))
                dve.wait_ge(S["lru_s"], l + 1)
                st.own(tt(lu, lu, lq, ALU.mult))
                for c in range(2):
                    st.lone(dve.tensor_tensor_scan(ycat[:, GC + c, :], la[:, c, :], lu[:, c, :], 0.0, ALU.mult, ALU.add))
                attention((3 + l) * NH, HD ** -0.5, "dilated", 0)
                for h in range(4):
                    bank = V.take(dve)
                    V.free(ts(zb[:, h, :], bank[:, 0:384], HD ** -0.5, None, ALU.mult))
                dve.wait_ge(V.freed, V.nc)
                st.say(dve.memset(tiny[:, 158:159], 0.0), "stick_z")
                dve.wait_ge(S["stick_l"], l + 1)
                st.own(stt(zl, zb, 0.0, zl, ALU.max, ALU.add))
                m01 = C("stick01").rearrange("p (o n) -> p o n", o=1).broadcast_to([P, 4, 384])
                madd = C("stick_add").rearrange("p (o n) -> p o n", o=1).broadcast_to([P, 4, 384])
                st.say(tt(zl, zl, m01, ALU.mult), "stick_n")
                st.own(tt(zb, zb, madd, ALU.add))
                for h in range(4):
                    bank = V.take(dve)
                    V.free(tt(zw[:, h, :], zb[:, h, :], bank[:, 0:384], ALU.add))
                dve.wait_ge(V.freed, V.nc)
                st.say(dve.memset(tiny[:, 159:160], 0.0), "stick_arg")
                for c in range(2):
                    bank = V.take(dve)
                    V.free(cp(ycat[:, GC + 2 + c, :], bank[:, 0:T]))
                dve.wait_ge(V.freed, V.nc)
                st.settle()
                st.wait_said("conv_done")
                st.say(tt(ycat, ycat, gate, ALU.mult), "y_ready")
                residual()
            norm(7, done["norm", 7], name="out_ready")

        @block.gpsimd
        def _(pool):
            st = Step(pool, sem("pool_step"))
            for n in range(5 * NH):
                i = n % NH
                pool.wait_ge(S["rz_ready"], n + 1)
                st.lone(pool.tensor_scalar(Lg[i % 3][:, 0:P], Lg[i % 3][:, 0:P], rz[:, i, 0:1], 1.0, ALU.mult, ALU.mult))
                st.say(pool.tensor_scalar(Lg[i % 3][:, P:384], Lg[i % 3][:, P:384], rz[:, i, 1:2], 1.0, ALU.mult, ALU.mult), "prob_ready")



def kernel(**inputs):
    import concourse.bacc as bacc
    from concourse.bass_utils import run_bass_kernel_spmd

    w = {k: np.asarray(v) for k, v in inputs.items()}

    def feature_major(v):
        return v.reshape(-1, P).T

    def slots(m):
        return m.reshape(DC, P, -1, SLOT_COLS).transpose(2, 1, 0, 3).reshape(-1, P, SLOT)

    def down_slots(m):
        return m.reshape(-1, 2, P, D).transpose(0, 2, 1, 3).reshape(-1, P, SLOT)

    def swiglu_slots(g, u, d):
        g, u, d = slots(g), slots(u), down_slots(d)
        order = [g[0], u[0]]
        for i in range(1, len(g)):
            order += [g[i], u[i], d[i - 1]]
        return np.stack(order + [d[-1]])

    w_in0 = w["w_in_0"]
    w_in0 = np.concatenate([w_in0[:, :1792 + 256 + 128], np.tile(w_in0[:, 1792 + 384:], (1, 4))], 1)
    w_in1 = w["w_in_1"]
    stream = [slots(w_in0), slots(w["w_out_0"]),
              swiglu_slots(w["ffn_wg_0"], w["ffn_wu_0"], w["ffn_wd_0"]),
              slots(w_in1[:, :3 * GW]), slots(w_in1[:, 3 * GW + NH:]), slots(w["w_out_1"])]
    stream += [swiglu_slots(w["moe_wg_1"][e], w["moe_wu_1"][e], w["moe_wd_1"][e]) for e in range(E)]
    for l in range(2):
        stream += [slots(w["w_in_2"][l]), slots(w["w_out_2"][l])]
    stream = np.concatenate(stream)

    def uq():
        m = w["mla_wuq_0"].reshape(256, NH, 96)
        m = np.concatenate([m[:, :, :64].reshape(256, 512), m[:, :, 64:].reshape(256, 256)], 1)
        return m.reshape(2, P, 768).transpose(1, 0, 2).reshape(P, -1)

    def ukv():
        m = w["mla_wukv_0"].reshape(P, NH, 128)
        return np.concatenate([m[:, :, :64].reshape(P, 512), m[:, :, 64:].reshape(P, 512)], 1)

    def block_diagonal(m):
        out = np.zeros((P, 2, 2, P), np.float32)
        for l in range(2):
            for n in range(4):
                h = n % 2
                out[h * 64:h * 64 + 64, l, n // 2, h * 64:h * 64 + 64] = m[l, n]
        return out.reshape(P, -1)

    def half(m, h):
        out = np.zeros((P, GW), np.float32)
        out[h * 64:h * 64 + 64] = m
        return out

    def rows(m):
        return m.reshape(DC, P, -1).transpose(1, 0, 2).reshape(P, -1)

    bf = np.zeros((P, 1), np.float32)
    bf[:NH, 0] = w["fox_bf_1"]
    gains = np.concatenate([w["norm_mix_0"], w["norm_ffn_0"], w["norm_mix_1"], w["norm_ffn_1"],
                            w["final_norm"], w["norm_gain_2"].reshape(-1), w["final_gain_2"]])
    small = dict(
        gains=feature_major(gains), mu=feature_major(w["shift_mu_0"]), w0=feature_major(w["rw_w0_0"]),
        a0=feature_major(w["rw_a0_0"]), kkp=feature_major(w["rw_kk_0"]), kap=feature_major(w["rw_ka_0"]),
        rkp=feature_major(w["rw_rk_0"]), lnxg=feature_major(w["rw_lnx_g_0"]), lnxb=feature_major(w["rw_lnx_b_0"]),
        qnorm=feature_major(w["mla_qnorm_0"]), kvnorm=feature_major(w["mla_kvnorm_0"]),
        w2z=half(w["rw_w2_0"], 0), a2z=half(w["rw_a2_0"], 1), g2=w["rw_g2_0"], wuq=uq(), wukv=ukv(),
        foxbf=bf, wf=rows(w_in1[:, 3 * GW:3 * GW + NH]), router=rows(w["router_1"]),
        convw=w["conv_w_2"].reshape(2, 4, 2, P).transpose(3, 0, 2, 1).reshape(P, -1),
        convb=feature_major(w["conv_b_2"]), gab=feature_major(w["gate_a_b_2"]), gxb=feature_major(w["gate_x_b_2"]),
        lam=feature_major(w["lru_lambda_2"]), gaw=block_diagonal(w["gate_a_w_2"]), gxw=block_diagonal(w["gate_x_w_2"]))
    params = np.concatenate([small[k] for k in PARAMS], 1)
    assert params.shape[1] == sum(PARAMS.values())

    consts = shape_constants()
    const_at, at = {}, 0
    for k, v in consts.items():
        const_at[k] = (at, v.shape[1])
        at += v.shape[1]
    arrays = {
        "x_dram": rows(w["x"][0].T), "const_dram": np.concatenate(list(consts.values()), 1),
        "param_dram": params, "w_dram": stream,
    }
    nc = bacc.Bacc("TRN2", target_bir_lowering=False, num_devices=1)
    arrays = {k: np.ascontiguousarray(v) for k, v in arrays.items()}
    args = [nc.dram_tensor(k, v.shape, F32, kind="ExternalInput").ap() for k, v in arrays.items()]
    out = nc.dram_tensor("out_dram", (P, DC * T), F32, kind="ExternalOutput").ap()
    program(nc, *args, out, const_at)
    r = run_bass_kernel_spmd(nc, [arrays], core_ids=[0])
    y = r.results[0]["out_dram"]
    return np.ascontiguousarray(y.reshape(P, DC, T).transpose(2, 1, 0).reshape(1, T, D))
```

```python
from contextlib import ExitStack

import numpy as np
import concourse.bass as bass
from concourse import mybir

F32 = mybir.dt.float32
BF16 = mybir.dt.bfloat16
I32 = mybir.dt.int32
ALU = mybir.AluOpType
ACT = mybir.ActivationFunctionType
AX_X = mybir.AxisListType.X

P = 128
T = 256
TT = T // P
D = 1024
DC = D // P
HD = 64
NH = 8
GW = NH * HD
GC = GW // P
E = 8
RING = 6
SLOT = 2048
SLOT_COLS = SLOT // DC

N_IN0, N_OUT, N_FFN, N_IN1 = 9, 4, 33, 12
FFN_STEPS = 11
MOE_STEPS = 14
MOE_SLOTS = 3 * MOE_STEPS
N_EARLY = N_IN0 + N_OUT + N_FFN + N_IN1 + N_OUT
N_MOE = E * MOE_SLOTS
N_IN2 = 14
N_LATE = 2 * (N_IN2 + N_OUT)
W_MOE = N_EARLY
W_LATE = N_EARLY + N_MOE
EPS = 1e-6
GN_EPS = 64e-5
NEG = -1e30
LAG = 3
NL = LAG + 2
LEVELS = (2, 4, 8, 16, 32, 64)



def rope_table(n_rot, theta, period, first=0):
    half = n_rot // 2
    inv = np.float32(theta) ** (-np.arange(0, n_rot, 2, dtype=np.float32) / np.float32(n_rot))
    ang = np.arange(T, dtype=np.float32)[None, :] * inv[:, None].astype(np.float32)
    cos, sin = np.ones((P, T), np.float32), np.zeros((P, T), np.float32)
    for f in range(P):
        if 0 <= f % period - first < n_rot:
            row = (f % period - first) % half
            cos[f], sin[f] = np.cos(ang[row]), np.sin(ang[row])
    return cos, sin


def rope_partner(n_rot, period, first=0):
    perm, half = np.zeros((P, P), np.float32), n_rot // 2
    for o in range(P):
        r = o % period - first
        if 0 <= r < half:
            perm[o + half, o] = -1.0
        elif half <= r < n_rot:
            perm[o - half, o] = 1.0
    return perm


def shape_constants():
    i, j = np.arange(P)[:, None], np.arange(P)[None, :]
    c = {}
    c["ident"] = (i == j)
    c["ones"] = np.ones((P, P))
    c["same_head"] = (i // HD == j // HD)
    strict, incl = (i < j), (i <= j)
    c["mask4"] = np.concatenate([strict, incl, strict, incl], 1)
    c["level1"] = (i == j + 1) & (i % 2 == 1)
    for m in (1,) + LEVELS:
        c[f"levelT{m}"] = (i // (2 * m) == j // (2 * m)) & (i // m < j // m)
    t, s = np.arange(T)[:, None], np.arange(T)[None, :]
    causal = np.where(s <= t, 0.0, NEG)
    gap = t - s
    count = ((gap >= 0) & (gap <= 128)) * 1.0 + ((gap >= 0) & (gap % 4 == 0)) + ((gap >= 0) & (gap % 16 == 0))
    dil = np.where(count > 0, np.log(np.maximum(count, 1)), NEG)
    for name, m in (("causal", causal), ("dilated", dil)):
        c[name] = np.concatenate([m[:P, :P], m[P:, :]], 1)
    stick = np.concatenate([strict, np.ones((P, P)), strict], 1)
    c["stick01"] = stick
    c["stick_add"] = np.where(stick > 0, 0.0, NEG)
    c["neg_tail"] = -1.0 * (i >= j)
    c["neg_ones"] = -np.ones((P, P))
    c["slot_iota"] = np.broadcast_to(np.arange(P), (P, P))
    lower = (np.arange(E)[None, :] < np.arange(E)[:, None]) * 1.0
    c["lower"] = np.broadcast_to(lower.reshape(1, E * E), (P, E * E))
    c["pick8"] = 8.0 * (np.arange(P)[:, None] == np.arange(NH)[None, :])
    for name, rot, theta, period, first in (("mla", 32, 1e4, 128, 64), ("full", 64, 1e4, 64, 0), ("part", 16, 5e5, 64, 0)):
        c[f"cos_{name}"], c[f"sin_{name}"] = rope_table(rot, theta, period, first)
        c[f"partner_{name}"] = rope_partner(rot, period, first)
    return {k: np.asarray(v, np.float32) for k, v in c.items()}


PARAMS = dict(
    gains=8 * DC, mu=14, w0=GC, a0=GC, kkp=GC, kap=GC, rkp=GC, lnxg=GC, lnxb=GC,
    qnorm=2, kvnorm=1, wa2=GW, g2=GW, wuq=2 * NH * P, wukv=NH * P + GW,
    foxbf=1, wf=DC * NH, router=DC * E, convw=2 * 2 * 4, convb=4, gab=4, gxb=4, lam=4,
    gaw=2 * 2 * P, gxw=2 * 2 * P)


def program(nc, x_dram, const_dram, param_dram, w_dram, out_dram, const_at):
    ctx = ExitStack()
    with ctx:
        def sb(name, cols, dt=F32):
            return ctx.enter_context(nc.sbuf_tensor(name, [P, cols], dt))

        def sem(name):
            return ctx.enter_context(nc.semaphore(name))

        ring = sb("weight_ring", RING * SLOT)
        hT_ = sb("hT", DC * T)
        uT_ = sb("uT", DC * T)
        yc_ = sb("ycat", DC * T)
        sq_ = sb("squares", DC * T)
        cst = sb("constants", const_dram.shape[1])
        par = sb("parameters", param_dram.shape[1])
        ARENA = 20480
        arena = sb("arena", ARENA)
        tiny = sb("tiny", 192)
        zero16 = sb("zero16", P, BF16)
        hT = hT_[:, :].rearrange("p (c t) -> p c t", c=DC)
        uT = uT_[:, :].rearrange("p (c t) -> p c t", c=DC)
        ycat = yc_[:, :].rearrange("p (c t) -> p c t", c=DC)
        sq = sq_[:, :].rearrange("p (c t) -> p c t", c=DC)

        def C(name):
            a, n = const_at[name]
            return cst[:, a:a + n]

        par_at, at = {}, 0
        for k, n in PARAMS.items():
            par_at[k] = (at, n)
            at += n

        def Pm(name):
            a, n = par_at[name]
            return par[:, a:a + n]

        def col(name, i):
            a, _ = par_at[name]
            return par[:, a + i:a + i + 1]

        class Arena:
            def __init__(self, start=0):
                self.at = start

            def take(self, n):
                a = self.at
                self.at += n
                assert self.at <= ARENA, self.at
                return arena[:, a:a + n]

        def chunks(ap, c):
            return ap.rearrange("p (c t) -> p c t", c=c)

        banks = [ctx.enter_context(nc.psum_tensor(f"bank{i}", [P, 512], F32)) for i in range(8)]

        loaded = sem("inputs_loaded")
        stored = sem("output_stored")
        landed = [sem(f"weights_landed{i}") for i in range(RING)]
        late_landed = [sem(f"late_weights_landed{i}") for i in range(RING)]
        used = sem("weights_used")
        late_used = sem("late_weights_used")
        flag_ready = sem("expert_passes_known")
        names = ("squares_ready", "std_ready", "u_ready", "h_ready", "y_ready",
                 "zero_ready",
                 "lora_in", "kk_in", "decay_in", "exp_in", "exp_out", "keys_ready", "bonus_in",
                 "masked", "level_ct", "inv_update", "solve_x", "solve_u", "state_ready", "tok_ready",
                 "gn_in", "gn_sq", "gn_std", "gn_var", "kk_sq", "kk_std", "lru_arg",
                 "mla_sq", "mla_std", "mla_q", "mla_kv", "rope_in", "rope_done",
                 "nmax_ready", "exp_done", "rz_ready", "prob_ready",
                 "fox_z", "fox_e", "fox_d", "stick_z", "stick_l", "stick_n", "stick_arg", "stick_w",
                 "conv_done", "lru_gates", "lru_a", "lru_t", "lru_q", "lru_s", "lam_in", "lam_e", "lam_c",
                 "gate_raw", "gate_done",
                 "router_l", "router_e", "router_sel", "tok_major", "onehot", "onehot_g",
                 "moe_tab", "moe_gu", "moe_sig", "moe_hid", "moe_down", "moe_x", "moe_y", "moe_ytok",
                 "moe_gt", "moe_gtt", "moe_g", "moe_sc", "moe_add", "moe_end",
                 "ffn_mid", "moe_mid", "moe_act", "moe_vec", "ffn_gu", "ffn_sig", "ffn_hid", "ffn_down", "out_ready")
        S = {n: sem(n) for n in names}

        class Channel:
            def __init__(self, which, filled, freed):
                self.which, self.filled, self.freed, self.np, self.nc = which, filled, freed, 0, 0

            def claim(self, pe):
                n = self.np
                if n >= len(self.which):
                    pe.wait_ge(self.freed, n - len(self.which) + 1)
                return banks[self.which[n % len(self.which)]]

            def fill(self, ins):
                ins.then_inc(self.filled, 1)
                self.np += 1
                return self.np

            def take(self, eng):
                eng.wait_ge(self.filled, self.nc + 1)
                return banks[self.which[self.nc % len(self.which)]]

            def free(self, ins):
                ins.then_inc(self.freed, 1)
                self.nc += 1
                return self.nc

        A = Channel((0, 1, 6, 7), sem("psum_for_scalar"), sem("scalar_read_psum"))
        V = Channel((2, 3, 4, 5), sem("psum_for_vector"), sem("vector_read_psum"))

        class Step:
            def __init__(self, eng, chain):
                self.eng, self.chain, self.n, self.said = eng, chain, 0, {}

            def own(self, ins):
                self.n += 1
                ins.then_inc(self.chain, 1)
                self.eng.wait_ge(self.chain, self.n)

            def lone(self, ins):
                self.n += 1
                ins.then_inc(self.chain, 1)

            def settle(self):
                self.eng.wait_ge(self.chain, self.n)

            def say(self, ins, name):
                self.said[name] = self.said.get(name, 0) + 1
                ins.then_inc(S[name], 1)

            def wait_said(self, name):
                self.eng.wait_ge(S[name], self.said[name])

        ar = Arena()
        raw = chunks(ar.take(14 * T), 14)
        qlat = chunks(ar.take(2 * T), 2)
        kvl = ar.take(T)
        kpe = ar.take(T)
        ATT = ar.at
        qh = chunks(ar.take(NH * T), NH)
        kh = chunks(ar.take(NH * T), NH)
        vml = ar.take(TT * GW).rearrange("p (a n) -> p a n", a=TT)
        qn = chunks(ar.take(2 * T), 2)
        kvn = ar.take(T)
        rt1 = ar.take(2 * T)
        rt2 = ar.take(2 * T)
        std_m = ar.take(T)
        att = Arena(ARENA - (NL + 4) * 384)
        Lg = [att.take(384) for _ in range(NL)]
        PTs = [att.take(384) for _ in range(4)]
        assert ar.at <= ARENA - (NL + 4) * 384

        aw = Arena(14 * T)
        rw = chunks(aw.take(14 * T), 14)
        lw = aw.take(T)
        sg = aw.take(T)
        logd = chunks(aw.take(GC * T), GC)
        iclr = chunks(aw.take(GC * T), GC)
        g_ = chunks(aw.take(GC * T), GC)
        cs = chunks(aw.take(GC * T), GC)
        csx = chunks(aw.take(GC * T), GC)
        lx = csx[:, 0, :]
        KR = aw.take(2 * GC * T).rearrange("p (c a k t) -> p c a k t", c=GC, a=TT, k=2)
        Bs = chunks(aw.take(GC * T), GC)
        Ks = chunks(aw.take(GC * T), GC)
        vtok = aw.take(TT * GW).rearrange("p (a n) -> p a n", a=TT)
        Btok = aw.take(GW)
        Ktok = aw.take(GW)
        Sbd = aw.take(GW).rearrange("p (c n) -> p c n", c=GC)
        Xn = aw.take(GW)
        Ut = aw.take(GW)
        yT = ycat[:, 0:GC, :]
        k2 = chunks(sq_[:, 0:GC * T], GC)
        bon = chunks(sq_[:, GC * T:2 * GC * T], GC)
        AT_A = arena[:, 0:14 * T]
        E1 = chunks(AT_A[:, 0:GC * T], GC)
        E2 = chunks(AT_A[:, GC * T:2 * GC * T], GC)
        E3 = chunks(AT_A[:, 2 * GC * T:3 * GC * T], GC)
        kk = chunks(uT_[:, 0:GC * T], GC)
        kkr = chunks(uT_[:, GC * T:2 * GC * T], GC)
        AT0 = arena[:, 14 * T:14 * T + NH * 512]
        AT = AT0.rearrange("p (h q s) -> p h q s", h=NH, q=4)
        Dm = chunks(AT_A[:, 0:NH * P], NH)
        DmT = chunks(AT_A[:, NH * P:2 * NH * P], NH)
        Gm = chunks(AT_A[:, 2 * NH * P:3 * NH * P], NH)
        CTm = [chunks(uT_[:, i * NH * P:(i + 1) * NH * P], NH) for i in range(2)]
        omka = tiny[:, 0:GC]
        fend = tiny[:, 8:8 + GC]

        a1 = Arena()
        fq2 = a1.take(2 * GC * T).rearrange("p (q c t) -> p q c t", q=2, c=GC)
        fk = chunks(a1.take(GC * T), GC)
        fv = a1.take(TT * GW).rearrange("p (a n) -> p a n", a=TT)
        mq = chunks(a1.take(GC * T), GC)
        mq2 = a1.take(2 * GC * T).rearrange("p (q c t) -> p q c t", q=2, c=GC)
        mk = chunks(a1.take(GC * T), GC)
        mv = a1.take(TT * GW).rearrange("p (a n) -> p a n", a=TT)
        fz, fe, fl, fd, fnd = [a1.take(T) for _ in range(5)]
        r1a, r1b = a1.take(2 * T), a1.take(2 * T)
        am = Arena()
        ttok = am.take(TT * D).rearrange("p (a n) -> p a n", a=TT)
        lg = am.take(TT * E)
        big = am.take(TT * E * E)
        big2 = am.take(TT * E * E)
        rank, selm, ex, comb, posm = [am.take(TT * E) for _ in range(5)]
        cnt = am.take(E)
        table = am.take(2 * E * 4).rearrange("p (e k) -> p e k", e=2 * E)
        cur = am.take(4)
        m0, den = am.take(TT), am.take(TT)
        mcnt = am.take(2)
        oh = am.take(TT * P).rearrange("p (a s) -> p a s", a=TT)
        ohg = am.take(TT * P).rearrange("p (a s) -> p a s", a=TT)
        ohgT = am.take(T)
        xg = am.take(DC * P).rearrange("p (c s) -> p c s", c=DC)
        ysl = am.take(D)
        sigb = [am.take(2 * T) for _ in range(2)]
        gtmp = [am.take(2 * T) for _ in range(2)]
        hid = [am.take(2 * T) for _ in range(2)]
        ah = Arena()
        hq = chunks(ah.take(GC * T), GC)
        hk = chunks(ah.take(GC * T), GC)
        hv = ah.take(TT * GW).rearrange("p (a n) -> p a n", a=TT)
        hq2_ = ah.take(2 * GC * T)
        hq2 = hq2_.rearrange("p (q c t) -> p q c t", q=2, c=GC)
        gsig = chunks(hq2_, DC)
        gate = chunks(ah.take(DC * T), DC)
        bx = chunks(ah.take(2 * T), 2)
        xc = chunks(ah.take(2 * T), 2)
        lr, li, la, lt, lq, lu = [chunks(ah.take(2 * T), 2) for _ in range(6)]
        cq2_ = ah.take(2 * 2 * T)
        cq2 = cq2_.rearrange("p (q c t) -> p q c t", q=2, c=2)
        ck = chunks(ah.take(2 * T), 2)
        cv = ah.take(TT * T).rearrange("p (a n) -> p a n", a=TT)
        hra, hrb = ah.take(2 * T), ah.take(2 * T)
        az = Arena()
        zb, zl, zw = [az.take(4 * 384).rearrange("p (h n) -> p h n", h=4) for _ in range(3)]
        assert max(ah.at, a1.at) <= ARENA - (NL + 4) * 384
        lam_t = tiny[:, 16:80]
        nmx = tiny[:, 80:96].rearrange("p (n k) -> p n k", k=2)
        zsum = tiny[:, 96:112].rearrange("p (n k) -> p n k", k=2)
        rz = tiny[:, 112:128].rearrange("p (n k) -> p n k", k=2)
        passes_i = ctx.enter_context(nc.sbuf_tensor("passes_i", [P, 1], I32))

        done = {}

        def slot(i):
            return ring[:, (i % RING) * SLOT:(i % RING + 1) * SLOT]

        block = ctx.enter_context(nc.Block())

        @block.sync
        def _(sp):
            sp.dma_start(hT_[:, :], x_dram).then_inc(loaded, 16)
            sp.dma_start(cst[:, :], const_dram).then_inc(loaded, 16)
            sp.dma_start(par[:, :], param_dram).then_inc(loaded, 16)

            for k in range(RING):
                sp.dma_start(slot(k), w_dram[k]).then_inc(landed[k], 16)
            with sp.Fori(1, N_EARLY // RING) as turn:
                for k in range(RING):
                    sp.wait_ge(used, turn * RING + (k + 1 - RING))
                    sp.dma_start(slot(k), w_dram[bass.ds(turn * RING + k, 1)].rearrange("o p n -> (o p) n"))\
                      .then_inc(landed[k], 16)
            for n in range(N_EARLY // RING * RING, N_EARLY):
                sp.wait_ge(used, n + 1 - RING)
                sp.dma_start(slot(n), w_dram[n]).then_inc(landed[n % RING], 16)
            sp.wait_ge(flag_ready, 1)
            passes = sp.value_load(passes_i[0:1, 0:1], min_val=1, max_val=2)
            with sp.Fori(0, passes) as ps:
                with sp.Fori(0, N_MOE // RING) as turn:
                    for k in range(RING):
                        n = N_EARLY + k
                        sp.wait_ge(used, ps * N_MOE + turn * RING + (n + 1 - RING))
                        sp.dma_start(slot(n), w_dram[bass.ds(turn * RING + n, 1)].rearrange("o p n -> (o p) n"))\
                          .then_inc(landed[n % RING], 16)
            sp.wait_ge(S["moe_end"], 1)
            for n in range(N_LATE):
                if n >= RING:
                    sp.wait_ge(late_used, n + 1 - RING)
                sp.dma_start(slot(n), w_dram[W_LATE + n]).then_inc(late_landed[n % RING], 16)
            sp.wait_ge(S["out_ready"], 1)
            sp.dma_start(out_dram, uT_[:, :]).then_inc(stored, 16)
            sp.wait_ge(stored, 16)

        @block.tensor
        def _(pe):
            wn = [0, 0]
            job = {}

            def next_slot(late):
                n = wn[late]
                pe.wait_ge((late_landed if late else landed)[n % RING], 16 * (n // RING + 1))
                return slot(n)

            owed = []

            def mm(out, lhsT, rhs, start=True, stop=True, tells=False):
                ins = pe.matmul(out, lhsT, rhs, start=start, stop=stop, skip_group_check=True)
                if owed and not tells:
                    ins.then_inc(owed.pop(), 1)
                return ins

            def tr(out, in_):
                return pe.transpose(out, in_, C("ident"))

            def project(ch, rhs, late=0):
                w = next_slot(late).rearrange("p (c n) -> p c n", c=DC)
                bank = ch.claim(pe)[:, :].rearrange("p (j t) -> p j t", j=2)
                for j in range(2):
                    for c in range(DC):
                        last = mm(bank[:, j, :], w[:, c, j * P:(j + 1) * P], rhs[:, c, :], start=(c == 0), stop=(c == DC - 1))
                ch.fill(last)
                free_slot(late)
                return ch.np

            def free_slot(late):
                owed.append(late_used if late else used)
                wn[late] += 1

            def project_tok(ch, lhs, late=0):
                w = next_slot(late).rearrange("p (c n) -> p c n", c=DC)
                bank = ch.claim(pe)[:, :].rearrange("p (a n) -> p a n", a=TT)
                for a in range(TT):
                    for c in range(DC):
                        last = mm(bank[:, a, :], lhs[:, c, a * P:(a + 1) * P], w[:, c, :], start=(c == 0), stop=(c == DC - 1))
                ch.fill(last)
                free_slot(late)

            def norm(k):
                bank = A.claim(pe)
                for c in range(DC):
                    if c % 4 == 0:
                        pe.wait_ge(S["squares_ready"], 2 * k + c // 4 + 1)
                    last = mm(bank[:, 0:T], C("ones"), sq[:, c, :], start=(c == 0), stop=(c == DC - 1))
                A.fill(last)

            def attention(scores, v, n0):
                prob = {}
                for i in range(NH + LAG + 2):
                    if i < NH:
                        bank = V.claim(pe)
                        V.fill(scores(i, bank))
                    h = i - LAG
                    if 0 <= h < NH:
                        pe.wait_ge(S["prob_ready"], n0 + h + 1)
                        bank = A.claim(pe)
                        for lo in (0, P, 2 * P):
                            last = tr(bank[:, lo:lo + P], Lg[h % NL][:, lo:lo + P])
                        prob[h] = A.fill(last)
                    if h >= 2 and h % 2 == 0:
                        bank = V.claim(pe)
                        pe.wait_ge(A.freed, prob[h - 1])
                        for g in (h - 2, h - 1):
                            o = bank[HD * (g % 2):HD * (g % 2) + HD, :]
                            mm(o[:, 0:T], v[:, 0, g * HD:(g + 1) * HD], PTs[g % 4][:, 0:T], stop=False)
                            last = mm(o[:, P:T], v[:, 1, g * HD:(g + 1) * HD], PTs[g % 4][:, T:T + P], start=False)
                        V.fill(last)

            def head_scores(q2, k):
                def go(h, bank):
                    q = q2[:, h % 2, h // 2, :]
                    mm(bank[:, 0:P], q[:, 0:P], k[:, h // 2, 0:P])
                    return mm(bank[:, P:P + T], q[:, P:T], k[:, h // 2, :], tells=True)
                return go

            def rope(x, n, which):
                for c in range(0, n, 2):
                    bank = V.claim(pe)
                    V.fill(mm(bank[:, :], C(f"partner_{which}"), x[:, c:c + 2, :], tells=True))

            pe.wait_ge(loaded, 48)
            norm(0)
            pe.wait_ge(S["u_ready"], 1)
            for _ in range(N_IN0):
                project(A, uT)

            bank = A.claim(pe)
            pe.wait_ge(S["mla_sq"], 1)
            for c in range(2):
                mm(bank[:, 0:T], C("ones"), sq[:, c, :], start=(c == 0), stop=(c == 1))
            A.fill(mm(bank[:, T:2 * T], C("ones"), sq[:, 2, :], tells=True))
            pe.wait_ge(S["mla_q"], 1)
            wuq = Pm("wuq").rearrange("p (k n) -> p k n", k=2)
            for j2 in range(NH // 2):
                bank = A.claim(pe)
                for j in range(2):
                    for c in range(2):
                        cc = (2 * j2 + j) * P
                        last = mm(bank[:, j * T:(j + 1) * T], wuq[:, c, cc:cc + P], qn[:, c, :], start=(c == 0), stop=(c == 1))
                A.fill(last)
            wukv = Pm("wukv")
            pe.wait_ge(S["mla_kv"], 1)
            for a in range(TT):
                bank = A.claim(pe)
                A.fill(mm(bank[:, :], kvn[:, a * P:(a + 1) * P], wukv[:, NH * P:NH * P + GW], tells=True))
            bank = V.claim(pe)
            V.fill(mm(bank[:, 0:T], C("partner_mla"), kpe, tells=True))
            for j2 in range(NH // 2):
                bank = V.claim(pe)
                for j in range(2):
                    cc = (2 * j2 + j) * P
                    last = mm(bank[:, j * T:(j + 1) * T], wukv[:, cc:cc + P], kvn)
                V.fill(last)
            pe.wait_ge(A.freed, A.np)
            rope(qh, NH, "mla")
            pe.wait_ge(S["rope_done"], 1 + NH // 2)

            def mla_scores(h, bank):
                mm(bank[:, 0:P], qh[:, h, 0:P], kh[:, h, 0:P])
                return mm(bank[:, P:P + T], qh[:, h, P:T], kh[:, h, :])

            attention(mla_scores, vml, 0)

            pe.wait_ge(S["lora_in"], 2)
            for w, x in ((Pm("wa2"), lw), (Pm("wa2"), lx), (Pm("g2"), sg)):
                for j2 in range(2):
                    bank = A.claim(pe)
                    for j in range(2):
                        cc = (2 * j2 + j) * P
                        last = mm(bank[:, j * T:(j + 1) * T], w[:, cc:cc + P], x)
                    A.fill(last)
            pe.wait_ge(S["kk_sq"], 1)
            for j2 in range(2):
                bank = A.claim(pe)
                A.fill(mm(bank[:, 0:512], C("same_head"), sq_[:, j2 * 512:(j2 + 1) * 512], tells=True))
            pe.wait_ge(S["bonus_in"], 1)
            for j2 in range(2):
                bank = V.claim(pe)
                V.fill(mm(bank[:, 0:512], C("same_head"), sq_[:, 1024 + j2 * 512:1024 + (j2 + 1) * 512], tells=True))
            for a in range(TT):
                bank = A.claim(pe)
                for c in range(GC):
                    last = tr(bank[:, c * P:(c + 1) * P], rw[:, 8 + c, a * P:(a + 1) * P])
                A.fill(last)
            pe.wait_ge(S["keys_ready"], 1)
            for src in (Bs, Ks):
                bank = A.claim(pe)
                for c in range(GC):
                    last = tr(bank[:, c * P:(c + 1) * P], src[:, c, 0:P])
                A.fill(last)

            for a in range(TT):
                lo, hi = a * P, (a + 1) * P
                for h in range(NH):
                    c, b = h // 2, HD * (h % 2)
                    bank = V.claim(pe)
                    kr = KR[b:b + HD, c, a].rearrange("p k t -> p (k t)")
                    mm(bank[:, 0:T], Bs[b:b + HD, c, lo:hi], kr)
                    V.fill(mm(bank[:, T:2 * T], Ks[b:b + HD, c, lo:hi], kr, tells=True))
                for par_ in range(2):
                    bank = V.claim(pe)
                    for h in range(par_, NH, 2):
                        c, b = h // 2, HD * par_
                        last = mm(bank[:, c * P:(c + 1) * P], KR[b:b + HD, c, a, 0, :], Bs[b:b + HD, c, lo:hi])
                    V.fill(last)
                dj = [V.np, V.np]
                for n, m in enumerate(LEVELS):
                    pe.wait_ge(S["level_ct"], a * len(LEVELS) + n + 1)
                    gj = []
                    for h4 in range(2):
                        pe.wait_ge(V.freed, dj[h4])
                        bank = A.claim(pe)
                        for h in range(4 * h4, 4 * h4 + 4):
                            last = mm(bank[:, (h % 4) * P:(h % 4 + 1) * P], CTm[n % 2][:, h, :], Dm[:, h, :])
                        gj.append(A.fill(last))
                    for h4 in range(2):
                        pe.wait_ge(A.freed, gj[h4])
                        if m != LEVELS[-1]:
                            bank = V.claim(pe)
                            for h in range(4 * h4, 4 * h4 + 4):
                                last = mm(bank[:, (h % 4) * P:(h % 4 + 1) * P], DmT[:, h, :], Gm[:, h, :])
                            V.fill(last)
                        bank = V.claim(pe)
                        for h in range(4 * h4, 4 * h4 + 4):
                            last = mm(bank[:, (h % 4) * P:(h % 4 + 1) * P], Gm[:, h, :], DmT[:, h, :])
                        dj[h4] = V.fill(last)
                bank = A.claim(pe)
                for c in range(GC):
                    if a:
                        mm(bank[:, c * P:(c + 1) * P], KR[:, c, a, 0, :], Sbd[:, c, :], stop=False)
                    for h in (2 * c, 2 * c + 1):
                        last = mm(bank[:, h * HD:(h + 1) * HD], AT[:, h, 2, :], vtok[:, a, h * HD:(h + 1) * HD],
                                  start=not a)
                nx = A.fill(last)
                pe.wait_ge(A.freed, nx)
                pe.wait_ge(V.freed, V.np)
                bank = A.claim(pe)
                for h in range(NH):
                    last = mm(bank[:, h * HD:(h + 1) * HD], DmT[:, h, :], Xn[:, h * HD:(h + 1) * HD])
                nu = A.fill(last)
                pe.wait_ge(A.freed, nu)
                bank = A.claim(pe)
                for c in range(GC):
                    if a:
                        mm(bank[:, c * P:(c + 1) * P], Sbd[:, c, :], KR[:, c, a, 1, :], stop=False)
                    for h in (2 * c, 2 * c + 1):
                        o = bank[HD * (h % 2):HD * (h % 2) + HD, c * P:(c + 1) * P]
                        mm(o, Ut[:, h * HD:(h + 1) * HD], AT[:, h, 1, :], start=not a, stop=False)
                        last = mm(o, vtok[:, a, h * HD:(h + 1) * HD], AT[:, h, 3, :], start=False)
                A.fill(last)
                if a == 0:
                    bank = V.claim(pe)
                    for c in range(GC):
                        mm(bank[:, c * P:(c + 1) * P], Btok[:, c * P:(c + 1) * P], Ut[:, c * P:(c + 1) * P], stop=False)
                        last = mm(bank[:, c * P:(c + 1) * P], Ktok[:, c * P:(c + 1) * P], vtok[:, 0, c * P:(c + 1) * P], start=False)
                    V.fill(last)
                    pe.wait_ge(S["state_ready"], 1)
            pe.wait_ge(A.freed, A.np)
            for j2 in range(2):
                bank = V.claim(pe)
                V.fill(mm(bank[:, :], C("same_head"), yT[:, 2 * j2:2 * j2 + 2, :], tells=True))
            pe.wait_ge(S["gn_sq"], 1)
            for j2 in range(2):
                bank = A.claim(pe)
                A.fill(mm(bank[:, :], C("same_head"), sq_[:, j2 * 512:(j2 + 1) * 512], tells=True))

            def out_projection(k, late=0):
                pe.wait_ge(S["y_ready"], k + 1)
                for _ in range(N_OUT):
                    project(V, ycat, late)

            out_projection(0)

            norm(1)
            pe.wait_ge(S["u_ready"], 2)
            pe.wait_ge(A.freed, A.np)
            pe.wait_ge(V.freed, V.np)
            pe.wait_ge(S["zero_ready"], 1)
            for b in range(4, 8):
                mm(banks[b][:, :], zero16[:, :], zero16[:, 0:1].broadcast_to([P, 512]), stop=False)

            w0 = wn[0]

            def ffn_gu(k, turn, step, first):
                for g in range(2):
                    n = k + g
                    pe.wait_ge(landed[n % RING], turn * 16 + 16 * (n // RING + 1))
                    w = slot(n).rearrange("p (c n) -> p c n", c=DC)
                    bank = banks[2 * g + step % 2]
                    for j in range(2):
                        for c in range(DC):
                            last = mm(bank[:, j * T:(j + 1) * T], w[:, c, j * P:(j + 1) * P], uT[:, c, :],
                                      start=(c == 0), stop=(c == DC - 1))
                    if g == 0:
                        owed.append(used)
                last.then_inc(S["ffn_gu"], 1)
                owed.append(used)

            def ffn_down(k, turn, step):
                pe.wait_ge(landed[k % RING], turn * 16 + 16 * (k // RING + 1))
                w = slot(k).rearrange("p (f n) -> p f n", f=2)
                hm = chunks(hid[step % 2], 2)
                for f in range(2):
                    for c in range(DC):
                        last = mm(banks[4 + c // 2][:, (c % 2) * T:(c % 2 + 1) * T], w[:, f, c * P:(c + 1) * P],
                                  hm[:, f, :], start=False, stop=False)
                last.then_inc(S["ffn_down"], 1)
                owed.append(used)

            ffn_gu(w0, 0, 0, True)
            with pe.Fori(0, (FFN_STEPS - 1) // 2) as it:
                for s in range(2):
                    k = w0 + 2 + 3 * s
                    ffn_gu(k, it, 1 + s, False)
                    pe.wait_ge(S["ffn_hid"], it * 2 + (s + 1))
                    ffn_down(k + 2, it, s)
            wn[0] += N_FFN
            pe.wait_ge(S["ffn_hid"], FFN_STEPS)
            ffn_down(wn[0] - 1, 0, 0)

            norm(2)
            pe.wait_ge(S["u_ready"], 3)
            bank = V.claim(pe)
            wf = Pm("wf").rearrange("p (c n) -> p c n", c=DC)
            for c in range(DC):
                last = mm(bank[0:NH, 0:T], wf[:, c, :], uT[:, c, :], start=(c == 0), stop=(c == DC - 1))
            V.fill(last)
            for which in "qkvQKV":
                for _ in range(2):
                    if which in "vV":
                        project_tok(A, uT)
                    else:
                        project(A, uT)
            pe.wait_ge(A.freed, A.np)
            rope(mq, GC, "full")
            rope(mk, GC, "full")
            pe.wait_ge(S["fox_d"], 1)
            pick = C("pick8")

            def fox_scores(h, bank):
                q = fq2[:, h % 2, h // 2, :]
                for lo, q0, nk in ((0, 0, P), (P, P, T)):
                    o = bank[:, lo:lo + nk]
                    mm(o, q[:, q0:q0 + P], fk[:, h // 2, 0:nk], stop=False)
                    last = mm(o, pick[:, h:h + 1].broadcast_to([P, P]), fnd[:, 0:nk], start=False)
                return last

            attention(fox_scores, fv, NH)
            pe.wait_ge(S["rope_done"], 1 + NH // 2 + GC)
            attention(head_scores(mq2, mk), mv, 2 * NH)
            out_projection(1)

            norm(3)
            pe.wait_ge(S["u_ready"], 4)
            bank = V.claim(pe)
            rw_ = Pm("router").rearrange("p (c n) -> p c n", c=DC)
            for a in range(TT):
                for c in range(DC):
                    last = mm(bank[:, a * E:(a + 1) * E], uT[:, c, a * P:(a + 1) * P], rw_[:, c, :],
                              start=(c == 0), stop=(c == DC - 1))
            V.fill(last)
            for a in range(TT):
                for c4 in range(2):
                    bank = A.claim(pe)
                    for c in range(4):
                        last = tr(bank[:, c * P:(c + 1) * P], uT[:, 4 * c4 + c, a * P:(a + 1) * P])
                    A.fill(last)
            pe.wait_ge(S["router_sel"], 1)
            bank = V.claim(pe)
            mm(bank[:, 0:E], C("mask4")[:, 0:P], selm[:, 0:E])
            mm(bank[:, E:2 * E], C("ones"), selm[:, 0:E], stop=False)
            mm(bank[:, E:2 * E], C("mask4")[:, 0:P], selm[:, E:2 * E], start=False)
            mm(bank[:, 2 * E:3 * E], C("ones"), selm[:, 0:E], stop=False)
            V.fill(mm(bank[:, 2 * E:3 * E], C("ones"), selm[:, E:2 * E], start=False, tells=True))
            pe.wait_ge(A.freed, A.np)
            pe.wait_ge(V.freed, V.np)
            pe.wait_ge(flag_ready, 1)
            passes = pe.value_load(passes_i[0:1, 0:1], min_val=1, max_val=2)

            def moe_gu(k, turn, step, half):
                bank = banks[half]
                for g in range(2):
                    n = k + g
                    pe.wait_ge(landed[n % RING], turn * 16 + 16 * (n // RING + 1))
                    w = slot(n).rearrange("p (c n) -> p c n", c=DC)
                    for j in range(2):
                        for c in range(DC):
                            last = mm(bank[:, (2 * g + j) * P:(2 * g + j + 1) * P], w[:, c, j * P:(j + 1) * P], xg[:, c, :],
                                      start=(c == 0), stop=(c == DC - 1))
                    if g == 0:
                        owed.append(used)
                last.then_inc(S["moe_gu"], 1)
                owed.append(used)

            def moe_down(k, turn, half):
                pe.wait_ge(landed[k % RING], turn * 16 + 16 * (k // RING + 1))
                w = slot(k).rearrange("p (f n) -> p f n", f=2)
                for f in range(2):
                    for o in range(2):
                        last = mm(banks[4 + o][:, :], hid[half][:, f * P:(f + 1) * P], w[:, f, o * 512:(o + 1) * 512],
                                  start=False, stop=False)
                last.then_inc(S["moe_down"], 1)
                owed.append(used)

            with pe.Fori(0, passes) as ps:
                with pe.Fori(0, E) as e:
                    ex_n = pe.snap(ps * E + e)
                    pe.wait_ge(S["onehot"], ex_n + 1)
                    for c4 in range(2):
                        for c in range(4):
                            for a in range(TT):
                                cc = 4 * c4 + c
                                last = mm(banks[6 + c4][:, c * P:(c + 1) * P], ttok[:, a, cc * P:(cc + 1) * P], oh[:, a, :],
                                          start=(a == 0), stop=(a == 1))
                    last.then_inc(S["moe_g"], 1)
                    for o in range(2):
                        mm(banks[4 + o][:, :], zero16[:, :], zero16[:, 0:1].broadcast_to([P, 512]), stop=False)
                    pe.wait_ge(S["moe_x"], ex_n + 1)
                    tb = ex_n * (MOE_SLOTS // RING)
                    sb_ = ex_n * MOE_STEPS
                    k0 = N_EARLY
                    moe_gu(k0, tb, 0, 0)
                    with pe.Fori(0, (MOE_STEPS - 2) // 2) as it:
                        tn = pe.snap(tb + it)
                        sn = pe.snap(sb_ + it * 2)
                        for s in range(2):
                            k = k0 + 2 + 3 * s
                            moe_gu(k, tn, 1 + s, (1 + s) % 2)
                            pe.wait_ge(S["moe_hid"], sn + (s + 1))
                            moe_down(k + 2, tn, s % 2)
                    k = k0 + 2 + 3 * (MOE_STEPS - 2)
                    moe_gu(k, tb, 13, 1)
                    pe.wait_ge(S["moe_hid"], sb_ + (MOE_STEPS - 1))
                    moe_down(k + 2, tb, 0)
                    pe.wait_ge(S["moe_hid"], sb_ + MOE_STEPS)
                    moe_down(k + 3, tb, 1)
                    pe.wait_ge(S["onehot_g"], ex_n + 1)
                    for a in range(TT):
                        last = tr(banks[6][:, a * P:(a + 1) * P], ohg[:, a, :])
                    last.then_inc(S["moe_gt"], 1)
                    pe.wait_ge(S["moe_ytok"], ex_n + 1)
                    for c2 in range(4):
                        bank = banks[(7, 2, 3, 7)[c2]]
                        if c2 == 3:
                            pe.wait_ge(S["moe_add"], ex_n * 4 + 1)
                        for c in range(2):
                            cc = 2 * c2 + c
                            last = mm(bank[:, c * T:(c + 1) * T], ysl[:, cc * P:(cc + 1) * P], ohgT)
                        last.then_inc(S["moe_sc"], 1)
                    pe.wait_ge(S["moe_add"], ex_n * 4 + 4)

            norm(4)
            for l in range(2):
                norm(5 + l)
                pe.wait_ge(S["u_ready"], 6 + l)
                for kind in ("q", "q", "k", "k", "v", "v", "g", "g", "x", "g", "q", "k", "v", "g"):
                    if kind == "v":
                        project_tok(A, uT, 1)
                    else:
                        project(A, uT, 1)
                pe.wait_ge(A.freed, A.np)
                rope(hq, GC, "part")
                rope(hk, GC, "part")
                pe.wait_ge(S["conv_done"], l + 1)
                for w in (Pm("gaw"), Pm("gxw")):
                    bank = A.claim(pe)
                    for c in range(2):
                        last = mm(bank[:, c * T:(c + 1) * T], w[:, (2 * l + c) * P:(2 * l + c + 1) * P], xc[:, c, :])
                    A.fill(last)
                pe.wait_ge(S["rope_done"], 1 + NH // 2 + GC * (2 + l))
                attention(head_scores(hq2, hk), hv, (3 + l) * NH)
                for h in range(4):
                    q, k = cq2[:, h % 2, h // 2, :], ck[:, h // 2, :]
                    bank = V.claim(pe)
                    mm(bank[:, 0:T], k[:, 0:P], q)
                    V.fill(mm(bank[:, T:T + P], k[:, P:T], q[:, P:T], tells=True))
                pe.wait_ge(S["stick_n"], l + 1)
                for h in range(4):
                    bank = V.claim(pe)
                    mm(bank[:, 0:T], C("neg_tail"), zl[:, h, 0:T], stop=False)
                    mm(bank[:, P:T], C("neg_ones"), zl[:, h, T:T + P], start=False)
                    V.fill(mm(bank[:, T:T + P], C("neg_tail"), zl[:, h, T:T + P], tells=True))
                pe.wait_ge(S["stick_w"], l + 1)
                for c in range(2):
                    bank = V.claim(pe)
                    for h in (2 * c, 2 * c + 1):
                        o = bank[HD * (h % 2):HD * (h % 2) + HD, :]
                        mm(o[:, 0:T], cv[:, 0, h * HD:(h + 1) * HD], zw[:, h, 0:T], stop=False)
                        last = mm(o[:, P:T], cv[:, 1, h * HD:(h + 1) * HD], zw[:, h, T:T + P], start=False)
                    V.fill(last)
                out_projection(2 + l, 1)
            norm(7)

        @block.scalar
        def _(act):
            st = Step(act, sem("scalar_step"))

            def a_(out, in_, f, **kw):
                return act.activation(out, in_, f, **kw)

            def evac(dst, width=512):
                bank = A.take(act)
                A.free(a_(dst, bank[:, 0:width], ACT.Copy))

            def split_heads(q2):
                bank = A.take(act)
                b3 = bank[:, :].rearrange("p (c t) -> p c t", c=2)
                st.lone(a_(q2[0:HD, 0], b3[0:HD], ACT.Copy))
                A.free(a_(q2[HD:P, 1], b3[HD:P], ACT.Copy))

            def norm(k, h_done):
                if h_done:
                    act.wait_ge(S["h_ready"], h_done)
                for c4 in range(2):
                    st.say(a_(sq[:, 4 * c4:4 * c4 + 4, :], hT[:, 4 * c4:4 * c4 + 4, :], ACT.Square), "squares_ready")
                bank = A.take(act)
                A.free(a_(rstd(), bank[:, 0:T], ACT.Sqrt, scale=1.0 / D, bias=epscol))
                done["norm", k] = A.nc

            def rstd():
                return yc_[:, 0:T]

            epscol = tiny[:, 130:131]
            gncol = tiny[:, 131:132]
            onecol = tiny[:, 132:133]
            zcol = tiny[:, 133:134]
            act.wait_ge(S["zero_ready"], 1)

            def attention(n0):
                done["attention", n0] = A.nc
                for i in range(NH + LAG):
                    if i >= LAG:
                        evac(PTs[(i - LAG) % 4], 384)
                    if i < NH:
                        n = n0 + i
                        act.wait_ge(S["nmax_ready"], n + 1)
                        st.lone(a_(Lg[i % NL][:, 0:P], Lg[i % NL][:, 0:P], ACT.Exp, bias=nmx[:, i, 0:1], accum_out=zsum[:, i, 0:1]))
                        st.say(a_(Lg[i % NL][:, P:384], Lg[i % NL][:, P:384], ACT.Exp, bias=nmx[:, i, 1:2], accum_out=zsum[:, i, 1:2]), "exp_done")

            act.wait_ge(loaded, 48)
            norm(0, 0)
            for n in range(7):
                evac(raw[:, 2 * n:2 * n + 2, :])
            evac(qlat)
            bank = A.take(act)
            st.lone(a_(kvl, bank[:, 0:T], ACT.Copy))
            A.free(a_(kpe, bank[:, T:2 * T], ACT.Copy))
            st.settle()
            act.wait_ge(A.freed, A.nc)
            st.lone(a_(sq[:, 0:2, :], qlat, ACT.Square))
            st.say(a_(sq[:, 2, :], kvl, ACT.Square), "mla_sq")
            bank = A.take(act)
            st.say(a_(std_m, bank[:, 0:T], ACT.Sqrt, scale=1.0 / 256, bias=epscol), "mla_std")
            A.free(a_(rt1[:, 0:T], bank[:, T:2 * T], ACT.Sqrt, scale=1.0 / 128, bias=epscol))
            done["mla_std"] = A.nc
            for j2 in range(NH // 2):
                evac(qh[:, 2 * j2:2 * j2 + 2, :])
            for a in range(TT):
                evac(vml[:, a, :])
            done["mla"] = A.nc
            attention(0)

            act.wait_ge(S["decay_in"], 1)
            st.say(a_(lw[0:HD], rw[0:HD, 12, :], ACT.Tanh), "lora_in")
            st.lone(a_(lx[HD:P], rw[HD:P, 12, :], ACT.Copy))
            st.settle()
            st.say(a_(sg, rw[:, 13, :], ACT.Sigmoid), "lora_in")
            for dst, bias in ((logd, "w0"), (iclr, "a0"), (g_, None)):
                for j2 in range(2):
                    bank = A.take(act)
                    for j in range(2):
                        c = 2 * j2 + j
                        if bias:
                            ins = a_(dst[:, c, :], bank[:, j * T:(j + 1) * T], ACT.Sigmoid, bias=col(bias, c))
                        else:
                            ins = a_(dst[:, c, :], bank[:, j * T:(j + 1) * T], ACT.Copy)
                        if j:
                            A.free(ins)
                        else:
                            st.lone(ins)
            st.settle()
            done["lora"] = A.nc
            act.wait_ge(S["kk_in"], 1)
            st.say(a_(sq_[:, 0:1024], kkr, ACT.Square), "kk_sq")
            for j2 in range(2):
                bank = A.take(act)
                A.free(a_(kk[:, 2 * j2:2 * j2 + 2, :], bank[:, :], ACT.Sqrt))
            done["kk"] = A.nc
            act.wait_ge(S["exp_in"], 1)
            st.lone(a_(E1, cs, ACT.Exp))
            st.lone(a_(E2, csx, ACT.Exp))
            st.lone(a_(E3, cs, ACT.Exp, scale=-1.0))
            st.settle()
            act.wait_ge(S["exp_in"], 2)
            st.say(a_(fend, tiny[:, 140:140 + GC], ACT.Exp), "exp_out")
            for a in range(TT):
                evac(vtok[:, a, :])
            evac(Btok)
            evac(Ktok)
            for a in range(TT):
                done["levels", a] = A.nc
                for m in LEVELS:
                    for h4 in range(2):
                        evac(Gm[:, 4 * h4:4 * h4 + 4, :])
                bank = A.take(act)
                A.free(a_(Xn, bank[:, :], ACT.Copy, scale=-1.0))
                evac(Ut)
                bank = A.take(act)
                A.free(a_(yT[:, :, a * P:(a + 1) * P], bank[:, :].rearrange("p (c t) -> p c t", c=GC), ACT.Copy))
                done["y", a] = A.nc
            act.wait_ge(S["gn_in"], 1)
            st.say(a_(sq_[:, 0:1024], yT, ACT.Square), "gn_sq")
            for j2 in range(2):
                bank = A.take(act)
                A.free(a_(cs[:, 2 * j2:2 * j2 + 2, :], bank[:, :], ACT.Sqrt, scale=1.0 / HD, bias=gncol))
            done["gn"] = A.nc

            norm(1, 1)
            with act.Fori(0, FFN_STEPS // 2) as it:
                for s in range(2):
                    act.wait_ge(S["ffn_gu"], it * 2 + (s + 1))
                    a_(sigb[s], banks[s][:, :], ACT.Sigmoid).then_inc(S["ffn_sig"], 1)
            act.wait_ge(S["ffn_gu"], FFN_STEPS)
            a_(sigb[0], banks[0][:, :], ACT.Sigmoid).then_inc(S["ffn_sig"], 1)

            norm(2, 2)
            for dst in (fq2, fk, fv, mq, mk, mv):
                for n in range(2):
                    if dst is fq2:
                        split_heads(fq2[:, :, 2 * n:2 * n + 2, :])
                    elif dst is fv or dst is mv:
                        bank = A.take(act)
                        A.free(a_(dst[:, :, n * T:(n + 1) * T], bank[:, :].rearrange("p (a n) -> p a n", a=TT), ACT.Copy))
                    else:
                        evac(dst[:, 2 * n:2 * n + 2, :])
            done["l1"] = A.nc
            act.wait_ge(S["fox_z"], 1)
            st.own(a_(fe[0:NH], fl[0:NH], ACT.Exp, scale=-1.0))
            st.say(a_(fe[0:NH], fe[0:NH], ACT.Ln, bias=tiny[0:NH, 132:133]), "fox_e")
            attention(NH)
            attention(2 * NH)

            norm(3, 3)
            for a in range(TT):
                for c4 in range(2):
                    evac(ttok[:, a, c4 * 512:(c4 + 1) * 512])
            act.wait_ge(S["router_l"], 1)
            st.say(a_(ex, ex, ACT.Exp), "router_e")
            act.wait_ge(flag_ready, 1)
            passes = act.value_load(passes_i[0:1, 0:1], min_val=1, max_val=2)
            with act.Fori(0, passes) as ps:
                with act.Fori(0, E) as e:
                    ex_n = act.snap(ps * E + e)
                    act.wait_ge(S["moe_g"], ex_n + 1)
                    a_(xg[:, 0:4, :], banks[6][:, :], ACT.Copy).then_inc(S["moe_act"], 1)
                    a_(xg[:, 4:8, :], banks[7][:, :], ACT.Copy).then_inc(S["moe_x"], 1)
                    with act.Fori(0, MOE_STEPS // 2) as it:
                        for s in range(2):
                            act.wait_ge(S["moe_gu"], ex_n * MOE_STEPS + it * 2 + (s + 1))
                            a_(sigb[s][:, 0:T], banks[s][:, 0:T], ACT.Sigmoid).then_inc(S["moe_sig"], 1)
                    act.wait_ge(S["moe_gt"], ex_n + 1)
                    act.wait_ge(S["moe_down"], ex_n * MOE_STEPS + MOE_STEPS)
                    a_(ohgT, banks[6][:, 0:T], ACT.Copy).then_inc(S["moe_act"], 1)
                    a_(ysl[:, 0:512], banks[4][:, :], ACT.Copy).then_inc(S["moe_act"], 1)
                    a_(ysl[:, 512:1024], banks[5][:, :], ACT.Copy).then_inc(S["moe_ytok"], 1)

            norm(4, 4)
            for l in range(2):
                norm(5 + l, 5 + l)
                for dst, n in ((hq, 0), (hq, 2), (hk, 0), (hk, 2), (hv, 0), (hv, 1), (gate, 0), (gate, 2),
                               (bx, 0), (gate, 4), (cq2, 0), (ck, 0), (cv, 0), (gate, 6)):
                    if dst is cq2:
                        split_heads(cq2)
                        continue
                    bank = A.take(act)
                    if dst is hv or dst is cv:
                        A.free(a_(dst[:, :, n * T:(n + 1) * T], bank[:, :].rearrange("p (a n) -> p a n", a=TT), ACT.Copy))
                    elif dst is gate:
                        st.lone(a_(gsig[:, n:n + 2, :], bank[:, :], ACT.Sigmoid))
                        A.free(a_(dst[:, n:n + 2, :], bank[:, :], ACT.Copy))
                    else:
                        A.free(a_(dst[:, n:n + 2, :], bank[:, :], ACT.Copy))
                st.settle()
                done["hybrid", l] = A.nc
                act.wait_ge(S["lam_in"], l + 1)
                st.say(a_(lam_t[:, 2:4], lam_t[:, 0:2], ACT.Exp, scale=-1.0), "lam_e")
                for dst, bias in ((lr, "gab"), (li, "gxb")):
                    bank = A.take(act)
                    st.lone(a_(dst[:, 0, :], bank[:, 0:T], ACT.Sigmoid, bias=col(bias, 2 * l)))
                    A.free(a_(dst[:, 1, :], bank[:, T:2 * T], ACT.Sigmoid, bias=col(bias, 2 * l + 1)))
                st.settle()
                act.wait_ge(A.freed, A.nc)
                act.wait_ge(S["lam_c"], l + 1)
                for c in range(2):
                    st.lone(a_(lt[:, c, :], lr[:, c, :], ACT.Tanh, scale=lam_t[:, 20 + c:21 + c]))
                for c in range(2):
                    ins = a_(la[:, c, :], lr[:, c, :], ACT.Exp, scale=lam_t[:, 20 + c:21 + c])
                    if c:
                        st.say(ins, "lru_a")
                    else:
                        st.lone(ins)
                act.wait_ge(S["lru_q"], l + 1)
                st.say(a_(lq, lq, ACT.Sqrt), "lru_s")
                attention((3 + l) * NH)
                act.wait_ge(S["stick_z"], l + 1)
                st.own(a_(zl, zb, ACT.Abs))
                st.own(a_(zl, zl, ACT.Exp, scale=-1.0))
                st.say(a_(zl, zl, ACT.Ln, bias=onecol), "stick_l")
                act.wait_ge(S["stick_arg"], l + 1)
                st.say(a_(zw, zw, ACT.Exp), "stick_w")
            norm(7, 7)

        @block.vector
        def _(dve):
            st = Step(dve, sem("vector_step"))
            tt, ts, stt, cp = dve.tensor_tensor, dve.tensor_scalar, dve.scalar_tensor_tensor, dve.tensor_copy
            rstd = yc_[:, 0:T]

            st.lone(dve.memset(tiny[:, 130:131], EPS))
            st.lone(dve.memset(tiny[:, 131:132], GN_EPS))
            st.lone(dve.memset(tiny[:, 132:133], 1.0))
            st.lone(dve.memset(tiny[:, 133:134], 0.0))
            st.lone(dve.memset(zero16[:, :], 0.0))
            st.settle()
            st.say(dve.memset(tiny[:, 134:135], 0.0), "zero_ready")

            def norm(k, a_count, dst=None, name="u_ready"):
                dst = uT if dst is None else dst
                dve.wait_ge(A.freed, a_count)
                st.own(dve.reciprocal(rstd, rstd))
                for c in range(DC):
                    ins = stt(dst[:, c, :], hT[:, c, :], col("gains", k * DC + c), rstd, ALU.mult, ALU.mult)
                    if c == DC - 1:
                        st.say(ins, name)
                    else:
                        st.lone(ins)
                st.settle()

            def attention(n0, scale, mask, y0, post=None):
                m384 = C(mask)
                for i in range(NH + LAG + 2):
                    if i < NH:
                        bank = V.take(dve)
                        if i >= NL:
                            dve.wait_ge(A.filled, done["attention", n0] + i - NL + 1)
                        V.free(stt(Lg[i % NL], bank[:, 0:384], scale, m384, ALU.mult, ALU.add))
                        dve.wait_ge(V.freed, V.nc)
                        st.lone(dve.tensor_reduce(nmx[:, i, 0:1], Lg[i % NL][:, 0:P], AX_X, ALU.max, negate=True))
                        st.say(dve.tensor_reduce(nmx[:, i, 1:2], Lg[i % NL][:, P:384], AX_X, ALU.max, negate=True), "nmax_ready")
                    if 1 <= i <= NH:
                        dve.wait_ge(S["exp_done"], n0 + i)
                        st.say(dve.reciprocal(rz[:, i - 1, :], zsum[:, i - 1, :]), "rz_ready")
                    h = i - LAG
                    if h >= 2 and h % 2 == 0:
                        bank = V.take(dve)
                        V.free(cp(ycat[:, y0 + h // 2 - 1, :], bank[:, 0:T]))

            def rope(x, n, which, ta, tb, into=None):
                cos2, sin2 = [C(f"{f}_{which}").rearrange("p (o t) -> p o t", o=1).broadcast_to([P, 2, T]) for f in ("cos", "sin")]
                ta, tb = chunks(ta, 2), chunks(tb, 2)
                for c in range(0, n, 2):
                    bank = V.take(dve)
                    x2 = x[:, c:c + 2, :]
                    V.free(tt(ta, bank[:, :].rearrange("p (c t) -> p c t", c=2), sin2, ALU.mult))
                    st.own(tt(tb, x2, cos2, ALU.mult))
                    dve.wait_ge(V.freed, V.nc)
                    if into is None:
                        st.say(tt(x2, ta, tb, ALU.add), "rope_done")
                    else:
                        st.lone(tt(into[0:HD, 0, c:c + 2, :], ta[0:HD], tb[0:HD], ALU.add))
                        st.say(tt(into[HD:P, 1, c:c + 2, :], ta[HD:P], tb[HD:P], ALU.add), "rope_done")
                    st.wait_said("rope_done")

            def clear_halves(q2):
                st.lone(dve.memset(q2[HD:P, 0], 0.0))
                st.lone(dve.memset(q2[0:HD, 1], 0.0))

            def residual():
                for n in range(N_OUT):
                    bank = V.take(dve)
                    ins = tt(hT[:, 2 * n:2 * n + 2, :], hT[:, 2 * n:2 * n + 2, :], bank[:, :], ALU.add)
                    V.free(ins)
                dve.wait_ge(V.freed, V.nc)
                st.say(dve.memset(tiny[:, 135:136], 0.0), "h_ready")

            dve.wait_ge(loaded, 48)
            norm(0, done["norm", 0])

            dve.wait_ge(A.freed, done["mla_std"])
            st.own(dve.reciprocal(std_m, std_m))
            st.own(dve.reciprocal(rt1[:, 0:T], rt1[:, 0:T]))
            st.lone(stt(qn[:, 0, :], qlat[:, 0, :], col("qnorm", 0), std_m, ALU.mult, ALU.mult))
            st.say(stt(qn[:, 1, :], qlat[:, 1, :], col("qnorm", 1), std_m, ALU.mult, ALU.mult), "mla_q")
            st.say(stt(kvn, kvl, col("kvnorm", 0), rt1[:, 0:T], ALU.mult, ALU.mult), "mla_kv")
            st.wait_said("mla_kv")
            bank = V.take(dve)
            V.free(tt(rt1[:, 0:T], bank[:, 0:T], C("sin_mla"), ALU.mult))
            st.own(tt(rt2[:, 0:T], kpe, C("cos_mla"), ALU.mult))
            dve.wait_ge(V.freed, V.nc)
            st.say(tt(kpe, rt1[:, 0:T], rt2[:, 0:T], ALU.add), "rope_done")
            st.wait_said("rope_done")
            kpe2 = kpe.rearrange("p (o t) -> p o t", o=1).broadcast_to([P, 2, T])
            for j2 in range(NH // 2):
                bank = V.take(dve)
                V.free(tt(kh[:, 2 * j2:2 * j2 + 2, :], bank[:, :].rearrange("p (c t) -> p c t", c=2), kpe2, ALU.add))
            dve.wait_ge(A.freed, done["mla"])
            rope(qh, NH, "mla", rt1, rt2)
            attention(0, (HD + 32) ** -0.5, "causal", GC)
            dve.wait_ge(V.freed, V.nc)

            st.lone(tt(rw[:, :, 1:T], raw[:, :, 0:T - 1], raw[:, :, 1:T], ALU.subtract))
            st.lone(ts(rw[:, :, 0:1], raw[:, :, 0:1], -1.0, None, ALU.mult))
            st.settle()
            for c in (12, 13) + tuple(range(12)):
                st.lone(stt(rw[:, c, :], rw[:, c, :], col("mu", c), raw[:, c, :], ALU.mult, ALU.add))
            st.settle()
            st.lone(dve.memset(lw[HD:P], 0.0))
            st.lone(dve.memset(lx[0:HD], 0.0))
            st.settle()
            st.say(dve.memset(tiny[:, 136:137], 0.0), "decay_in")
            r_, k_, v_ = rw[:, 0:4, :], rw[:, 4:8, :], rw[:, 8:12, :]
            for c in range(GC):
                ins = ts(kkr[:, c, :], rw[:, 4 + c, :], col("kkp", c), None, ALU.mult)
                if c == GC - 1:
                    st.say(ins, "kk_in")
                else:
                    st.lone(ins)
            st.lone(ts(omka, Pm("kap"), -1.0, 1.0, ALU.mult, ALU.add))
            st.settle()
            st.wait_said("kk_in")
            dve.wait_ge(A.freed, done["lora"])
            st.own(ts(logd, logd, -float(np.exp(-0.5)), None, ALU.mult))
            for c in range(GC):
                for a in range(TT):
                    st.lone(dve.tensor_tensor_scan(cs[:, c, a * P:(a + 1) * P], C("ones"), logd[:, c, a * P:(a + 1) * P],
                                                   0.0, ALU.mult, ALU.add))
            st.settle()
            cs8 = cs.rearrange("p c (a t) -> p (c a) t", a=TT)
            mid = tiny[:, 144:152]
            st.own(cp(mid, cs8[:, :, HD - 1:HD].rearrange("p n o -> p (n o)")))
            st.own(tt(cs8, cs8, mid.rearrange("p (n o) -> p n o", o=1).broadcast_to([P, 8, P]), ALU.subtract))
            st.say(tt(csx, cs, logd, ALU.subtract), "exp_in")
            st.own(tt(tiny[:, 140:144], cs[:, :, P - 1:P].rearrange("p c o -> p (c o)"),
                      mid.rearrange("p (c a) -> p c a", a=TT)[:, :, 1], ALU.add))
            st.say(dve.memset(tiny[:, 137:138], 0.0), "exp_in")
            for c in range(GC):
                st.lone(ts(bon[:, c, :], iclr[:, c, :], col("kap", c), omka[:, c:c + 1], ALU.mult, ALU.add))
            st.settle()
            dve.wait_ge(A.freed, done["kk"])
            st.own(tt(k2, k_, bon, ALU.mult))
            st.own(ts(kk, kk, 1e-12, None, ALU.max))
            st.own(dve.reciprocal(kk, kk))
            st.own(tt(kk, kk, kkr, ALU.mult))
            for c in range(GC):
                ins = stt(bon[:, c, :], rw[:, c, :], col("rkp", c), k2[:, c, :], ALU.mult, ALU.mult)
                if c == GC - 1:
                    st.say(ins, "bonus_in")
                else:
                    st.lone(ins)
            dve.wait_ge(S["exp_out"], 1)
            v4 = lambda x: x.rearrange("p c (a t) -> p c a t", a=TT)
            st.lone(tt(KR[:, :, :, 0, :], v4(kk), v4(E2), ALU.mult))
            st.lone(tt(KR[:, :, :, 1, :], v4(r_), v4(E1), ALU.mult))
            st.own(tt(Ks, k2, E3, ALU.mult))
            st.own(tt(Bs, kk, iclr, ALU.mult))
            st.own(tt(Bs, Bs, E3, ALU.mult))
            st.say(dve.memset(tiny[:, 138:139], 0.0), "keys_ready")
            for j2 in range(2):
                bank = V.take(dve)
                V.free(tt(csx[:, 2 * j2:2 * j2 + 2, :], v_[:, 2 * j2:2 * j2 + 2, :], bank[:, :], ALU.mult))

            idb = C("ident").rearrange("p (o s) -> p o s", o=1).broadcast_to([P, 4, P])
            for a in range(TT):
                if a:
                    dve.wait_ge(A.freed, done["y", 0])
                for h in range(NH):
                    bank = V.take(dve)
                    V.free(tt(AT[:, h].rearrange("p q s -> p (q s)"), bank[:, :], C("mask4"), ALU.mult))
                dve.wait_ge(V.freed, V.nc)
                for par_ in range(2):
                    hs = slice(par_, NH, 2)
                    bank = V.take(dve)
                    b3 = bank[:, :].rearrange("p (h s) -> p h s", h=4)
                    l1 = C("level1").rearrange("p (o s) -> p o s", o=1).broadcast_to([P, 4, P])
                    l1T = C("levelT1").rearrange("p (o s) -> p o s", o=1).broadcast_to([P, 4, P])
                    V.free(tt(Dm[:, hs, :], b3, l1, ALU.mult))
                    dve.wait_ge(V.freed, V.nc)
                    st.own(tt(Dm[:, hs, :], idb, Dm[:, hs, :], ALU.subtract))
                    st.own(tt(DmT[:, hs, :], AT[:, hs, 0, :], l1T, ALU.mult))
                    st.own(tt(DmT[:, hs, :], idb, DmT[:, hs, :], ALU.subtract))
                for n, m in enumerate(LEVELS):
                    lT = C(f"levelT{m}").rearrange("p (o s) -> p o s", o=1).broadcast_to([P, NH, P])
                    if n == 0:
                        st.say(tt(CTm[0], AT[:, :, 0, :], lT, ALU.mult), "level_ct")
                    if n + 1 < len(LEVELS):
                        lT = C(f"levelT{LEVELS[n + 1]}").rearrange("p (o s) -> p o s", o=1).broadcast_to([P, NH, P])
                        if n:
                            dve.wait_ge(A.freed, done["levels", a] + 2 * n)
                        st.say(tt(CTm[(n + 1) % 2], AT[:, :, 0, :], lT, ALU.mult), "level_ct")
                    for h4 in range(2):
                        hs = slice(4 * h4, 4 * h4 + 4)
                        if m != LEVELS[-1]:
                            b1 = V.take(dve)
                            V.free(tt(Dm[:, hs, :], Dm[:, hs, :], b1[:, :].rearrange("p (h s) -> p h s", h=4), ALU.subtract))
                        b2 = V.take(dve)
                        V.free(tt(DmT[:, hs, :], DmT[:, hs, :], b2[:, :].rearrange("p (h s) -> p h s", h=4), ALU.subtract))
                    dve.wait_ge(V.freed, V.nc)
                if a == 0:
                    bank = V.take(dve)
                    dve.wait_ge(S["exp_out"], 1)
                    for c in range(GC):
                        ins = stt(Sbd[:, c, :], bank[:, c * P:(c + 1) * P], fend[:, c:c + 1], C("same_head"), ALU.mult, ALU.mult)
                        if c == GC - 1:
                            V.free(ins)
                        else:
                            st.lone(ins)
                    st.settle()
                    dve.wait_ge(V.freed, V.nc)
                    st.say(dve.memset(tiny[:, 139:140], 0.0), "state_ready")
            dve.wait_ge(A.freed, done["y", 1])
            for j2 in range(2):
                bank = V.take(dve)
                y2 = yT[:, 2 * j2:2 * j2 + 2, :]
                V.free(stt(y2, bank[:, :].rearrange("p (j t) -> p j t", j=2), -1.0 / HD, y2, ALU.mult, ALU.add))
            dve.wait_ge(V.freed, V.nc)
            st.say(dve.memset(tiny[:, 152:153], 0.0), "gn_in")
            dve.wait_ge(A.freed, done["gn"])
            st.own(dve.reciprocal(cs, cs))
            st.own(tt(yT, yT, cs, ALU.mult))
            for c in range(GC):
                st.lone(ts(yT[:, c, :], yT[:, c, :], col("lnxg", c), col("lnxb", c), ALU.mult, ALU.add))
            st.settle()
            st.own(tt(yT, yT, csx, ALU.add))
            st.own(tt(ycat[:, 0:GC, :], yT, g_, ALU.mult))
            st.say(dve.memset(tiny[:, 153:154], 0.0), "y_ready")
            residual()

            norm(1, done["norm", 1])

            def ffn_step(s, n_sig, first):
                dve.wait_ge(S["ffn_sig"], n_sig)
                tt(gtmp[s], sigb[s], banks[s][:, :], ALU.mult).then_inc(S["ffn_mid"], 1)
                dve.wait_ge(S["ffn_mid"], n_sig)
                tt(hid[s], gtmp[s], banks[2 + s][:, :], ALU.mult).then_inc(S["ffn_hid"], 1)

            ffn_step(0, 1, True)
            ffn_step(1, 2, True)
            with dve.Fori(1, FFN_STEPS // 2) as it:
                for s in range(2):
                    dve.wait_ge(S["ffn_down"], it * 2 + (s - 1))
                    ffn_step(s, it * 2 + (s + 1), False)
            dve.wait_ge(S["ffn_down"], FFN_STEPS - 2)
            ffn_step(0, FFN_STEPS, False)
            dve.wait_ge(S["ffn_down"], FFN_STEPS)
            for n in range(4):
                st.lone(tt(hT[:, 2 * n:2 * n + 2, :], hT[:, 2 * n:2 * n + 2, :], banks[4 + n][:, :], ALU.add))
            st.settle()
            st.say(dve.memset(tiny[:, 154:155], 0.0), "h_ready")

            clear_halves(fq2)
            clear_halves(mq2)
            st.say(dve.memset(fnd, 0.0), "zero_ready")
            norm(2, done["norm", 2])
            bank = V.take(dve)
            z8 = fz[0:NH]
            V.free(ts(z8, bank[0:NH, 0:T], par[0:NH, par_at["foxbf"][0]:par_at["foxbf"][0] + 1], None, ALU.add))
            dve.wait_ge(V.freed, V.nc)
            st.own(ts(fe[0:NH], z8, -1.0, None, ALU.mult))
            st.say(tt(fl[0:NH], fe[0:NH], z8, ALU.max), "fox_z")
            st.own(ts(z8, z8, 0.0, None, ALU.min))
            dve.wait_ge(S["fox_e"], 1)
            st.own(tt(z8, z8, fe[0:NH], ALU.subtract))
            st.own(ts(fl[0:NH], z8, 0.0, 1.0, ALU.mult, ALU.add))
            st.wait_said("zero_ready")
            st.own(dve.tensor_tensor_scan(fd[0:NH], fl[0:NH], z8, 0.0, ALU.mult, ALU.add))
            st.say(ts(fnd[0:NH], fd[0:NH], -1.0, None, ALU.mult), "fox_d")
            dve.wait_ge(A.freed, done["l1"])
            rope(mq, GC, "full", r1a, r1b, mq2)
            rope(mk, GC, "full", r1a, r1b)
            attention(NH, HD ** -0.5, "causal", 0)
            attention(2 * NH, HD ** -0.5, "causal", GC)
            dve.wait_ge(V.freed, V.nc)
            st.say(dve.memset(tiny[:, 155:156], 0.0), "y_ready")
            residual()

            norm(3, done["norm", 3])
            bank = V.take(dve)
            V.free(cp(lg, bank[:, 0:TT * E]))
            dve.wait_ge(V.freed, V.nc)
            l3 = lg.rearrange("p (a e) -> p a e", a=TT)
            m3 = lambda x: x.rearrange("p (a o) -> p a o", o=1).broadcast_to([P, TT, E])
            st.own(dve.tensor_reduce(m0, l3, AX_X, ALU.max))
            st.say(tt(ex.rearrange("p (a e) -> p a e", a=TT), l3, m3(m0), ALU.subtract), "router_l")
            low = C("lower").rearrange("p (e j) -> p e j", e=E)
            for a in range(TT):
                la_ = lg[:, a * E:(a + 1) * E]
                lj = la_.rearrange("p (o j) -> p o j", o=1).broadcast_to([P, E, E])
                le = la_.rearrange("p (e o) -> p e o", o=1).broadcast_to([P, E, E])
                b1 = big[:, a * E * E:(a + 1) * E * E].rearrange("p (e j) -> p e j", e=E)
                b2 = big2[:, a * E * E:(a + 1) * E * E].rearrange("p (e j) -> p e j", e=E)
                st.lone(tt(b1, lj, le, ALU.is_gt))
                st.own(tt(b2, lj, le, ALU.is_equal))
                st.own(tt(b2, b2, low, ALU.mult))
                st.own(tt(b1, b1, b2, ALU.add))
                st.own(dve.tensor_reduce(rank[:, a * E:(a + 1) * E], b1, AX_X, ALU.add))
            st.say(ts(selm, rank, 1.5, None, ALU.is_lt), "router_sel")
            st.wait_said("router_sel")
            dve.wait_ge(S["router_e"], 1)
            st.own(tt(comb, ex, selm, ALU.mult))
            c3 = comb.rearrange("p (a e) -> p a e", a=TT)
            st.own(dve.tensor_reduce(den, c3, AX_X, ALU.add))
            st.own(dve.reciprocal(den, den))
            st.own(tt(c3, c3, m3(den), ALU.mult))
            bank = V.take(dve)
            st.lone(cp(posm, bank[:, 0:2 * E]))
            V.free(cp(cnt, bank[:, 2 * E:3 * E]))
            st.settle()
            dve.wait_ge(V.freed, V.nc)
            st.own(ts(rank, selm, -1e4, 1e4, ALU.mult, ALU.add))
            st.own(tt(posm, posm, rank, ALU.add))
            for a in range(TT):
                st.lone(cp(table[:, 0:E, a], posm[:, a * E:(a + 1) * E]))
                st.lone(ts(table[:, E:2 * E, a], posm[:, a * E:(a + 1) * E], -float(P), None, ALU.add))
                st.lone(cp(table[:, 0:E, 2 + a], comb[:, a * E:(a + 1) * E]))
                st.lone(cp(table[:, E:2 * E, 2 + a], comb[:, a * E:(a + 1) * E]))
            st.own(dve.tensor_reduce(mcnt[:, 0:1], cnt, AX_X, ALU.max))
            st.own(ts(mcnt[:, 1:2], mcnt[:, 0:1], P + 0.5, 1.0, ALU.is_gt, ALU.add))
            cp(passes_i[:, :], mcnt[:, 1:2]).then_inc(flag_ready, 1)
            dve.wait_ge(flag_ready, 1)
            passes = dve.value_load(passes_i[0:1, 0:1], min_val=1, max_val=2)
            with dve.Fori(0, passes) as ps:
                with dve.Fori(0, E) as e:
                    ex_n = dve.snap(ps * E + e)
                    cp(cur, table[:, bass.ds(ex_n, 1), :].rearrange("p o k -> p (o k)")).then_inc(S["moe_tab"], 1)
                    dve.wait_ge(S["moe_tab"], ex_n + 1)
                    ts(oh[:, 0, :], C("slot_iota"), cur[:, 0:1], None, ALU.is_equal).then_inc(S["moe_vec"], 1)
                    ts(oh[:, 1, :], C("slot_iota"), cur[:, 1:2], None, ALU.is_equal).then_inc(S["onehot"], 1)
                    dve.wait_ge(S["onehot"], ex_n + 1)
                    ts(ohg[:, 0, :], oh[:, 0, :], cur[:, 2:3], None, ALU.mult).then_inc(S["moe_vec"], 1)
                    ts(ohg[:, 1, :], oh[:, 1, :], cur[:, 3:4], None, ALU.mult).then_inc(S["onehot_g"], 1)

                    def step(s, n):
                        dve.wait_ge(S["moe_sig"], n)
                        tt(gtmp[s][:, 0:T], sigb[s][:, 0:T], banks[s][:, 0:T], ALU.mult).then_inc(S["moe_mid"], 1)
                        dve.wait_ge(S["moe_mid"], n)
                        tt(hid[s][:, 0:T], gtmp[s][:, 0:T], banks[s][:, T:2 * T], ALU.mult).then_inc(S["moe_hid"], 1)

                    base = dve.snap(ex_n * MOE_STEPS)
                    step(0, base + 1)
                    step(1, base + 2)
                    with dve.Fori(1, MOE_STEPS // 2) as it:
                        for s in range(2):
                            dve.wait_ge(S["moe_down"], base + it * 2 + (s - 1))
                            step(s, base + it * 2 + (s + 1))
                    for c2 in range(4):
                        bank = banks[(7, 2, 3, 7)[c2]]
                        dve.wait_ge(S["moe_sc"], ex_n * 4 + (c2 + 1))
                        tt(hT[:, 2 * c2:2 * c2 + 2, :], hT[:, 2 * c2:2 * c2 + 2, :], bank[:, :], ALU.add).then_inc(S["moe_add"], 1)
            st.say(dve.memset(tiny[:, 160:161], 0.0), "moe_end")
            st.say(dve.memset(tiny[:, 156:157], 0.0), "h_ready")

            norm(4, done["norm", 4], dst=hT, name="u_ready")
            st.wait_said("u_ready")
            st.say(dve.memset(tiny[:, 157:158], 0.0), "h_ready")
            for l in range(2):
                clear_halves(cq2)
                norm(5 + l, done["norm", 5 + l])
                lam = Pm("lam")[:, 2 * l:2 * l + 2]
                L = lambda i: lam_t[:, 2 * i:2 * i + 2]
                st.own(ts(L(2), lam, -1.0, None, ALU.mult))
                st.say(tt(L(0), L(2), lam, ALU.max), "lam_in")
                dve.wait_ge(S["lam_e"], l + 1)
                st.own(ts(L(3), L(1), 2.0, None, ALU.add))
                st.own(dve.reciprocal(L(3), L(3)))
                st.own(tt(L(3), L(3), L(1), ALU.mult))
                st.own(tt(L(4), L(3), L(3), ALU.mult))
                st.own(ts(L(5), L(4), 1.0 / 17, 1.0 / 15, ALU.mult, ALU.add))
                for k in (13, 11, 9, 7, 5, 3, 1):
                    st.own(tt(L(5), L(5), L(4), ALU.mult))
                    st.own(ts(L(5), L(5), 1.0 / k, None, ALU.add))
                st.own(tt(L(5), L(5), L(3), ALU.mult))
                st.own(ts(L(6), lam, 0.0, None, ALU.min))
                st.own(stt(L(6), L(5), -2.0, L(6), ALU.mult, ALU.add))
                st.say(ts(L(10), L(6), 8.0, None, ALU.mult), "lam_c")

                dve.wait_ge(A.freed, done["hybrid", l])
                for c in range(2):
                    w = lambda j: col("convw", (2 * l + c) * 4 + j)
                    st.own(ts(xc[:, c, :], bx[:, c, :], w(3), col("convb", 2 * l + c), ALU.mult, ALU.add))
                    for j in range(3):
                        sh = 3 - j
                        st.own(stt(xc[:, c, sh:T], bx[:, c, 0:T - sh], w(j), xc[:, c, sh:T], ALU.mult, ALU.add))
                st.say(tt(gate, gate, gsig, ALU.mult), "conv_done")
                st.wait_said("conv_done")
                clear_halves(hq2)
                st.settle()
                rope(hq, GC, "part", hra, hrb, hq2)
                rope(hk, GC, "part", hra, hrb)
                dve.wait_ge(S["lru_a"], l + 1)
                st.own(ts(lq, lt, -1.0, 1.0, ALU.mult, ALU.add))
                st.own(dve.reciprocal(lq, lq))
                st.say(stt(lq, lt, -2.0, lq, ALU.mult, ALU.mult), "lru_q")
                st.own(tt(lu, li, xc, ALU.mult))
                dve.wait_ge(S["lru_s"], l + 1)
                st.own(tt(lu, lu, lq, ALU.mult))
                for c in range(2):
                    st.lone(dve.tensor_tensor_scan(ycat[:, GC + c, :], la[:, c, :], lu[:, c, :], 0.0, ALU.mult, ALU.add))
                attention((3 + l) * NH, HD ** -0.5, "dilated", 0)
                for h in range(4):
                    bank = V.take(dve)
                    V.free(ts(zb[:, h, :], bank[:, 0:384], HD ** -0.5, None, ALU.mult))
                dve.wait_ge(V.freed, V.nc)
                st.say(dve.memset(tiny[:, 158:159], 0.0), "stick_z")
                dve.wait_ge(S["stick_l"], l + 1)
                st.own(stt(zl, zb, 0.0, zl, ALU.max, ALU.add))
                m01 = C("stick01").rearrange("p (o n) -> p o n", o=1).broadcast_to([P, 4, 384])
                madd = C("stick_add").rearrange("p (o n) -> p o n", o=1).broadcast_to([P, 4, 384])
                st.say(tt(zl, zl, m01, ALU.mult), "stick_n")
                st.own(tt(zb, zb, madd, ALU.add))
                for h in range(4):
                    bank = V.take(dve)
                    V.free(tt(zw[:, h, :], zb[:, h, :], bank[:, 0:384], ALU.add))
                dve.wait_ge(V.freed, V.nc)
                st.say(dve.memset(tiny[:, 159:160], 0.0), "stick_arg")
                for c in range(2):
                    bank = V.take(dve)
                    V.free(cp(ycat[:, GC + 2 + c, :], bank[:, 0:T]))
                dve.wait_ge(V.freed, V.nc)
                st.settle()
                st.wait_said("conv_done")
                st.say(tt(ycat, ycat, gate, ALU.mult), "y_ready")
                residual()
            norm(7, done["norm", 7], name="out_ready")

        @block.gpsimd
        def _(pool):
            st = Step(pool, sem("pool_step"))
            for n in range(5 * NH):
                i = n % NH
                pool.wait_ge(S["rz_ready"], n + 1)
                st.lone(pool.tensor_scalar(Lg[i % NL][:, 0:P], Lg[i % NL][:, 0:P], rz[:, i, 0:1], 1.0, ALU.mult, ALU.mult))
                st.say(pool.tensor_scalar(Lg[i % NL][:, P:384], Lg[i % NL][:, P:384], rz[:, i, 1:2], 1.0, ALU.mult, ALU.mult), "prob_ready")



def kernel(**inputs):
    import concourse.bacc as bacc
    from concourse.bass_utils import run_bass_kernel_spmd

    w = {k: np.asarray(v) for k, v in inputs.items()}

    def feature_major(v):
        return v.reshape(-1, P).T

    def slots(m):
        return m.reshape(DC, P, -1, SLOT_COLS).transpose(2, 1, 0, 3).reshape(-1, P, SLOT)

    def down_slots(m):
        return m.reshape(-1, 2, P, D).transpose(0, 2, 1, 3).reshape(-1, P, SLOT)

    def swiglu_slots(g, u, d):
        g, u, d = slots(g), slots(u), down_slots(d)
        order = [g[0], u[0]]
        for i in range(1, len(g)):
            order += [g[i], u[i], d[i - 1]]
        return np.stack(order + [d[-1]])

    w_in0 = w["w_in_0"]
    w_in0 = np.concatenate([w_in0[:, :1792 + 256 + 128], np.pad(w_in0[:, 1792 + 384:], ((0, 0), (HD, 32)))], 1)
    w_in1 = w["w_in_1"]
    stream = [slots(w_in0), slots(w["w_out_0"]),
              swiglu_slots(w["ffn_wg_0"], w["ffn_wu_0"], w["ffn_wd_0"]),
              slots(w_in1[:, :3 * GW]), slots(w_in1[:, 3 * GW + NH:]), slots(w["w_out_1"])]
    stream += [swiglu_slots(w["moe_wg_1"][e], w["moe_wu_1"][e], w["moe_wd_1"][e]) for e in range(E)]
    for l in range(2):
        stream += [slots(w["w_in_2"][l]), slots(w["w_out_2"][l])]
    stream = np.concatenate(stream)

    def uq():
        m = np.pad(w["mla_wuq_0"].reshape(256, NH, 96), ((0, 0), (0, 0), (0, 32)))
        return m.reshape(2, P, NH * P).transpose(1, 0, 2).reshape(P, -1)

    def ukv():
        m = w["mla_wukv_0"].reshape(P, NH, 128)
        k = np.pad(m[:, :, :64], ((0, 0), (0, 0), (0, 64)))
        return np.concatenate([k.reshape(P, NH * P), m[:, :, 64:].reshape(P, GW)], 1)

    def block_diagonal(m):
        out = np.zeros((P, 2, 2, P), np.float32)
        for l in range(2):
            for n in range(4):
                h = n % 2
                out[h * 64:h * 64 + 64, l, n // 2, h * 64:h * 64 + 64] = m[l, n]
        return out.reshape(P, -1)

    def rows(m):
        return m.reshape(DC, P, -1).transpose(1, 0, 2).reshape(P, -1)

    bf = np.zeros((P, 1), np.float32)
    bf[:NH, 0] = w["fox_bf_1"]
    gains = np.concatenate([w["norm_mix_0"], w["norm_ffn_0"], w["norm_mix_1"], w["norm_ffn_1"],
                            w["final_norm"], w["norm_gain_2"].reshape(-1), w["final_gain_2"]])
    small = dict(
        gains=feature_major(gains), mu=feature_major(w["shift_mu_0"]), w0=feature_major(w["rw_w0_0"]),
        a0=feature_major(w["rw_a0_0"]), kkp=feature_major(w["rw_kk_0"]), kap=feature_major(w["rw_ka_0"]),
        rkp=feature_major(w["rw_rk_0"]), lnxg=feature_major(w["rw_lnx_g_0"]), lnxb=feature_major(w["rw_lnx_b_0"]),
        qnorm=feature_major(w["mla_qnorm_0"]), kvnorm=feature_major(w["mla_kvnorm_0"]),
        wa2=np.concatenate([w["rw_w2_0"], w["rw_a2_0"]]), g2=w["rw_g2_0"], wuq=uq(), wukv=ukv(),
        foxbf=bf, wf=rows(w_in1[:, 3 * GW:3 * GW + NH]), router=rows(w["router_1"]),
        convw=w["conv_w_2"].reshape(2, 4, 2, P).transpose(3, 0, 2, 1).reshape(P, -1),
        convb=feature_major(w["conv_b_2"]), gab=feature_major(w["gate_a_b_2"]), gxb=feature_major(w["gate_x_b_2"]),
        lam=feature_major(w["lru_lambda_2"]), gaw=block_diagonal(w["gate_a_w_2"]), gxw=block_diagonal(w["gate_x_w_2"]))
    params = np.concatenate([small[k] for k in PARAMS], 1)
    assert params.shape[1] == sum(PARAMS.values())

    consts = shape_constants()
    const_at, at = {}, 0
    for k, v in consts.items():
        const_at[k] = (at, v.shape[1])
        at += v.shape[1]
    arrays = {
        "x_dram": rows(w["x"][0].T), "const_dram": np.concatenate(list(consts.values()), 1),
        "param_dram": params, "w_dram": stream,
    }
    nc = bacc.Bacc("TRN2", target_bir_lowering=False, num_devices=1)
    arrays = {k: np.ascontiguousarray(v) for k, v in arrays.items()}
    args = [nc.dram_tensor(k, v.shape, F32, kind="ExternalInput").ap() for k, v in arrays.items()]
    out = nc.dram_tensor("out_dram", (P, DC * T), F32, kind="ExternalOutput").ap()
    program(nc, *args, out, const_at)
    r = run_bass_kernel_spmd(nc, [arrays], core_ids=[0])
    y = r.results[0]["out_dram"]
    return np.ascontiguousarray(y.reshape(P, DC, T).transpose(2, 1, 0).reshape(1, T, D))
```

```python
from contextlib import ExitStack

import numpy as np
import concourse.bass as bass
from concourse import mybir

F32 = mybir.dt.float32
F32R = mybir.dt.float32r
BF16 = mybir.dt.bfloat16
I32 = mybir.dt.int32
ALU = mybir.AluOpType
ACT = mybir.ActivationFunctionType
AX_X = mybir.AxisListType.X

P = 128
T = 256
TT = T // P
D = 1024
DC = D // P
HD = 64
NH = 8
GW = NH * HD
GC = GW // P
E = 8
RING = 3
SLOT = 2048
SLOT_COLS = SLOT // DC

N_IN0, N_OUT, N_FFN, N_IN1 = 9, 4, 33, 12
FFN_STEPS = 11
MOE_STEPS = 14
MOE_SLOTS = 3 * MOE_STEPS
N_EARLY = N_IN0 + N_OUT + N_FFN + N_IN1 + N_OUT
N_MOE = E * MOE_SLOTS
N_IN2 = 14
N_LATE = 2 * (N_IN2 + N_OUT)
W_MOE = N_EARLY
W_LATE = N_EARLY + N_MOE
EPS = 1e-6
GN_EPS = 64e-5
NEG = -1e30
LAG = 3
NL = LAG + 2
LEVELS = (2, 4, 8, 16, 32, 64)



def rope_table(n_rot, theta, period, first=0):
    half = n_rot // 2
    inv = np.float32(theta) ** (-np.arange(0, n_rot, 2, dtype=np.float32) / np.float32(n_rot))
    ang = np.arange(T, dtype=np.float32)[None, :] * inv[:, None].astype(np.float32)
    cos, sin = np.ones((P, T), np.float32), np.zeros((P, T), np.float32)
    for f in range(P):
        if 0 <= f % period - first < n_rot:
            row = (f % period - first) % half
            cos[f], sin[f] = np.cos(ang[row]), np.sin(ang[row])
    return cos, sin


def rope_partner(n_rot, period, first=0):
    perm, half = np.zeros((P, P), np.float32), n_rot // 2
    for o in range(P):
        r = o % period - first
        if 0 <= r < half:
            perm[o + half, o] = -1.0
        elif half <= r < n_rot:
            perm[o - half, o] = 1.0
    return perm


def shape_constants():
    i, j = np.arange(P)[:, None], np.arange(P)[None, :]
    c = {}
    c["ident"] = (i == j)
    c["ones"] = np.ones((P, P))
    c["same_head"] = (i // HD == j // HD)
    strict, incl = (i < j), (i <= j)
    c["mask4"] = np.concatenate([strict, incl, strict, incl], 1)
    c["level1"] = (i == j + 1) & (i % 2 == 1)
    for m in (1,) + LEVELS:
        c[f"levelT{m}"] = (i // (2 * m) == j // (2 * m)) & (i // m < j // m)
    t, s = np.arange(T)[:, None], np.arange(T)[None, :]
    causal = np.where(s <= t, 0.0, NEG)
    gap = t - s
    count = ((gap >= 0) & (gap <= 128)) * 1.0 + ((gap >= 0) & (gap % 4 == 0)) + ((gap >= 0) & (gap % 16 == 0))
    dil = np.where(count > 0, np.log(np.maximum(count, 1)), NEG)
    for name, m in (("causal", causal), ("dilated", dil)):
        c[name] = np.concatenate([m[:P, :P], m[P:, :]], 1)
    stick = np.concatenate([strict, np.ones((P, P)), strict], 1)
    c["stick01"] = stick
    c["stick_add"] = np.where(stick > 0, 0.0, NEG)
    c["neg_tail"] = -1.0 * (i >= j)
    c["neg_ones"] = -np.ones((P, P))
    c["slot_iota"] = np.broadcast_to(np.arange(P), (P, P))
    lower = (np.arange(E)[None, :] < np.arange(E)[:, None]) * 1.0
    c["lower"] = np.broadcast_to(lower.reshape(1, E * E), (P, E * E))
    c["pick8"] = 8.0 * (np.arange(P)[:, None] == np.arange(NH)[None, :])
    for name, rot, theta, period, first in (("mla", 32, 1e4, 128, 64), ("full", 64, 1e4, 64, 0), ("part", 16, 5e5, 64, 0)):
        c[f"cos_{name}"], c[f"sin_{name}"] = rope_table(rot, theta, period, first)
        c[f"partner_{name}"] = rope_partner(rot, period, first)
    return {k: np.asarray(v, np.float32) for k, v in c.items()}


PARAMS = dict(
    gains=8 * DC, mu=14, w0=GC, a0=GC, kkp=GC, kap=GC, rkp=GC, lnxg=GC, lnxb=GC,
    qnorm=2, kvnorm=1, wa2=GW, g2=GW, wuq=2 * NH * P, wukv=NH * P + GW,
    foxbf=1, wf=DC * NH, router=DC * E, convw=2 * 2 * 4, convb=4, gab=4, gxb=4, lam=4,
    gaw=2 * 2 * P, gxw=2 * 2 * P)


def program(nc, x_dram, const_dram, param_dram, w_dram, out_dram, const_at):
    ctx = ExitStack()
    with ctx:
        def sb(name, cols, dt=F32):
            return ctx.enter_context(nc.sbuf_tensor(name, [P, cols], dt))

        def sem(name):
            return ctx.enter_context(nc.semaphore(name))

        ring = sb("weight_ring", RING * SLOT)
        with nc.sbuf_tensor("rwkv_scratch", [P, 7168], F32) as scratch_b:
            pass
        whi = [sb(f"weights_high{i}", SLOT, F32R) for i in range(2)]
        wlo = [sb(f"weights_low{i}", SLOT, F32R) for i in range(2)]
        uhi_ = sb("operand_high", DC * T, F32R)
        ulo_ = sb("operand_low", DC * T, F32R)
        hT_ = sb("hT", DC * T)
        yc_ = sb("ycat", DC * T)
        sq_ = sb("squares", DC * T)
        cst = sb("constants", const_dram.shape[1])
        par = sb("parameters", param_dram.shape[1])
        tiny = sb("tiny", 192)
        zero16 = sb("zero16", P, BF16)
        passes_i = sb("expert_passes", 1, I32)
        ARENA = 15872
        with nc.sbuf_tensor("arena", [P, ARENA], F32) as arena:
            pass
        with ExitStack() as over:
            over.enter_context(nc.sbuf_tensor("arena_start", [P, ARENA - 2 * SLOT - 4 * 512], F32))
            whi.append(over.enter_context(nc.sbuf_tensor("weights_high2", [P, SLOT], F32R)))
            wlo.append(over.enter_context(nc.sbuf_tensor("weights_low2", [P, SLOT], F32R)))
            hhi = [over.enter_context(nc.sbuf_tensor(f"hidden_high{i}", [P, 512], F32R)) for i in range(2)]
            hlo = [over.enter_context(nc.sbuf_tensor(f"hidden_low{i}", [P, 512], F32R)) for i in range(2)]
        uT_ = sq_
        hT = hT_[:, :].rearrange("p (c t) -> p c t", c=DC)
        uT = sq_[:, :].rearrange("p (c t) -> p c t", c=DC)
        uhi = uhi_[:, :].rearrange("p (c t) -> p c t", c=DC)
        ulo = ulo_[:, :].rearrange("p (c t) -> p c t", c=DC)
        xhi = uhi_[:, 0:DC * P].rearrange("p (c s) -> p c s", c=DC)
        xlo = ulo_[:, 0:DC * P].rearrange("p (c s) -> p c s", c=DC)
        ycat = yc_[:, :].rearrange("p (c t) -> p c t", c=DC)
        sq = sq_[:, :].rearrange("p (c t) -> p c t", c=DC)

        def C(name):
            a, n = const_at[name]
            return cst[:, a:a + n]

        par_at, at = {}, 0
        for k, n in PARAMS.items():
            par_at[k] = (at, n)
            at += n

        def Pm(name):
            a, n = par_at[name]
            return par[:, a:a + n]

        def col(name, i):
            a, _ = par_at[name]
            return par[:, a + i:a + i + 1]

        class Arena:
            def __init__(self, start=0):
                self.at = start

            def take(self, n):
                a = self.at
                self.at += n
                assert self.at <= ARENA, self.at
                return arena[:, a:a + n]

        def chunks(ap, c):
            return ap.rearrange("p (c t) -> p c t", c=c)

        banks = [ctx.enter_context(nc.psum_tensor(f"bank{i}", [P, 512], F32)) for i in range(8)]

        loaded = sem("inputs_loaded")
        tables_loaded = sem("tables_loaded")
        stored = sem("output_stored")
        landed = [sem(f"weights_landed{i}") for i in range(RING)]
        late_landed = [sem(f"late_weights_landed{i}") for i in range(RING)]
        high = [sem("weights_high_ready"), sem("late_weights_high_ready")]
        split = [sem("weights_split"), sem("late_weights_split")]
        flag_ready = sem("expert_passes_known")
        names = ("squares_ready", "std_ready", "u_half", "u_ready", "h_ready", "y_ready",
                 "zero_ready",
                 "lora_in", "kk_in", "decay_in", "exp_in", "exp_out", "keys_ready", "bonus_in",
                 "masked", "level_ct", "inv_update", "solve_x", "solve_u", "state_ready", "tok_ready",
                 "gn_in", "gn_sq", "gn_std", "gn_var", "kk_sq", "kk_std", "lru_arg",
                 "mla_sq", "mla_std", "mla_q", "mla_kv", "rope_in", "rope_done",
                 "nmax_ready", "exp_done", "rz_ready", "prob_ready",
                 "fox_z", "fox_e", "fox_d", "stick_z", "stick_l", "stick_n", "stick_arg", "stick_w",
                 "conv_done", "lru_gates", "lru_a", "lru_t", "lru_q", "lru_s", "lam_in", "lam_e", "lam_c",
                 "gate_raw", "gate_done",
                 "router_l", "router_e", "router_sel", "tok_major", "onehot", "onehot_g",
                 "moe_tab", "moe_gu", "moe_sig", "moe_hid", "moe_down", "moe_x", "moe_y", "moe_ytok",
                 "moe_gt", "moe_gtt", "moe_g", "moe_sc", "moe_add", "moe_end",
                 "act_hi", "act_lo", "moe_xh", "moe_h", "moe_tr", "moe_hh", "ffn_mid", "ffn_h", "ffn_hh", "moe_mid", "moe_act", "moe_vec", "ffn_gate", "ffn_gu", "ffn_sig", "ffn_hid", "ffn_down", "out_ready")
        S = {n: sem(n) for n in names}

        class Channel:
            def __init__(self, which, filled, freed):
                self.which, self.filled, self.freed, self.np, self.nc = which, filled, freed, 0, 0

            def claim(self, pe):
                n = self.np
                if n >= len(self.which):
                    pe.wait_ge(self.freed, n - len(self.which) + 1)
                return banks[self.which[n % len(self.which)]]

            def fill(self, ins):
                ins.then_inc(self.filled, 1)
                self.np += 1
                return self.np

            def take(self, eng):
                eng.wait_ge(self.filled, self.nc + 1)
                return banks[self.which[self.nc % len(self.which)]]

            def free(self, ins):
                ins.then_inc(self.freed, 1)
                self.nc += 1
                return self.nc

        A = Channel((0, 1, 6, 7), sem("psum_for_scalar"), sem("scalar_read_psum"))
        V = Channel((2, 3, 4, 5), sem("psum_for_vector"), sem("vector_read_psum"))

        class Step:
            def __init__(self, eng, chain):
                self.eng, self.chain, self.n, self.said = eng, chain, 0, {}

            def own(self, ins):
                self.n += 1
                ins.then_inc(self.chain, 1)
                self.eng.wait_ge(self.chain, self.n)

            def lone(self, ins):
                self.n += 1
                ins.then_inc(self.chain, 1)

            def settle(self):
                self.eng.wait_ge(self.chain, self.n)

            def say(self, ins, name):
                self.said[name] = self.said.get(name, 0) + 1
                ins.then_inc(S[name], 1)

            def wait_said(self, name):
                self.eng.wait_ge(S[name], self.said[name])

        ar = Arena()
        raw = chunks(ar.take(14 * T), 14)
        qlat = chunks(ar.take(2 * T), 2)
        kvl = ar.take(T)
        kpe = ar.take(T)
        ATT = ar.at
        qh = chunks(ar.take(NH * T), NH)
        kh = chunks(ar.take(NH * T), NH)
        vml = ar.take(TT * GW).rearrange("p (a n) -> p a n", a=TT)
        qn = chunks(ar.take(2 * T), 2)
        kvn = ar.take(T)
        rt1 = ar.take(2 * T)
        rt2 = ar.take(2 * T)
        std_m = ar.take(T)
        att_area = arena[:, ARENA - (NL + 4) * 384:ARENA]
        att = Arena(ARENA - (NL + 4) * 384)
        Lg = [att.take(384) for _ in range(NL)]
        PTs = [att.take(384) for _ in range(4)]
        assert ar.at <= ARENA - (NL + 4) * 384

        aw = Arena(14 * T)
        rw = chunks(aw.take(14 * T), 14)
        lw = aw.take(T)
        sg = aw.take(T)
        logd = chunks(aw.take(GC * T), GC)
        iclr = chunks(aw.take(GC * T), GC)
        g_ = chunks(aw.take(GC * T), GC)
        cs = chunks(aw.take(GC * T), GC)
        csx = chunks(aw.take(GC * T), GC)
        lx = csx[:, 0, :]
        KR = scratch_b[:, 2048:4096].rearrange("p (c a k t) -> p c a k t", c=GC, a=TT, k=2)
        Bs = chunks(scratch_b[:, 4096:5120], GC)
        Ks = chunks(scratch_b[:, 5120:6144], GC)
        vtok = aw.take(TT * GW).rearrange("p (a n) -> p a n", a=TT)
        Btok = aw.take(GW)
        Ktok = aw.take(GW)
        Sbd = aw.take(GW).rearrange("p (c n) -> p c n", c=GC)
        Xn = scratch_b[:, 6144:6656]
        Ut = scratch_b[:, 6656:7168]
        yT = ycat[:, 0:GC, :]
        k2 = chunks(sq_[:, 0:GC * T], GC)
        bon = chunks(sq_[:, GC * T:2 * GC * T], GC)
        AT_A = arena[:, 0:14 * T]
        E1 = chunks(AT_A[:, 0:GC * T], GC)
        E2 = chunks(AT_A[:, GC * T:2 * GC * T], GC)
        E3 = chunks(AT_A[:, 2 * GC * T:3 * GC * T], GC)
        kk = chunks(scratch_b[:, 0:GC * T], GC)
        kkr = chunks(scratch_b[:, GC * T:2 * GC * T], GC)
        AT0 = arena[:, 14 * T:14 * T + NH * 512]
        AT = AT0.rearrange("p (h q s) -> p h q s", h=NH, q=4)
        Dm = chunks(AT_A[:, 0:NH * P], NH)
        DmT = chunks(AT_A[:, NH * P:2 * NH * P], NH)
        Gm = chunks(AT_A[:, 2 * NH * P:3 * NH * P], NH)
        CTm = [chunks(scratch_b[:, i * NH * P:(i + 1) * NH * P], NH) for i in range(2)]
        omka = tiny[:, 0:GC]
        fend = tiny[:, 8:8 + GC]

        a1 = Arena()
        fq2 = a1.take(2 * GC * T).rearrange("p (q c t) -> p q c t", q=2, c=GC)
        fk = chunks(a1.take(GC * T), GC)
        fv = a1.take(TT * GW).rearrange("p (a n) -> p a n", a=TT)
        mq = chunks(a1.take(GC * T), GC)
        mq2 = a1.take(2 * GC * T).rearrange("p (q c t) -> p q c t", q=2, c=GC)
        mk = chunks(a1.take(GC * T), GC)
        mv = a1.take(TT * GW).rearrange("p (a n) -> p a n", a=TT)
        fz, fe, fl, fd, fnd = [a1.take(T) for _ in range(5)]
        r1a, r1b = att_area[:, 0:2 * T], att_area[:, 2 * T:4 * T]
        am = Arena()
        ttok = am.take(TT * D).rearrange("p (a n) -> p a n", a=TT)
        lg = am.take(TT * E)
        big = am.take(TT * E * E)
        big2 = am.take(TT * E * E)
        rank, selm, ex, comb, posm = [am.take(TT * E) for _ in range(5)]
        cnt = am.take(E)
        table = am.take((2 * E + 1) * 4).rearrange("p (e k) -> p e k", e=2 * E + 1)
        cur = am.take(4)
        m0, den = am.take(TT), am.take(TT)
        mcnt = am.take(2)
        oh = am.take(TT * P).rearrange("p (a s) -> p a s", a=TT)
        ohg = am.take(TT * P).rearrange("p (a s) -> p a s", a=TT)
        ohgT = am.take(T)
        xg = am.take(DC * P).rearrange("p (c s) -> p c s", c=DC)
        ysl = am.take(D)
        sigb = [am.take(2 * T) for _ in range(2)]
        gtmp = [am.take(2 * T) for _ in range(2)]
        hf = [am.take(2 * T) for _ in range(2)]
        assert am.at <= ARENA - 2 * SLOT - 4 * 512
        ah = Arena()
        hq = chunks(ah.take(GC * T), GC)
        hk = chunks(ah.take(GC * T), GC)
        hv = ah.take(TT * GW).rearrange("p (a n) -> p a n", a=TT)
        hq2_ = ah.take(2 * GC * T)
        hq2 = hq2_.rearrange("p (q c t) -> p q c t", q=2, c=GC)
        gsig = chunks(hq2_, DC)
        gate = chunks(ah.take(DC * T), DC)
        bx = chunks(ah.take(2 * T), 2)
        xc = chunks(ah.take(2 * T), 2)
        lr, li, lt = [chunks(ah.take(2 * T), 2) for _ in range(3)]
        la, lu, lq = lr, li, bx
        cq2_ = ah.take(2 * 2 * T)
        cq2 = cq2_.rearrange("p (q c t) -> p q c t", q=2, c=2)
        ck = chunks(ah.take(2 * T), 2)
        cv = ah.take(TT * T).rearrange("p (a n) -> p a n", a=TT)
        hra, hrb = r1a, r1b
        az = Arena()
        zb, zl, zw = [az.take(4 * 384).rearrange("p (h n) -> p h n", h=4) for _ in range(3)]
        assert max(ah.at, a1.at) <= ARENA - (NL + 4) * 384
        lam_t = tiny[:, 16:80]
        nmx = tiny[:, 80:96].rearrange("p (n k) -> p n k", k=2)
        zsum = tiny[:, 96:112].rearrange("p (n k) -> p n k", k=2)
        rz = tiny[:, 112:128].rearrange("p (n k) -> p n k", k=2)

        consumed = {}
        done = {}

        def slot(i):
            return ring[:, (i % RING) * SLOT:(i % RING + 1) * SLOT]

        block = ctx.enter_context(nc.Block())

        @block.sync
        def _(sp):
            sp.dma_start(hT_[:, :], x_dram).then_inc(loaded, 16)
            c_head = const_at["same_head"][0]
            p_head = par_at["wa2"][0]
            sp.dma_start(cst[:, 0:c_head], const_dram[:, 0:c_head]).then_inc(loaded, 16)
            sp.dma_start(par[:, 0:p_head], param_dram[:, 0:p_head]).then_inc(loaded, 16)

            for k in range(RING):
                sp.dma_start(slot(k), w_dram[k]).then_inc(landed[k], 16)
            sp.dma_start(cst[:, c_head:], const_dram[:, c_head:]).then_inc(tables_loaded, 16)
            sp.dma_start(par[:, p_head:], param_dram[:, p_head:]).then_inc(tables_loaded, 16)
            with sp.Fori(1, N_EARLY // RING) as turn:
                for k in range(RING):
                    sp.wait_ge(split[0], turn * RING + (k + 1 - RING))
                    sp.dma_start(slot(k), w_dram[bass.ds(turn * RING + k, 1)].rearrange("o p n -> (o p) n"))\
                      .then_inc(landed[k], 16)
            for n in range(N_EARLY // RING * RING, N_EARLY):
                sp.wait_ge(split[0], n + 1 - RING)
                sp.dma_start(slot(n), w_dram[n]).then_inc(landed[n % RING], 16)
            sp.wait_ge(flag_ready, 1)
            passes = sp.value_load(passes_i[0:1, 0:1], min_val=1, max_val=2)
            with sp.Fori(0, passes) as ps:
                with sp.Fori(0, N_MOE // RING) as turn:
                    for k in range(RING):
                        n = N_EARLY + k
                        sp.wait_ge(split[0], ps * N_MOE + turn * RING + (n + 1 - RING))
                        sp.dma_start(slot(n), w_dram[bass.ds(turn * RING + n, 1)].rearrange("o p n -> (o p) n"))\
                          .then_inc(landed[n % RING], 16)
            for k in range(2):
                n = N_EARLY + k
                sp.wait_ge(split[0], passes * N_MOE + (n + 1 - RING))
                sp.dma_start(slot(n), w_dram[n]).then_inc(landed[n % RING], 16)
            sp.wait_ge(S["moe_end"], 1)
            for n in range(N_LATE):
                if n >= RING:
                    sp.wait_ge(split[1], n + 1 - RING)
                sp.dma_start(slot(n), w_dram[W_LATE + n]).then_inc(late_landed[n % RING], 16)
            sp.wait_ge(S["out_ready"], 1)
            sp.dma_start(out_dram, uT_[:, :]).then_inc(stored, 16)
            sp.wait_ge(stored, 16)

        @block.tensor
        def _(pe):
            wn = [0, 0]

            def mm(out, lhsT, rhs, start=True, stop=True):
                return pe.matmul(out, lhsT, rhs, start=start, stop=stop, skip_group_check=True)

            def mm3(out, lhs, rhs, start, stop):
                mm(out, lhs[0], rhs[0], start=start, stop=False)
                mm(out, lhs[0], rhs[1], start=False, stop=False)
                return mm(out, lhs[1], rhs[0], start=False, stop=stop)

            def tr(out, in_):
                return pe.transpose(out, in_, C("ident"))

            def parts(n, bufs, inner):
                return [x[n % bufs][:, :].rearrange("p (c n) -> p c n", c=inner) for x in (whi, wlo)]

            halves = [0, 0]

            def operand_split():
                halves[0] += 2
                halves[1] += 1
                pe.wait_ge(S["act_lo"], halves[1])

            def second_half(c):
                if c == DC // 2 and halves[1] < halves[0]:
                    halves[1] += 1
                    pe.wait_ge(S["act_lo"], halves[1])

            def project(ch, late=0):
                n = wn[late]
                pe.wait_ge(split[late], n + 1)
                h, l = parts(n, 2, DC)
                bank = ch.claim(pe)[:, :].rearrange("p (j t) -> p j t", j=2)
                for j in range(2):
                    cols = slice(j * P, (j + 1) * P)
                    for c in range(DC):
                        second_half(c)
                        last = mm3(bank[:, j, :], (h[:, c, cols], l[:, c, cols]), (uhi[:, c, :], ulo[:, c, :]), c == 0, c == DC - 1)
                consumed[late, n] = (ch.filled, ch.fill(last))
                wn[late] += 1

            def project_tok(ch, late=0):
                n = wn[late]
                pe.wait_ge(split[late], n + 1)
                h, l = parts(n, 2, DC)
                bank = ch.claim(pe)[:, :].rearrange("p (a n) -> p a n", a=TT)
                for a in range(TT):
                    rows = slice(a * P, (a + 1) * P)
                    for c in range(DC):
                        second_half(c)
                        last = mm3(bank[:, a, :], (uhi[:, c, rows], ulo[:, c, rows]), (h[:, c, :], l[:, c, :]), c == 0, c == DC - 1)
                consumed[late, n] = (ch.filled, ch.fill(last))
                wn[late] += 1


            def norm(k):
                bank = A.claim(pe)
                for c in range(DC):
                    if c % 4 == 0:
                        pe.wait_ge(S["squares_ready"], 2 * k + c // 4 + 1)
                    last = mm(bank[:, 0:T], C("ones"), sq[:, c, :], start=(c == 0), stop=(c == DC - 1))
                A.fill(last)

            def attention(scores, v, n0):
                prob = {}
                for i in range(NH + LAG + 2):
                    if i < NH:
                        bank = V.claim(pe)
                        V.fill(scores(i, bank))
                    h = i - LAG
                    if 0 <= h < NH:
                        pe.wait_ge(S["prob_ready"], n0 + h + 1)
                        bank = A.claim(pe)
                        for lo in (0, P, 2 * P):
                            last = tr(bank[:, lo:lo + P], Lg[h % NL][:, lo:lo + P])
                        prob[h] = A.fill(last)
                    if h >= 2 and h % 2 == 0:
                        bank = V.claim(pe)
                        pe.wait_ge(A.freed, prob[h - 1])
                        for g in (h - 2, h - 1):
                            o = bank[HD * (g % 2):HD * (g % 2) + HD, :]
                            mm(o[:, 0:T], v[:, 0, g * HD:(g + 1) * HD], PTs[g % 4][:, 0:T], stop=False)
                            last = mm(o[:, P:T], v[:, 1, g * HD:(g + 1) * HD], PTs[g % 4][:, T:T + P], start=False)
                        V.fill(last)

            def head_scores(q2, k):
                def go(h, bank):
                    q = q2[:, h % 2, h // 2, :]
                    mm(bank[:, 0:P], q[:, 0:P], k[:, h // 2, 0:P])
                    return mm(bank[:, P:P + T], q[:, P:T], k[:, h // 2, :])
                return go

            def rope(x, n, which):
                for c in range(0, n, 2):
                    bank = V.claim(pe)
                    V.fill(mm(bank[:, :], C(f"partner_{which}"), x[:, c:c + 2, :]))

            pe.wait_ge(loaded, 48)
            norm(0)
            operand_split()
            for _ in range(N_IN0):
                project(A)

            pe.wait_ge(tables_loaded, 32)
            bank = A.claim(pe)
            pe.wait_ge(S["mla_sq"], 1)
            for c in range(2):
                mm(bank[:, 0:T], C("ones"), sq[:, c, :], start=(c == 0), stop=(c == 1))
            A.fill(mm(bank[:, T:2 * T], C("ones"), sq[:, 2, :]))
            pe.wait_ge(S["mla_q"], 1)
            wuq = Pm("wuq").rearrange("p (k n) -> p k n", k=2)
            for j2 in range(NH // 2):
                bank = A.claim(pe)
                for j in range(2):
                    for c in range(2):
                        cc = (2 * j2 + j) * P
                        last = mm(bank[:, j * T:(j + 1) * T], wuq[:, c, cc:cc + P], qn[:, c, :], start=(c == 0), stop=(c == 1))
                A.fill(last)
            wukv = Pm("wukv")
            pe.wait_ge(S["mla_kv"], 1)
            for a in range(TT):
                bank = A.claim(pe)
                A.fill(mm(bank[:, :], kvn[:, a * P:(a + 1) * P], wukv[:, NH * P:NH * P + GW]))
            bank = V.claim(pe)
            V.fill(mm(bank[:, 0:T], C("partner_mla"), kpe))
            for j2 in range(NH // 2):
                bank = V.claim(pe)
                for j in range(2):
                    cc = (2 * j2 + j) * P
                    last = mm(bank[:, j * T:(j + 1) * T], wukv[:, cc:cc + P], kvn)
                V.fill(last)
            pe.wait_ge(A.freed, A.np)
            rope(qh, NH, "mla")
            pe.wait_ge(S["rope_done"], 1 + NH // 2)

            def mla_scores(h, bank):
                mm(bank[:, 0:P], qh[:, h, 0:P], kh[:, h, 0:P])
                return mm(bank[:, P:P + T], qh[:, h, P:T], kh[:, h, :])

            attention(mla_scores, vml, 0)

            pe.wait_ge(S["lora_in"], 2)
            for w, x in ((Pm("wa2"), lw), (Pm("wa2"), lx), (Pm("g2"), sg)):
                for j2 in range(2):
                    bank = A.claim(pe)
                    for j in range(2):
                        cc = (2 * j2 + j) * P
                        last = mm(bank[:, j * T:(j + 1) * T], w[:, cc:cc + P], x)
                    A.fill(last)
            pe.wait_ge(S["kk_sq"], 1)
            for j2 in range(2):
                bank = A.claim(pe)
                A.fill(mm(bank[:, 0:512], C("same_head"), sq_[:, j2 * 512:(j2 + 1) * 512]))
            pe.wait_ge(S["bonus_in"], 1)
            for j2 in range(2):
                bank = V.claim(pe)
                V.fill(mm(bank[:, 0:512], C("same_head"), sq_[:, 1024 + j2 * 512:1024 + (j2 + 1) * 512]))
            for a in range(TT):
                bank = A.claim(pe)
                for c in range(GC):
                    last = tr(bank[:, c * P:(c + 1) * P], rw[:, 8 + c, a * P:(a + 1) * P])
                A.fill(last)
            pe.wait_ge(S["keys_ready"], 1)
            for src in (Bs, Ks):
                bank = A.claim(pe)
                for c in range(GC):
                    last = tr(bank[:, c * P:(c + 1) * P], src[:, c, 0:P])
                A.fill(last)

            for a in range(TT):
                lo, hi = a * P, (a + 1) * P
                for h in range(NH):
                    c, b = h // 2, HD * (h % 2)
                    bank = V.claim(pe)
                    kr = KR[b:b + HD, c, a].rearrange("p k t -> p (k t)")
                    mm(bank[:, 0:T], Bs[b:b + HD, c, lo:hi], kr)
                    V.fill(mm(bank[:, T:2 * T], Ks[b:b + HD, c, lo:hi], kr))
                for par_ in range(2):
                    bank = V.claim(pe)
                    for h in range(par_, NH, 2):
                        c, b = h // 2, HD * par_
                        last = mm(bank[:, c * P:(c + 1) * P], KR[b:b + HD, c, a, 0, :], Bs[b:b + HD, c, lo:hi])
                    V.fill(last)
                dj = [V.np, V.np]
                for n, m in enumerate(LEVELS):
                    pe.wait_ge(S["level_ct"], a * len(LEVELS) + n + 1)
                    gj = []
                    for h4 in range(2):
                        pe.wait_ge(V.freed, dj[h4])
                        bank = A.claim(pe)
                        for h in range(4 * h4, 4 * h4 + 4):
                            last = mm(bank[:, (h % 4) * P:(h % 4 + 1) * P], CTm[n % 2][:, h, :], Dm[:, h, :])
                        gj.append(A.fill(last))
                    for h4 in range(2):
                        pe.wait_ge(A.freed, gj[h4])
                        if m != LEVELS[-1]:
                            bank = V.claim(pe)
                            for h in range(4 * h4, 4 * h4 + 4):
                                last = mm(bank[:, (h % 4) * P:(h % 4 + 1) * P], DmT[:, h, :], Gm[:, h, :])
                            V.fill(last)
                        bank = V.claim(pe)
                        for h in range(4 * h4, 4 * h4 + 4):
                            last = mm(bank[:, (h % 4) * P:(h % 4 + 1) * P], Gm[:, h, :], DmT[:, h, :])
                        dj[h4] = V.fill(last)
                bank = A.claim(pe)
                for c in range(GC):
                    if a:
                        mm(bank[:, c * P:(c + 1) * P], KR[:, c, a, 0, :], Sbd[:, c, :], stop=False)
                    for h in (2 * c, 2 * c + 1):
                        last = mm(bank[:, h * HD:(h + 1) * HD], AT[:, h, 2, :], vtok[:, a, h * HD:(h + 1) * HD],
                                  start=not a)
                nx = A.fill(last)
                pe.wait_ge(A.freed, nx)
                pe.wait_ge(V.freed, V.np)
                bank = A.claim(pe)
                for h in range(NH):
                    last = mm(bank[:, h * HD:(h + 1) * HD], DmT[:, h, :], Xn[:, h * HD:(h + 1) * HD])
                nu = A.fill(last)
                pe.wait_ge(A.freed, nu)
                bank = A.claim(pe)
                for c in range(GC):
                    if a:
                        mm(bank[:, c * P:(c + 1) * P], Sbd[:, c, :], KR[:, c, a, 1, :], stop=False)
                    for h in (2 * c, 2 * c + 1):
                        o = bank[HD * (h % 2):HD * (h % 2) + HD, c * P:(c + 1) * P]
                        mm(o, Ut[:, h * HD:(h + 1) * HD], AT[:, h, 1, :], start=not a, stop=False)
                        last = mm(o, vtok[:, a, h * HD:(h + 1) * HD], AT[:, h, 3, :], start=False)
                A.fill(last)
                if a == 0:
                    bank = V.claim(pe)
                    for c in range(GC):
                        mm(bank[:, c * P:(c + 1) * P], Btok[:, c * P:(c + 1) * P], Ut[:, c * P:(c + 1) * P], stop=False)
                        last = mm(bank[:, c * P:(c + 1) * P], Ktok[:, c * P:(c + 1) * P], vtok[:, 0, c * P:(c + 1) * P], start=False)
                    V.fill(last)
                    pe.wait_ge(S["state_ready"], 1)
            pe.wait_ge(A.freed, A.np)
            for j2 in range(2):
                bank = V.claim(pe)
                V.fill(mm(bank[:, :], C("same_head"), yT[:, 2 * j2:2 * j2 + 2, :]))
            pe.wait_ge(S["gn_sq"], 1)
            for j2 in range(2):
                bank = A.claim(pe)
                A.fill(mm(bank[:, :], C("same_head"), sq_[:, j2 * 512:(j2 + 1) * 512]))

            def out_projection(k, late=0):
                operand_split()
                for _ in range(N_OUT):
                    project(V, late)

            out_projection(0)

            norm(1)
            operand_split()
            pe.wait_ge(A.freed, A.np)
            pe.wait_ge(V.freed, V.np)
            for b in range(4, 8):
                last = mm(banks[b][:, :], zero16[:, :], zero16[:, 0:1].broadcast_to([P, 512]), stop=False)
            last.then_inc(S["ffn_down"], 1)

            def ffn_gu(k, ahead, step):
                for g in range(2):
                    n = k + g
                    pe.wait_ge(split[0], ahead + (n + 1))
                    h, l = parts(n, 2, DC)
                    bank = banks[2 * g + step % 2]
                    for j in range(2):
                        cols = slice(j * P, (j + 1) * P)
                        for c in range(DC):
                            second_half(c)
                            last = mm3(bank[:, j * T:(j + 1) * T], (h[:, c, cols], l[:, c, cols]), (uhi[:, c, :], ulo[:, c, :]),
                                       c == 0, c == DC - 1)
                    last.then_inc(S["ffn_gate" if g == 0 else "ffn_gu"], 1)

            def ffn_down(k, ahead, step):
                pe.wait_ge(split[0], ahead + (k + 1))
                h, l = parts(k, 2, 2)
                hh, hl = chunks(hhi[step % 2][:, :], 2), chunks(hlo[step % 2][:, :], 2)
                for f in range(2):
                    for c in range(DC):
                        cols = slice(c * P, (c + 1) * P)
                        last = mm3(banks[4 + c // 2][:, (c % 2) * T:(c % 2 + 1) * T], (h[:, f, cols], l[:, f, cols]),
                                   (hh[:, f, :], hl[:, f, :]), False, False)
                last.then_inc(S["ffn_down"], 1)

            w0 = wn[0]
            ffn_gu(w0, 0, 0)
            with pe.Fori(0, (FFN_STEPS - 1) // 2) as it:
                for s in range(2):
                    k = w0 + 2 + 3 * s
                    ffn_gu(k, it * 6, 1 + s)
                    pe.wait_ge(S["ffn_hid"], it * 2 + (s + 1))
                    ffn_down(k + 2, it * 6, s)
            wn[0] += N_FFN
            pe.wait_ge(S["ffn_hid"], FFN_STEPS)
            ffn_down(wn[0] - 1, 0, 0)
            consumed[0, wn[0] - 2] = (S["ffn_down"], FFN_STEPS)
            consumed[0, wn[0] - 1] = (S["ffn_down"], FFN_STEPS + 1)

            norm(2)
            pe.wait_ge(S["u_ready"], 3)
            bank = V.claim(pe)
            wf = Pm("wf").rearrange("p (c n) -> p c n", c=DC)
            for c in range(DC):
                last = mm(bank[0:NH, 0:T], wf[:, c, :], uT[:, c, :], start=(c == 0), stop=(c == DC - 1))
            V.fill(last)
            operand_split()
            for which in "qkvQKV":
                for _ in range(2):
                    if which in "vV":
                        project_tok(A)
                    else:
                        project(A)
            pe.wait_ge(A.freed, A.np)
            rope(mq, GC, "full")
            rope(mk, GC, "full")
            pe.wait_ge(S["fox_d"], 1)
            pick = C("pick8")

            def fox_scores(h, bank):
                q = fq2[:, h % 2, h // 2, :]
                for lo, q0, nk in ((0, 0, P), (P, P, T)):
                    o = bank[:, lo:lo + nk]
                    mm(o, q[:, q0:q0 + P], fk[:, h // 2, 0:nk], stop=False)
                    last = mm(o, pick[:, h:h + 1].broadcast_to([P, P]), fnd[:, 0:nk], start=False)
                return last

            attention(fox_scores, fv, NH)
            pe.wait_ge(S["rope_done"], 1 + NH // 2 + GC)
            attention(head_scores(mq2, mk), mv, 2 * NH)
            out_projection(1)

            norm(3)
            pe.wait_ge(S["u_ready"], 4)
            bank = V.claim(pe)
            rw_ = Pm("router").rearrange("p (c n) -> p c n", c=DC)
            for a in range(TT):
                for c in range(DC):
                    last = mm(bank[:, a * E:(a + 1) * E], uT[:, c, a * P:(a + 1) * P], rw_[:, c, :],
                              start=(c == 0), stop=(c == DC - 1))
            V.fill(last)
            for a in range(TT):
                for c4 in range(2):
                    bank = A.claim(pe)
                    for c in range(4):
                        last = tr(bank[:, c * P:(c + 1) * P], uT[:, 4 * c4 + c, a * P:(a + 1) * P])
                    A.fill(last)
            pe.wait_ge(S["router_sel"], 1)
            bank = V.claim(pe)
            mm(bank[:, 0:E], C("mask4")[:, 0:P], selm[:, 0:E])
            mm(bank[:, E:2 * E], C("ones"), selm[:, 0:E], stop=False)
            mm(bank[:, E:2 * E], C("mask4")[:, 0:P], selm[:, E:2 * E], start=False)
            mm(bank[:, 2 * E:3 * E], C("ones"), selm[:, 0:E], stop=False)
            V.fill(mm(bank[:, 2 * E:3 * E], C("ones"), selm[:, E:2 * E], start=False))
            pe.wait_ge(A.freed, A.np)
            pe.wait_ge(V.freed, V.np)
            pe.wait_ge(flag_ready, 1)
            passes = pe.value_load(passes_i[0:1, 0:1], min_val=1, max_val=2)

            def moe_up(k, ahead, half, g):
                pe.wait_ge(split[0], ahead + (k + 1))
                h, l = parts(k, 3, DC)
                for c in range(DC):
                    last = mm3(banks[half][:, g * T:(g + 1) * T], (xhi[:, c, :], xlo[:, c, :]), (h[:, c, :], l[:, c, :]),
                               c == 0, c == DC - 1)
                if g:
                    last.then_inc(S["moe_gu"], 1)

            def moe_turn(count, half):
                pe.wait_ge(S["moe_h"], count)
                for f in range(2):
                    last = tr(banks[3][:, f * P:(f + 1) * P], hf[half][:, f * P:(f + 1) * P])
                last.then_inc(S["moe_tr"], 1)

            def moe_down(k, ahead, count, half):
                pe.wait_ge(S["moe_hid"], count)
                pe.wait_ge(split[0], ahead + (k + 1))
                h, l = parts(k, 3, 2)
                for f in range(2):
                    rows = slice(f * P, (f + 1) * P)
                    for o in range(2):
                        cols = slice(o * 512, (o + 1) * 512)
                        last = mm3(banks[4 + o][:, :], (hhi[half][:, rows], hlo[half][:, rows]), (h[:, f, cols], l[:, f, cols]),
                                   False, False)
                last.then_inc(S["moe_down"], 1)

            mm(banks[4][:, :], zero16[:, :], zero16[:, 0:1].broadcast_to([P, 512])).then_inc(S["moe_down"], 1)

            def gather(count):
                pe.wait_ge(S["onehot"], count)
                for c4 in range(2):
                    for c in range(4):
                        for a in range(TT):
                            cc = 4 * c4 + c
                            last = mm(banks[6 + c4][:, c * P:(c + 1) * P], ttok[:, a, cc * P:(cc + 1) * P], oh[:, a, :],
                                      start=(a == 0), stop=(a == 1))
                last.then_inc(S["moe_g"], 1)

            def open_outputs():
                for o in range(2):
                    mm(banks[4 + o][:, :], zero16[:, :], zero16[:, 0:1].broadcast_to([P, 512]), stop=False)

            gather(1)
            open_outputs()
            with pe.Fori(0, passes) as ps:
                with pe.Fori(0, E) as e:
                    ex_n = pe.snap(ps * E + e)
                    pe.wait_ge(S["moe_x"], ex_n + 1)
                    slots_n = pe.snap(ex_n * MOE_SLOTS)
                    steps_n = pe.snap(ex_n * MOE_STEPS)
                    k0 = N_EARLY
                    moe_up(k0, slots_n, 0, 0)
                    moe_up(k0 + 1, slots_n, 0, 1)

                    def step(k, slots_, steps_, s):
                        moe_up(k, slots_, (s + 1) % 2, 0)
                        moe_turn(steps_ + (s + 1), s % 2)
                        moe_up(k + 1, slots_, (s + 1) % 2, 1)
                        moe_down(k + 2, slots_, steps_ + (s + 1), s % 2)

                    with pe.Fori(0, (MOE_STEPS - 2) // 2) as it:
                        slots_i = pe.snap(slots_n + it * 6)
                        steps_i = pe.snap(steps_n + it * 2)
                        for s in range(2):
                            step(k0 + 2 + 3 * s, slots_i, steps_i, s)
                    s = MOE_STEPS - 2
                    step(k0 + 2 + 3 * s, slots_n, steps_n, s)
                    moe_turn(steps_n + MOE_STEPS, 1)
                    gather(ex_n + 2)
                    pe.wait_ge(S["onehot_g"], ex_n + 1)
                    for a in range(TT):
                        last = tr(banks[2][:, a * P:(a + 1) * P], ohg[:, a, :])
                    last.then_inc(S["moe_gt"], 1)
                    moe_down(k0 + MOE_SLOTS - 1, slots_n, steps_n + MOE_STEPS, 1)
                    pe.wait_ge(S["moe_ytok"], ex_n + 1)
                    for c2 in range(4):
                        bank = banks[c2]
                        for c in range(2):
                            cc = 2 * c2 + c
                            last = mm(bank[:, c * T:(c + 1) * T], ysl[:, cc * P:(cc + 1) * P], ohgT)
                        last.then_inc(S["moe_sc"], 1)
                    open_outputs()
                    pe.wait_ge(S["moe_add"], ex_n * 4 + 2)
            pe.wait_ge(S["moe_end"], 1)

            norm(4)
            for l in range(2):
                norm(5 + l)
                operand_split()
                for kind in ("q", "q", "k", "k", "v", "v", "g", "g", "x", "g", "q", "k", "v", "g"):
                    if kind == "v":
                        project_tok(A, 1)
                    else:
                        project(A, 1)
                pe.wait_ge(A.freed, A.np)
                rope(hq, GC, "part")
                rope(hk, GC, "part")
                pe.wait_ge(S["conv_done"], l + 1)
                for w in (Pm("gaw"), Pm("gxw")):
                    bank = A.claim(pe)
                    for c in range(2):
                        last = mm(bank[:, c * T:(c + 1) * T], w[:, (2 * l + c) * P:(2 * l + c + 1) * P], xc[:, c, :])
                    A.fill(last)
                pe.wait_ge(S["rope_done"], 1 + NH // 2 + GC * (2 + l))
                attention(head_scores(hq2, hk), hv, (3 + l) * NH)
                for h in range(4):
                    q, k = cq2[:, h % 2, h // 2, :], ck[:, h // 2, :]
                    bank = V.claim(pe)
                    mm(bank[:, 0:T], k[:, 0:P], q)
                    V.fill(mm(bank[:, T:T + P], k[:, P:T], q[:, P:T]))
                pe.wait_ge(S["stick_n"], l + 1)
                for h in range(4):
                    bank = V.claim(pe)
                    mm(bank[:, 0:T], C("neg_tail"), zl[:, h, 0:T], stop=False)
                    mm(bank[:, P:T], C("neg_ones"), zl[:, h, T:T + P], start=False)
                    V.fill(mm(bank[:, T:T + P], C("neg_tail"), zl[:, h, T:T + P]))
                pe.wait_ge(S["stick_w"], l + 1)
                for c in range(2):
                    bank = V.claim(pe)
                    for h in (2 * c, 2 * c + 1):
                        o = bank[HD * (h % 2):HD * (h % 2) + HD, :]
                        mm(o[:, 0:T], cv[:, 0, h * HD:(h + 1) * HD], zw[:, h, 0:T], stop=False)
                        last = mm(o[:, P:T], cv[:, 1, h * HD:(h + 1) * HD], zw[:, h, T:T + P], start=False)
                    V.fill(last)
                out_projection(2 + l, 1)
            norm(7)

        @block.scalar
        def _(act):
            st = Step(act, sem("scalar_step"))

            def a_(out, in_, f, **kw):
                return act.activation(out, in_, f, **kw)

            def evac(dst, width=512):
                bank = A.take(act)
                A.free(a_(dst, bank[:, 0:width], ACT.Copy))

            def hi(n, late=0):
                lands = late_landed if late else landed
                act.wait_ge(lands[n % RING], 16 * (n // RING + 1))
                if n >= 2:
                    act.wait_ge(*consumed[late, n - 2])
                a_(whi[n % 2][:, :], slot(n), ACT.Copy).then_inc(high[late], 1)

            def operand_hi(src, norm_k=None):
                for half, ready in enumerate(("u_half", "u_ready")):
                    if norm_k is not None:
                        act.wait_ge(S[ready], norm_k + 1)
                    cols = slice(half * 4 * T, (half + 1) * 4 * T)
                    st.say(a_(uhi_[:, cols], src[:, cols], ACT.Copy), "act_hi")

            def split_heads(q2):
                bank = A.take(act)
                b3 = bank[:, :].rearrange("p (c t) -> p c t", c=2)
                st.lone(a_(q2[0:HD, 0], b3[0:HD], ACT.Copy))
                A.free(a_(q2[HD:P, 1], b3[HD:P], ACT.Copy))

            def norm(k, h_done):
                if h_done:
                    act.wait_ge(S["h_ready"], h_done)
                for c4 in range(2):
                    st.say(a_(sq[:, 4 * c4:4 * c4 + 4, :], hT[:, 4 * c4:4 * c4 + 4, :], ACT.Square), "squares_ready")
                bank = A.take(act)
                A.free(a_(rstd(), bank[:, 0:T], ACT.Sqrt, scale=1.0 / D, bias=epscol))
                done["norm", k] = A.nc

            def rstd():
                return yc_[:, 0:T]

            epscol = tiny[:, 130:131]
            gncol = tiny[:, 131:132]
            onecol = tiny[:, 132:133]
            zcol = tiny[:, 133:134]
            act.wait_ge(S["zero_ready"], 1)

            def attention(n0):
                done["attention", n0] = A.nc
                for i in range(NH + LAG):
                    if i >= LAG:
                        evac(PTs[(i - LAG) % 4], 384)
                    if i < NH:
                        n = n0 + i
                        act.wait_ge(S["nmax_ready"], n + 1)
                        st.lone(a_(Lg[i % NL][:, 0:P], Lg[i % NL][:, 0:P], ACT.Exp, bias=nmx[:, i, 0:1], accum_out=zsum[:, i, 0:1]))
                        st.say(a_(Lg[i % NL][:, P:384], Lg[i % NL][:, P:384], ACT.Exp, bias=nmx[:, i, 1:2], accum_out=zsum[:, i, 1:2]), "exp_done")

            hi(0)
            hi(1)
            act.wait_ge(loaded, 48)
            norm(0, 0)
            operand_hi(uT_, 0)
            for n in range(7):
                evac(raw[:, 2 * n:2 * n + 2, :])
                hi(n + 2)
            evac(qlat)
            bank = A.take(act)
            st.lone(a_(kvl, bank[:, 0:T], ACT.Copy))
            A.free(a_(kpe, bank[:, T:2 * T], ACT.Copy))
            st.settle()
            act.wait_ge(tables_loaded, 32)
            act.wait_ge(A.freed, A.nc)
            st.lone(a_(sq[:, 0:2, :], qlat, ACT.Square))
            st.say(a_(sq[:, 2, :], kvl, ACT.Square), "mla_sq")
            bank = A.take(act)
            st.say(a_(std_m, bank[:, 0:T], ACT.Sqrt, scale=1.0 / 256, bias=epscol), "mla_std")
            A.free(a_(rt1[:, 0:T], bank[:, T:2 * T], ACT.Sqrt, scale=1.0 / 128, bias=epscol))
            done["mla_std"] = A.nc
            for j2 in range(NH // 2):
                evac(qh[:, 2 * j2:2 * j2 + 2, :])
            for a in range(TT):
                evac(vml[:, a, :])
            done["mla"] = A.nc
            attention(0)

            act.wait_ge(S["decay_in"], 1)
            st.say(a_(lw[0:HD], rw[0:HD, 12, :], ACT.Tanh), "lora_in")
            st.lone(a_(lx[HD:P], rw[HD:P, 12, :], ACT.Copy))
            st.settle()
            st.say(a_(sg, rw[:, 13, :], ACT.Sigmoid), "lora_in")
            for dst, bias in ((logd, "w0"), (iclr, "a0"), (g_, None)):
                for j2 in range(2):
                    bank = A.take(act)
                    for j in range(2):
                        c = 2 * j2 + j
                        if bias:
                            ins = a_(dst[:, c, :], bank[:, j * T:(j + 1) * T], ACT.Sigmoid, bias=col(bias, c))
                        else:
                            ins = a_(dst[:, c, :], bank[:, j * T:(j + 1) * T], ACT.Copy)
                        if j:
                            A.free(ins)
                        else:
                            st.lone(ins)
            st.settle()
            done["lora"] = A.nc
            act.wait_ge(S["kk_in"], 1)
            st.say(a_(sq_[:, 0:1024], kkr, ACT.Square), "kk_sq")
            for j2 in range(2):
                bank = A.take(act)
                A.free(a_(kk[:, 2 * j2:2 * j2 + 2, :], bank[:, :], ACT.Sqrt))
            done["kk"] = A.nc
            act.wait_ge(S["exp_in"], 1)
            st.lone(a_(E1, cs, ACT.Exp))
            st.lone(a_(E2, csx, ACT.Exp))
            st.lone(a_(E3, cs, ACT.Exp, scale=-1.0))
            st.settle()
            act.wait_ge(S["exp_in"], 2)
            st.say(a_(fend, tiny[:, 140:140 + GC], ACT.Exp), "exp_out")
            for a in range(TT):
                evac(vtok[:, a, :])
            evac(Btok)
            evac(Ktok)
            for a in range(TT):
                done["levels", a] = A.nc
                for m in LEVELS:
                    for h4 in range(2):
                        evac(Gm[:, 4 * h4:4 * h4 + 4, :])
                bank = A.take(act)
                A.free(a_(Xn, bank[:, :], ACT.Copy, scale=-1.0))
                evac(Ut)
                bank = A.take(act)
                A.free(a_(yT[:, :, a * P:(a + 1) * P], bank[:, :].rearrange("p (c t) -> p c t", c=GC), ACT.Copy))
                done["y", a] = A.nc
            act.wait_ge(S["gn_in"], 1)
            st.say(a_(sq_[:, 0:1024], yT, ACT.Square), "gn_sq")
            for j2 in range(2):
                bank = A.take(act)
                A.free(a_(cs[:, 2 * j2:2 * j2 + 2, :], bank[:, :], ACT.Sqrt, scale=1.0 / HD, bias=gncol))
            done["gn"] = A.nc

            n = N_IN0
            hi(n)
            hi(n + 1)
            act.wait_ge(S["y_ready"], 1)
            operand_hi(yc_)
            for n in range(N_IN0 + 2, N_IN0 + N_OUT + 2):
                hi(n)
            norm(1, 1)
            operand_hi(uT_, 1)

            def loop_hi(k, turns, bufs):
                act.wait_ge(landed[k % RING], turns * 16 + 16 * (k // RING + 1))
                a_(whi[k % bufs][:, :], slot(k), ACT.Copy).then_inc(high[0], 1)

            w0 = N_IN0 + N_OUT
            with act.Fori(0, FFN_STEPS // 2) as it:
                for s in range(2):
                    act.wait_ge(S["ffn_gu"], it * 2 + (s + 1))
                    loop_hi(w0 + 2 + 3 * s, it * 2, 2)
                    a_(sigb[s], banks[s][:, :], ACT.Sigmoid).then_inc(S["ffn_sig"], 1)
                    act.wait_ge(S["ffn_down"], it * 2 + (s + 1))
                    loop_hi(w0 + 3 + 3 * s, it * 2, 2)
                    act.wait_ge(S["ffn_gate"], it * 2 + (s + 2))
                    loop_hi(w0 + 4 + 3 * s, it * 2, 2)
            act.wait_ge(S["ffn_gu"], FFN_STEPS)
            a_(sigb[0], banks[0][:, :], ACT.Sigmoid).then_inc(S["ffn_sig"], 1)
            w1 = w0 + N_FFN
            loop_hi(w1 - 1, 0, 2)
            hi(w1)
            hi(w1 + 1)

            norm(2, 2)
            operand_hi(uT_, 2)
            for i, dst in enumerate((fq2, fk, fv, mq, mk, mv)):
                for n in range(2):
                    if dst is fq2:
                        split_heads(fq2[:, :, 2 * n:2 * n + 2, :])
                    elif dst is fv or dst is mv:
                        bank = A.take(act)
                        A.free(a_(dst[:, :, n * T:(n + 1) * T], bank[:, :].rearrange("p (a n) -> p a n", a=TT), ACT.Copy))
                    else:
                        evac(dst[:, 2 * n:2 * n + 2, :])
                    hi(w1 + 2 + 2 * i + n)
            done["l1"] = A.nc
            act.wait_ge(S["fox_z"], 1)
            st.own(a_(fe[0:NH], fl[0:NH], ACT.Exp, scale=-1.0))
            st.say(a_(fe[0:NH], fe[0:NH], ACT.Ln, bias=tiny[0:NH, 132:133]), "fox_e")
            attention(NH)
            attention(2 * NH)

            act.wait_ge(S["y_ready"], 2)
            operand_hi(yc_)
            hi(N_EARLY - 2)
            hi(N_EARLY - 1)
            norm(3, 3)
            for a in range(TT):
                for c4 in range(2):
                    evac(ttok[:, a, c4 * 512:(c4 + 1) * 512])
            act.wait_ge(S["router_l"], 1)
            st.say(a_(ex, ex, ACT.Exp), "router_e")
            act.wait_ge(flag_ready, 1)
            passes = act.value_load(passes_i[0:1, 0:1], min_val=1, max_val=2)
            k0 = N_EARLY

            def gathered(count):
                act.wait_ge(S["moe_g"], count)
                a_(uhi_[:, 0:512], banks[6][:, :], ACT.Copy).then_inc(S["moe_act"], 1)
                a_(uhi_[:, 512:1024], banks[7][:, :], ACT.Copy).then_inc(S["moe_xh"], 1)

            act.wait_ge(S["moe_down"], 1)
            loop_hi(k0, 0, 3)
            loop_hi(k0 + 1, 0, 3)
            gathered(1)
            with act.Fori(0, passes) as ps:
                with act.Fori(0, E) as e:
                    ex_n = act.snap(ps * E + e)
                    slots_t = act.snap(ex_n * (MOE_SLOTS // RING))
                    steps_n = act.snap(ex_n * MOE_STEPS)
                    act.wait_ge(S["moe_down"], steps_n + 1)
                    loop_hi(k0 + 2, slots_t, 3)

                    def step(k, turns, steps_, s, ahead):
                        act.wait_ge(S["moe_gu"], steps_ + (s + 1))
                        a_(sigb[s % 2][:, 0:T], banks[s % 2][:, 0:T], ACT.Sigmoid).then_inc(S["moe_sig"], 1)
                        loop_hi(k, turns, 3)
                        act.wait_ge(S["moe_down"], steps_ + (s + 1))
                        loop_hi(k + 1, turns, 3)
                        act.wait_ge(S["moe_tr"], steps_ + (s + 1))
                        a_(hhi[s % 2][:, 0:T], banks[3][:, 0:T], ACT.Copy).then_inc(S["moe_hh"], 1)
                        if ahead:
                            loop_hi(k + 2, turns, 3)

                    with act.Fori(0, (MOE_STEPS - 2) // 2) as it:
                        turns_i = act.snap(slots_t + it * 2)
                        steps_i = act.snap(steps_n + it * 2)
                        for s in range(2):
                            step(k0 + 3 + 3 * s, turns_i, steps_i, s, True)
                    step(k0 + MOE_SLOTS - 3, slots_t, steps_n, MOE_STEPS - 2, False)
                    act.wait_ge(S["moe_gu"], steps_n + MOE_STEPS)
                    a_(sigb[1][:, 0:T], banks[1][:, 0:T], ACT.Sigmoid).then_inc(S["moe_sig"], 1)
                    loop_hi(k0 + MOE_SLOTS - 1, slots_t, 3)
                    loop_hi(k0 + MOE_SLOTS, slots_t, 3)
                    act.wait_ge(S["moe_tr"], steps_n + MOE_STEPS)
                    a_(hhi[1][:, 0:T], banks[3][:, 0:T], ACT.Copy).then_inc(S["moe_hh"], 1)
                    gathered(ex_n + 2)
                    act.wait_ge(S["moe_down"], steps_n + MOE_STEPS)
                    loop_hi(k0 + MOE_SLOTS + 1, slots_t, 3)
                    act.wait_ge(S["moe_gt"], ex_n + 1)
                    a_(ohgT, banks[2][:, 0:T], ACT.Copy).then_inc(S["moe_act"], 1)
                    act.wait_ge(S["moe_down"], steps_n + (MOE_STEPS + 1))
                    a_(ysl[:, 0:512], banks[4][:, :], ACT.Copy).then_inc(S["moe_act"], 1)
                    a_(ysl[:, 512:1024], banks[5][:, :], ACT.Copy).then_inc(S["moe_ytok"], 1)

            hi(0, 1)
            hi(1, 1)
            norm(4, 4)
            for l in range(2):
                norm(5 + l, 5 + l)
                operand_hi(uT_, 5 + l)
                wl = l * (N_IN2 + N_OUT)
                for i, (dst, n) in enumerate(((hq, 0), (hq, 2), (hk, 0), (hk, 2), (hv, 0), (hv, 1), (gate, 0), (gate, 2),
                               (bx, 0), (gate, 4), (cq2, 0), (ck, 0), (cv, 0), (gate, 6))):
                    if dst is cq2:
                        split_heads(cq2)
                        hi(wl + 2 + i, 1)
                        continue
                    bank = A.take(act)
                    if dst is hv or dst is cv:
                        A.free(a_(dst[:, :, n * T:(n + 1) * T], bank[:, :].rearrange("p (a n) -> p a n", a=TT), ACT.Copy))
                    elif dst is gate:
                        st.lone(a_(gsig[:, n:n + 2, :], bank[:, :], ACT.Sigmoid))
                        A.free(a_(dst[:, n:n + 2, :], bank[:, :], ACT.Copy))
                    else:
                        A.free(a_(dst[:, n:n + 2, :], bank[:, :], ACT.Copy))
                    hi(wl + 2 + i, 1)
                st.settle()
                done["hybrid", l] = A.nc
                act.wait_ge(S["lam_in"], l + 1)
                st.say(a_(lam_t[:, 2:4], lam_t[:, 0:2], ACT.Exp, scale=-1.0), "lam_e")
                for dst, bias in ((lr, "gab"), (li, "gxb")):
                    bank = A.take(act)
                    st.lone(a_(dst[:, 0, :], bank[:, 0:T], ACT.Sigmoid, bias=col(bias, 2 * l)))
                    A.free(a_(dst[:, 1, :], bank[:, T:2 * T], ACT.Sigmoid, bias=col(bias, 2 * l + 1)))
                st.settle()
                act.wait_ge(A.freed, A.nc)
                act.wait_ge(S["lam_c"], l + 1)
                for c in range(2):
                    st.lone(a_(lt[:, c, :], lr[:, c, :], ACT.Tanh, scale=lam_t[:, 20 + c:21 + c]))
                for c in range(2):
                    ins = a_(la[:, c, :], lr[:, c, :], ACT.Exp, scale=lam_t[:, 20 + c:21 + c])
                    if c:
                        st.say(ins, "lru_a")
                    else:
                        st.lone(ins)
                act.wait_ge(S["lru_q"], l + 1)
                st.say(a_(lq, lq, ACT.Sqrt), "lru_s")
                attention((3 + l) * NH)
                act.wait_ge(S["stick_z"], l + 1)
                st.own(a_(zl, zb, ACT.Abs))
                st.own(a_(zl, zl, ACT.Exp, scale=-1.0))
                st.say(a_(zl, zl, ACT.Ln, bias=onecol), "stick_l")
                act.wait_ge(S["stick_arg"], l + 1)
                st.say(a_(zw, zw, ACT.Exp), "stick_w")
                act.wait_ge(S["y_ready"], 3 + l)
                operand_hi(yc_)
                for n in range(wl + N_IN2 + 2, min(wl + N_IN2 + 6, N_LATE)):
                    hi(n, 1)
            norm(7, 7)

        @block.vector
        def _(dve):
            st = Step(dve, sem("vector_step"))
            tt, ts, stt, cp = dve.tensor_tensor, dve.tensor_scalar, dve.scalar_tensor_tensor, dve.tensor_copy
            rstd = yc_[:, 0:T]

            st.lone(dve.memset(tiny[:, 130:131], EPS))
            st.lone(dve.memset(tiny[:, 131:132], GN_EPS))
            st.lone(dve.memset(tiny[:, 132:133], 1.0))
            st.lone(dve.memset(tiny[:, 133:134], 0.0))
            st.lone(dve.memset(zero16[:, :], 0.0))
            st.settle()
            st.say(dve.memset(tiny[:, 134:135], 0.0), "zero_ready")

            def norm(k, a_count, dst=None, name="u_ready"):
                dst = uT if dst is None else dst
                dve.wait_ge(A.freed, a_count)
                st.own(dve.reciprocal(rstd, rstd))
                for c in range(DC):
                    ins = stt(dst[:, c, :], hT[:, c, :], col("gains", k * DC + c), rstd, ALU.mult, ALU.mult)
                    if c == DC - 1:
                        st.say(ins, name)
                    elif c == DC // 2 - 1:
                        st.say(ins, "u_half")
                    else:
                        st.lone(ins)
                st.settle()

            def lo(n, late=0):
                dve.wait_ge(high[late], n + 1)
                tt(wlo[n % 2][:, :], slot(n), whi[n % 2][:, :].bitcast(F32), ALU.subtract).then_inc(split[late], 1)

            def operand_lo(src):
                for half in range(2):
                    cols = slice(half * 4 * T, (half + 1) * 4 * T)
                    dve.wait_ge(S["act_hi"], st.said.get("act_lo", 0) + 1)
                    st.say(tt(ulo_[:, cols], src[:, cols], uhi_[:, cols].bitcast(F32), ALU.subtract), "act_lo")

            def attention(n0, scale, mask, y0):
                m384 = C(mask)
                for i in range(NH + LAG + 2):
                    if i < NH:
                        bank = V.take(dve)
                        if i >= NL:
                            dve.wait_ge(A.filled, done["attention", n0] + i - NL + 1)
                        V.free(stt(Lg[i % NL], bank[:, 0:384], scale, m384, ALU.mult, ALU.add))
                        dve.wait_ge(V.freed, V.nc)
                        st.lone(dve.tensor_reduce(nmx[:, i, 0:1], Lg[i % NL][:, 0:P], AX_X, ALU.max, negate=True))
                        st.say(dve.tensor_reduce(nmx[:, i, 1:2], Lg[i % NL][:, P:384], AX_X, ALU.max, negate=True), "nmax_ready")
                    if 1 <= i <= NH:
                        dve.wait_ge(S["exp_done"], n0 + i)
                        st.say(dve.reciprocal(rz[:, i - 1, :], zsum[:, i - 1, :]), "rz_ready")
                    h = i - LAG
                    if h >= 2 and h % 2 == 0:
                        bank = V.take(dve)
                        V.free(cp(ycat[:, y0 + h // 2 - 1, :], bank[:, 0:T]))

            def rope(x, n, which, ta, tb, into=None):
                cos2, sin2 = [C(f"{f}_{which}").rearrange("p (o t) -> p o t", o=1).broadcast_to([P, 2, T]) for f in ("cos", "sin")]
                ta, tb = chunks(ta, 2), chunks(tb, 2)
                for c in range(0, n, 2):
                    bank = V.take(dve)
                    x2 = x[:, c:c + 2, :]
                    V.free(tt(ta, bank[:, :].rearrange("p (c t) -> p c t", c=2), sin2, ALU.mult))
                    st.own(tt(tb, x2, cos2, ALU.mult))
                    dve.wait_ge(V.freed, V.nc)
                    if into is None:
                        st.say(tt(x2, ta, tb, ALU.add), "rope_done")
                    else:
                        st.lone(tt(into[0:HD, 0, c:c + 2, :], ta[0:HD], tb[0:HD], ALU.add))
                        st.say(tt(into[HD:P, 1, c:c + 2, :], ta[HD:P], tb[HD:P], ALU.add), "rope_done")
                    st.wait_said("rope_done")

            def clear_halves(q2):
                st.lone(dve.memset(q2[HD:P, 0], 0.0))
                st.lone(dve.memset(q2[0:HD, 1], 0.0))

            def residual(ahead, late=0):
                for n in range(N_OUT):
                    if n:
                        lo_if(ahead + n - 1, late)
                    bank = V.take(dve)
                    ins = tt(hT[:, 2 * n:2 * n + 2, :], hT[:, 2 * n:2 * n + 2, :], bank[:, :], ALU.add)
                    V.free(ins)
                dve.wait_ge(V.freed, V.nc)
                st.say(dve.memset(tiny[:, 135:136], 0.0), "h_ready")
                lo_if(ahead + N_OUT - 1, late)

            def lo_if(n, late):
                if n < (N_LATE if late else N_EARLY):
                    lo(n, late)

            lo(0)
            lo(1)
            dve.wait_ge(loaded, 48)
            norm(0, done["norm", 0])
            operand_lo(uT_)
            for n in range(2, N_IN0):
                lo(n)

            dve.wait_ge(tables_loaded, 32)
            dve.wait_ge(A.freed, done["mla_std"])
            st.own(dve.reciprocal(std_m, std_m))
            st.own(dve.reciprocal(rt1[:, 0:T], rt1[:, 0:T]))
            st.lone(stt(qn[:, 0, :], qlat[:, 0, :], col("qnorm", 0), std_m, ALU.mult, ALU.mult))
            st.say(stt(qn[:, 1, :], qlat[:, 1, :], col("qnorm", 1), std_m, ALU.mult, ALU.mult), "mla_q")
            st.say(stt(kvn, kvl, col("kvnorm", 0), rt1[:, 0:T], ALU.mult, ALU.mult), "mla_kv")
            st.wait_said("mla_kv")
            bank = V.take(dve)
            V.free(tt(rt1[:, 0:T], bank[:, 0:T], C("sin_mla"), ALU.mult))
            st.own(tt(rt2[:, 0:T], kpe, C("cos_mla"), ALU.mult))
            dve.wait_ge(V.freed, V.nc)
            st.say(tt(kpe, rt1[:, 0:T], rt2[:, 0:T], ALU.add), "rope_done")
            st.wait_said("rope_done")
            kpe2 = kpe.rearrange("p (o t) -> p o t", o=1).broadcast_to([P, 2, T])
            for j2 in range(NH // 2):
                bank = V.take(dve)
                V.free(tt(kh[:, 2 * j2:2 * j2 + 2, :], bank[:, :].rearrange("p (c t) -> p c t", c=2), kpe2, ALU.add))
            dve.wait_ge(A.freed, done["mla"])
            rope(qh, NH, "mla", rt1, rt2)
            attention(0, (HD + 32) ** -0.5, "causal", GC)
            dve.wait_ge(V.freed, V.nc)

            st.lone(tt(rw[:, :, 1:T], raw[:, :, 0:T - 1], raw[:, :, 1:T], ALU.subtract))
            st.lone(ts(rw[:, :, 0:1], raw[:, :, 0:1], -1.0, None, ALU.mult))
            st.settle()
            for c in (12, 13) + tuple(range(12)):
                st.lone(stt(rw[:, c, :], rw[:, c, :], col("mu", c), raw[:, c, :], ALU.mult, ALU.add))
            st.settle()
            st.lone(dve.memset(lw[HD:P], 0.0))
            st.lone(dve.memset(lx[0:HD], 0.0))
            st.settle()
            st.say(dve.memset(tiny[:, 136:137], 0.0), "decay_in")
            r_, k_, v_ = rw[:, 0:4, :], rw[:, 4:8, :], rw[:, 8:12, :]
            for c in range(GC):
                ins = ts(kkr[:, c, :], rw[:, 4 + c, :], col("kkp", c), None, ALU.mult)
                if c == GC - 1:
                    st.say(ins, "kk_in")
                else:
                    st.lone(ins)
            st.lone(ts(omka, Pm("kap"), -1.0, 1.0, ALU.mult, ALU.add))
            st.settle()
            st.wait_said("kk_in")
            dve.wait_ge(A.freed, done["lora"])
            st.own(ts(logd, logd, -float(np.exp(-0.5)), None, ALU.mult))
            for c in range(GC):
                for a in range(TT):
                    st.lone(dve.tensor_tensor_scan(cs[:, c, a * P:(a + 1) * P], C("ones"), logd[:, c, a * P:(a + 1) * P],
                                                   0.0, ALU.mult, ALU.add))
            st.settle()
            cs8 = cs.rearrange("p c (a t) -> p (c a) t", a=TT)
            mid = tiny[:, 144:152]
            st.own(cp(mid, cs8[:, :, HD - 1:HD].rearrange("p n o -> p (n o)")))
            st.own(tt(cs8, cs8, mid.rearrange("p (n o) -> p n o", o=1).broadcast_to([P, 8, P]), ALU.subtract))
            st.say(tt(csx, cs, logd, ALU.subtract), "exp_in")
            st.own(tt(tiny[:, 140:144], cs[:, :, P - 1:P].rearrange("p c o -> p (c o)"),
                      mid.rearrange("p (c a) -> p c a", a=TT)[:, :, 1], ALU.add))
            st.say(dve.memset(tiny[:, 137:138], 0.0), "exp_in")
            for c in range(GC):
                st.lone(ts(bon[:, c, :], iclr[:, c, :], col("kap", c), omka[:, c:c + 1], ALU.mult, ALU.add))
            st.settle()
            dve.wait_ge(A.freed, done["kk"])
            st.own(tt(k2, k_, bon, ALU.mult))
            st.own(ts(kk, kk, 1e-12, None, ALU.max))
            st.own(dve.reciprocal(kk, kk))
            st.own(tt(kk, kk, kkr, ALU.mult))
            for c in range(GC):
                ins = stt(bon[:, c, :], rw[:, c, :], col("rkp", c), k2[:, c, :], ALU.mult, ALU.mult)
                if c == GC - 1:
                    st.say(ins, "bonus_in")
                else:
                    st.lone(ins)
            dve.wait_ge(S["exp_out"], 1)
            v4 = lambda x: x.rearrange("p c (a t) -> p c a t", a=TT)
            st.lone(tt(KR[:, :, :, 0, :], v4(kk), v4(E2), ALU.mult))
            st.lone(tt(KR[:, :, :, 1, :], v4(r_), v4(E1), ALU.mult))
            st.own(tt(Ks, k2, E3, ALU.mult))
            st.own(tt(Bs, kk, iclr, ALU.mult))
            st.own(tt(Bs, Bs, E3, ALU.mult))
            st.say(dve.memset(tiny[:, 138:139], 0.0), "keys_ready")
            for j2 in range(2):
                bank = V.take(dve)
                V.free(tt(csx[:, 2 * j2:2 * j2 + 2, :], v_[:, 2 * j2:2 * j2 + 2, :], bank[:, :], ALU.mult))

            idb = C("ident").rearrange("p (o s) -> p o s", o=1).broadcast_to([P, 4, P])
            for a in range(TT):
                if a:
                    dve.wait_ge(A.freed, done["y", 0])
                for h in range(NH):
                    bank = V.take(dve)
                    V.free(tt(AT[:, h].rearrange("p q s -> p (q s)"), bank[:, :], C("mask4"), ALU.mult))
                dve.wait_ge(V.freed, V.nc)
                for par_ in range(2):
                    hs = slice(par_, NH, 2)
                    bank = V.take(dve)
                    b3 = bank[:, :].rearrange("p (h s) -> p h s", h=4)
                    l1 = C("level1").rearrange("p (o s) -> p o s", o=1).broadcast_to([P, 4, P])
                    l1T = C("levelT1").rearrange("p (o s) -> p o s", o=1).broadcast_to([P, 4, P])
                    V.free(tt(Dm[:, hs, :], b3, l1, ALU.mult))
                    dve.wait_ge(V.freed, V.nc)
                    st.own(tt(Dm[:, hs, :], idb, Dm[:, hs, :], ALU.subtract))
                    st.own(tt(DmT[:, hs, :], AT[:, hs, 0, :], l1T, ALU.mult))
                    st.own(tt(DmT[:, hs, :], idb, DmT[:, hs, :], ALU.subtract))
                for n, m in enumerate(LEVELS):
                    lT = C(f"levelT{m}").rearrange("p (o s) -> p o s", o=1).broadcast_to([P, NH, P])
                    if n == 0:
                        st.say(tt(CTm[0], AT[:, :, 0, :], lT, ALU.mult), "level_ct")
                    if n + 1 < len(LEVELS):
                        lT = C(f"levelT{LEVELS[n + 1]}").rearrange("p (o s) -> p o s", o=1).broadcast_to([P, NH, P])
                        if n:
                            dve.wait_ge(A.freed, done["levels", a] + 2 * n)
                        st.say(tt(CTm[(n + 1) % 2], AT[:, :, 0, :], lT, ALU.mult), "level_ct")
                    for h4 in range(2):
                        hs = slice(4 * h4, 4 * h4 + 4)
                        if m != LEVELS[-1]:
                            b1 = V.take(dve)
                            V.free(tt(Dm[:, hs, :], Dm[:, hs, :], b1[:, :].rearrange("p (h s) -> p h s", h=4), ALU.subtract))
                        b2 = V.take(dve)
                        V.free(tt(DmT[:, hs, :], DmT[:, hs, :], b2[:, :].rearrange("p (h s) -> p h s", h=4), ALU.subtract))
                    dve.wait_ge(V.freed, V.nc)
                if a == 0:
                    bank = V.take(dve)
                    dve.wait_ge(S["exp_out"], 1)
                    for c in range(GC):
                        ins = stt(Sbd[:, c, :], bank[:, c * P:(c + 1) * P], fend[:, c:c + 1], C("same_head"), ALU.mult, ALU.mult)
                        if c == GC - 1:
                            V.free(ins)
                        else:
                            st.lone(ins)
                    st.settle()
                    dve.wait_ge(V.freed, V.nc)
                    st.say(dve.memset(tiny[:, 139:140], 0.0), "state_ready")
            dve.wait_ge(A.freed, done["y", 1])
            for j2 in range(2):
                bank = V.take(dve)
                y2 = yT[:, 2 * j2:2 * j2 + 2, :]
                V.free(stt(y2, bank[:, :].rearrange("p (j t) -> p j t", j=2), -1.0 / HD, y2, ALU.mult, ALU.add))
            dve.wait_ge(V.freed, V.nc)
            st.say(dve.memset(tiny[:, 152:153], 0.0), "gn_in")
            dve.wait_ge(A.freed, done["gn"])
            st.own(dve.reciprocal(cs, cs))
            st.own(tt(yT, yT, cs, ALU.mult))
            for c in range(GC):
                st.lone(ts(yT[:, c, :], yT[:, c, :], col("lnxg", c), col("lnxb", c), ALU.mult, ALU.add))
            st.settle()
            st.own(tt(yT, yT, csx, ALU.add))
            st.own(tt(ycat[:, 0:GC, :], yT, g_, ALU.mult))
            st.say(dve.memset(tiny[:, 153:154], 0.0), "y_ready")
            lo(N_IN0)
            lo(N_IN0 + 1)
            operand_lo(yc_)
            residual(N_IN0 + 2)

            norm(1, done["norm", 1])
            operand_lo(uT_)

            def loop_lo(k, ahead, bufs):
                dve.wait_ge(high[0], ahead + (k + 1))
                tt(wlo[k % bufs][:, :], slot(k), whi[k % bufs][:, :].bitcast(F32), ALU.subtract).then_inc(split[0], 1)

            def ffn_step(s, n):
                dve.wait_ge(S["ffn_sig"], n)
                tt(gtmp[s], sigb[s], banks[s][:, :], ALU.mult).then_inc(S["ffn_mid"], 1)
                dve.wait_ge(S["ffn_mid"], n)
                tt(hf[s], gtmp[s], banks[2 + s][:, :], ALU.mult).then_inc(S["ffn_h"], 1)
                dve.wait_ge(S["ffn_h"], n)
                cp(hhi[s][:, :], hf[s]).then_inc(S["ffn_hh"], 1)
                dve.wait_ge(S["ffn_hh"], n)
                tt(hlo[s][:, :], hf[s], hhi[s][:, :].bitcast(F32), ALU.subtract).then_inc(S["ffn_hid"], 1)

            w0 = N_IN0 + N_OUT
            with dve.Fori(0, FFN_STEPS // 2) as it:
                for s in range(2):
                    k = w0 + 2 + 3 * s
                    loop_lo(k, it * 6, 2)
                    ffn_step(s, it * 2 + (s + 1))
                    loop_lo(k + 1, it * 6, 2)
                    loop_lo(k + 2, it * 6, 2)
            ffn_step(0, FFN_STEPS)
            w1 = w0 + N_FFN
            lo(w1 - 1)
            lo(w1)
            dve.wait_ge(S["ffn_down"], FFN_STEPS + 1)
            for n in range(4):
                st.lone(tt(hT[:, 2 * n:2 * n + 2, :], hT[:, 2 * n:2 * n + 2, :], banks[4 + n][:, :], ALU.add))
            st.settle()
            st.say(dve.memset(tiny[:, 154:155], 0.0), "h_ready")

            lo(w1 + 1)
            clear_halves(fq2)
            clear_halves(mq2)
            st.say(dve.memset(fnd, 0.0), "zero_ready")
            norm(2, done["norm", 2])
            operand_lo(uT_)
            for n in range(w1 + 2, w1 + N_IN1 + 2):
                lo(n)
            bank = V.take(dve)
            z8 = fz[0:NH]
            V.free(ts(z8, bank[0:NH, 0:T], par[0:NH, par_at["foxbf"][0]:par_at["foxbf"][0] + 1], None, ALU.add))
            dve.wait_ge(V.freed, V.nc)
            st.own(ts(fe[0:NH], z8, -1.0, None, ALU.mult))
            st.say(tt(fl[0:NH], fe[0:NH], z8, ALU.max), "fox_z")
            st.own(ts(z8, z8, 0.0, None, ALU.min))
            dve.wait_ge(S["fox_e"], 1)
            st.own(tt(z8, z8, fe[0:NH], ALU.subtract))
            st.own(ts(fl[0:NH], z8, 0.0, 1.0, ALU.mult, ALU.add))
            st.wait_said("zero_ready")
            st.own(dve.tensor_tensor_scan(fd[0:NH], fl[0:NH], z8, 0.0, ALU.mult, ALU.add))
            st.say(ts(fnd[0:NH], fd[0:NH], -1.0, None, ALU.mult), "fox_d")
            dve.wait_ge(A.freed, done["l1"])
            rope(mq, GC, "full", r1a, r1b, mq2)
            rope(mk, GC, "full", r1a, r1b)
            attention(NH, HD ** -0.5, "causal", 0)
            attention(2 * NH, HD ** -0.5, "causal", GC)
            dve.wait_ge(V.freed, V.nc)
            st.say(dve.memset(tiny[:, 155:156], 0.0), "y_ready")
            operand_lo(yc_)
            residual(w1 + N_IN1 + 2)

            norm(3, done["norm", 3])
            bank = V.take(dve)
            V.free(cp(lg, bank[:, 0:TT * E]))
            dve.wait_ge(V.freed, V.nc)
            l3 = lg.rearrange("p (a e) -> p a e", a=TT)
            m3 = lambda x: x.rearrange("p (a o) -> p a o", o=1).broadcast_to([P, TT, E])
            st.own(dve.tensor_reduce(m0, l3, AX_X, ALU.max))
            st.say(tt(ex.rearrange("p (a e) -> p a e", a=TT), l3, m3(m0), ALU.subtract), "router_l")
            low = C("lower").rearrange("p (e j) -> p e j", e=E)
            for a in range(TT):
                la_ = lg[:, a * E:(a + 1) * E]
                lj = la_.rearrange("p (o j) -> p o j", o=1).broadcast_to([P, E, E])
                le = la_.rearrange("p (e o) -> p e o", o=1).broadcast_to([P, E, E])
                b1 = big[:, a * E * E:(a + 1) * E * E].rearrange("p (e j) -> p e j", e=E)
                b2 = big2[:, a * E * E:(a + 1) * E * E].rearrange("p (e j) -> p e j", e=E)
                st.lone(tt(b1, lj, le, ALU.is_gt))
                st.own(tt(b2, lj, le, ALU.is_equal))
                st.own(tt(b2, b2, low, ALU.mult))
                st.own(tt(b1, b1, b2, ALU.add))
                st.own(dve.tensor_reduce(rank[:, a * E:(a + 1) * E], b1, AX_X, ALU.add))
            st.say(ts(selm, rank, 1.5, None, ALU.is_lt), "router_sel")
            st.wait_said("router_sel")
            dve.wait_ge(S["router_e"], 1)
            st.own(tt(comb, ex, selm, ALU.mult))
            c3 = comb.rearrange("p (a e) -> p a e", a=TT)
            st.own(dve.tensor_reduce(den, c3, AX_X, ALU.add))
            st.own(dve.reciprocal(den, den))
            st.own(tt(c3, c3, m3(den), ALU.mult))
            bank = V.take(dve)
            st.lone(cp(posm, bank[:, 0:2 * E]))
            V.free(cp(cnt, bank[:, 2 * E:3 * E]))
            st.settle()
            dve.wait_ge(V.freed, V.nc)
            st.own(ts(rank, selm, -1e4, 1e4, ALU.mult, ALU.add))
            st.own(tt(posm, posm, rank, ALU.add))
            for a in range(TT):
                st.lone(cp(table[:, 0:E, a], posm[:, a * E:(a + 1) * E]))
                st.lone(ts(table[:, E:2 * E, a], posm[:, a * E:(a + 1) * E], -float(P), None, ALU.add))
                st.lone(cp(table[:, 0:E, 2 + a], comb[:, a * E:(a + 1) * E]))
                st.lone(cp(table[:, E:2 * E, 2 + a], comb[:, a * E:(a + 1) * E]))
            st.lone(dve.memset(table[:, 2 * E:2 * E + 1, :], -1.0))
            st.own(dve.tensor_reduce(mcnt[:, 0:1], cnt, AX_X, ALU.max))
            st.own(ts(mcnt[:, 1:2], mcnt[:, 0:1], P + 0.5, 1.0, ALU.is_gt, ALU.add))
            cp(passes_i[:, :], mcnt[:, 1:2]).then_inc(flag_ready, 1)
            dve.wait_ge(flag_ready, 1)
            passes = dve.value_load(passes_i[0:1, 0:1], min_val=1, max_val=2)
            k0 = N_EARLY

            def choose(expert, count):
                cp(cur, table[:, bass.ds(expert, 1), :].rearrange("p o k -> p (o k)")).then_inc(S["moe_tab"], 1)
                dve.wait_ge(S["moe_tab"], count)
                ts(oh[:, 0, :], C("slot_iota"), cur[:, 0:1], None, ALU.is_equal).then_inc(S["moe_vec"], 1)
                ts(oh[:, 1, :], C("slot_iota"), cur[:, 1:2], None, ALU.is_equal).then_inc(S["onehot"], 1)

            def gathered(count):
                dve.wait_ge(S["moe_xh"], count)
                tt(ulo_[:, 0:512], banks[6][:, :], uhi_[:, 0:512].bitcast(F32), ALU.subtract).then_inc(S["moe_vec"], 1)
                tt(ulo_[:, 512:1024], banks[7][:, :], uhi_[:, 512:1024].bitcast(F32), ALU.subtract).then_inc(S["moe_x"], 1)

            choose(0, 1)
            loop_lo(k0, 0, 3)
            loop_lo(k0 + 1, 0, 3)
            gathered(1)
            with dve.Fori(0, passes) as ps:
                with dve.Fori(0, E) as e:
                    ex_n = dve.snap(ps * E + e)
                    dve.wait_ge(S["onehot"], ex_n + 1)
                    ts(ohg[:, 0, :], oh[:, 0, :], cur[:, 2:3], None, ALU.mult).then_inc(S["moe_vec"], 1)
                    ts(ohg[:, 1, :], oh[:, 1, :], cur[:, 3:4], None, ALU.mult).then_inc(S["onehot_g"], 1)

                    slots_n = dve.snap(ex_n * MOE_SLOTS)
                    steps_n = dve.snap(ex_n * MOE_STEPS)
                    loop_lo(k0 + 2, slots_n, 3)

                    def hidden(steps_, s):
                        n, h = steps_ + (s + 1), s % 2
                        dve.wait_ge(S["moe_sig"], n)
                        tt(gtmp[h][:, 0:T], sigb[h][:, 0:T], banks[h][:, 0:T], ALU.mult).then_inc(S["moe_mid"], 1)
                        dve.wait_ge(S["moe_mid"], n)
                        tt(hf[h][:, 0:T], gtmp[h][:, 0:T], banks[h][:, T:2 * T], ALU.mult).then_inc(S["moe_h"], 1)

                    def hidden_low(steps_, s):
                        n, h = steps_ + (s + 1), s % 2
                        dve.wait_ge(S["moe_hh"], n)
                        tt(hlo[h][:, 0:T], banks[3][:, 0:T], hhi[h][:, 0:T].bitcast(F32), ALU.subtract).then_inc(S["moe_hid"], 1)

                    with dve.Fori(0, (MOE_STEPS - 2) // 2) as it:
                        slots_i = dve.snap(slots_n + it * 6)
                        steps_i = dve.snap(steps_n + it * 2)
                        for s in range(2):
                            hidden(steps_i, s)
                            loop_lo(k0 + 3 + 3 * s, slots_i, 3)
                            loop_lo(k0 + 4 + 3 * s, slots_i, 3)
                            hidden_low(steps_i, s)
                            loop_lo(k0 + 5 + 3 * s, slots_i, 3)
                    hidden(steps_n, MOE_STEPS - 2)
                    loop_lo(k0 + MOE_SLOTS - 3, slots_n, 3)
                    choose(ex_n + 1, ex_n + 2)
                    loop_lo(k0 + MOE_SLOTS - 2, slots_n, 3)
                    hidden_low(steps_n, MOE_STEPS - 2)
                    hidden(steps_n, MOE_STEPS - 1)
                    loop_lo(k0 + MOE_SLOTS - 1, slots_n, 3)
                    hidden_low(steps_n, MOE_STEPS - 1)
                    loop_lo(k0 + MOE_SLOTS, slots_n, 3)
                    gathered(ex_n + 2)
                    loop_lo(k0 + MOE_SLOTS + 1, slots_n, 3)
                    for c2 in range(4):
                        bank = banks[c2]
                        dve.wait_ge(S["moe_sc"], ex_n * 4 + (c2 + 1))
                        tt(hT[:, 2 * c2:2 * c2 + 2, :], hT[:, 2 * c2:2 * c2 + 2, :], bank[:, :], ALU.add).then_inc(S["moe_add"], 1)
            st.say(dve.memset(tiny[:, 160:161], 0.0), "moe_end")
            st.say(dve.memset(tiny[:, 156:157], 0.0), "h_ready")

            lo(0, 1)
            lo(1, 1)
            norm(4, done["norm", 4], dst=hT, name="u_ready")
            st.wait_said("u_ready")
            st.say(dve.memset(tiny[:, 157:158], 0.0), "h_ready")
            for l in range(2):
                clear_halves(cq2)
                norm(5 + l, done["norm", 5 + l])
                wl = l * (N_IN2 + N_OUT)
                operand_lo(uT_)
                for n in range(wl + 2, wl + N_IN2 + 2):
                    lo(n, 1)
                lam = Pm("lam")[:, 2 * l:2 * l + 2]
                L = lambda i: lam_t[:, 2 * i:2 * i + 2]
                st.own(ts(L(2), lam, -1.0, None, ALU.mult))
                st.say(tt(L(0), L(2), lam, ALU.max), "lam_in")
                dve.wait_ge(S["lam_e"], l + 1)
                st.own(ts(L(3), L(1), 2.0, None, ALU.add))
                st.own(dve.reciprocal(L(3), L(3)))
                st.own(tt(L(3), L(3), L(1), ALU.mult))
                st.own(tt(L(4), L(3), L(3), ALU.mult))
                st.own(ts(L(5), L(4), 1.0 / 17, 1.0 / 15, ALU.mult, ALU.add))
                for k in (13, 11, 9, 7, 5, 3, 1):
                    st.own(tt(L(5), L(5), L(4), ALU.mult))
                    st.own(ts(L(5), L(5), 1.0 / k, None, ALU.add))
                st.own(tt(L(5), L(5), L(3), ALU.mult))
                st.own(ts(L(6), lam, 0.0, None, ALU.min))
                st.own(stt(L(6), L(5), -2.0, L(6), ALU.mult, ALU.add))
                st.say(ts(L(10), L(6), 8.0, None, ALU.mult), "lam_c")
                dve.wait_ge(A.freed, done["hybrid", l])
                for c in range(2):
                    w = lambda j: col("convw", (2 * l + c) * 4 + j)
                    st.own(ts(xc[:, c, :], bx[:, c, :], w(3), col("convb", 2 * l + c), ALU.mult, ALU.add))
                    for j in range(3):
                        sh = 3 - j
                        st.own(stt(xc[:, c, sh:T], bx[:, c, 0:T - sh], w(j), xc[:, c, sh:T], ALU.mult, ALU.add))
                st.say(tt(gate, gate, gsig, ALU.mult), "conv_done")
                st.wait_said("conv_done")
                clear_halves(hq2)
                st.settle()
                rope(hq, GC, "part", hra, hrb, hq2)
                rope(hk, GC, "part", hra, hrb)
                dve.wait_ge(S["lru_a"], l + 1)
                st.own(ts(lq, lt, -1.0, 1.0, ALU.mult, ALU.add))
                st.own(dve.reciprocal(lq, lq))
                st.say(stt(lq, lt, -2.0, lq, ALU.mult, ALU.mult), "lru_q")
                st.own(tt(lu, li, xc, ALU.mult))
                dve.wait_ge(S["lru_s"], l + 1)
                st.own(tt(lu, lu, lq, ALU.mult))
                for c in range(2):
                    st.lone(dve.tensor_tensor_scan(ycat[:, GC + c, :], la[:, c, :], lu[:, c, :], 0.0, ALU.mult, ALU.add))
                attention((3 + l) * NH, HD ** -0.5, "dilated", 0)
                for h in range(4):
                    bank = V.take(dve)
                    V.free(ts(zb[:, h, :], bank[:, 0:384], HD ** -0.5, None, ALU.mult))
                dve.wait_ge(V.freed, V.nc)
                st.say(dve.memset(tiny[:, 158:159], 0.0), "stick_z")
                dve.wait_ge(S["stick_l"], l + 1)
                st.own(stt(zl, zb, 0.0, zl, ALU.max, ALU.add))
                m01 = C("stick01").rearrange("p (o n) -> p o n", o=1).broadcast_to([P, 4, 384])
                madd = C("stick_add").rearrange("p (o n) -> p o n", o=1).broadcast_to([P, 4, 384])
                st.say(tt(zl, zl, m01, ALU.mult), "stick_n")
                st.own(tt(zb, zb, madd, ALU.add))
                for h in range(4):
                    bank = V.take(dve)
                    V.free(tt(zw[:, h, :], zb[:, h, :], bank[:, 0:384], ALU.add))
                dve.wait_ge(V.freed, V.nc)
                st.say(dve.memset(tiny[:, 159:160], 0.0), "stick_arg")
                for c in range(2):
                    bank = V.take(dve)
                    V.free(cp(ycat[:, GC + 2 + c, :], bank[:, 0:T]))
                dve.wait_ge(V.freed, V.nc)
                st.settle()
                st.wait_said("conv_done")
                st.say(tt(ycat, ycat, gate, ALU.mult), "y_ready")
                operand_lo(yc_)
                residual(wl + N_IN2 + 2, 1)
            norm(7, done["norm", 7], name="out_ready")

        @block.gpsimd
        def _(pool):
            st = Step(pool, sem("pool_step"))
            for n in range(5 * NH):
                i = n % NH
                pool.wait_ge(S["rz_ready"], n + 1)
                st.lone(pool.tensor_scalar(Lg[i % NL][:, 0:P], Lg[i % NL][:, 0:P], rz[:, i, 0:1], 1.0, ALU.mult, ALU.mult))
                st.say(pool.tensor_scalar(Lg[i % NL][:, P:384], Lg[i % NL][:, P:384], rz[:, i, 1:2], 1.0, ALU.mult, ALU.mult), "prob_ready")



def kernel(**inputs):
    import concourse.bacc as bacc
    from concourse.bass_utils import run_bass_kernel_spmd

    w = {k: np.asarray(v) for k, v in inputs.items()}

    def feature_major(v):
        return v.reshape(-1, P).T

    def slots(m):
        return m.reshape(DC, P, -1, SLOT_COLS).transpose(2, 1, 0, 3).reshape(-1, P, SLOT)

    def down_slots(m):
        return m.reshape(-1, 2, P, D).transpose(0, 2, 1, 3).reshape(-1, P, SLOT)

    def swiglu_slots(g, u, d):
        g, u, d = slots(g), slots(u), down_slots(d)
        order = [g[0], u[0]]
        for i in range(1, len(g)):
            order += [g[i], u[i], d[i - 1]]
        return np.stack(order + [d[-1]])

    w_in0 = w["w_in_0"]
    w_in0 = np.concatenate([w_in0[:, :1792 + 256 + 128], np.pad(w_in0[:, 1792 + 384:], ((0, 0), (HD, 32)))], 1)
    w_in1 = w["w_in_1"]
    stream = [slots(w_in0), slots(w["w_out_0"]),
              swiglu_slots(w["ffn_wg_0"], w["ffn_wu_0"], w["ffn_wd_0"]),
              slots(w_in1[:, :3 * GW]), slots(w_in1[:, 3 * GW + NH:]), slots(w["w_out_1"])]
    stream += [swiglu_slots(w["moe_wg_1"][e], w["moe_wu_1"][e], w["moe_wd_1"][e]) for e in range(E)]
    for l in range(2):
        stream += [slots(w["w_in_2"][l]), slots(w["w_out_2"][l])]
    stream = np.concatenate(stream)

    def uq():
        m = np.pad(w["mla_wuq_0"].reshape(256, NH, 96), ((0, 0), (0, 0), (0, 32)))
        return m.reshape(2, P, NH * P).transpose(1, 0, 2).reshape(P, -1)

    def ukv():
        m = w["mla_wukv_0"].reshape(P, NH, 128)
        k = np.pad(m[:, :, :64], ((0, 0), (0, 0), (0, 64)))
        return np.concatenate([k.reshape(P, NH * P), m[:, :, 64:].reshape(P, GW)], 1)

    def block_diagonal(m):
        out = np.zeros((P, 2, 2, P), np.float32)
        for l in range(2):
            for n in range(4):
                h = n % 2
                out[h * 64:h * 64 + 64, l, n // 2, h * 64:h * 64 + 64] = m[l, n]
        return out.reshape(P, -1)

    def rows(m):
        return m.reshape(DC, P, -1).transpose(1, 0, 2).reshape(P, -1)

    bf = np.zeros((P, 1), np.float32)
    bf[:NH, 0] = w["fox_bf_1"]
    gains = np.concatenate([w["norm_mix_0"], w["norm_ffn_0"], w["norm_mix_1"], w["norm_ffn_1"],
                            w["final_norm"], w["norm_gain_2"].reshape(-1), w["final_gain_2"]])
    small = dict(
        gains=feature_major(gains), mu=feature_major(w["shift_mu_0"]), w0=feature_major(w["rw_w0_0"]),
        a0=feature_major(w["rw_a0_0"]), kkp=feature_major(w["rw_kk_0"]), kap=feature_major(w["rw_ka_0"]),
        rkp=feature_major(w["rw_rk_0"]), lnxg=feature_major(w["rw_lnx_g_0"]), lnxb=feature_major(w["rw_lnx_b_0"]),
        qnorm=feature_major(w["mla_qnorm_0"]), kvnorm=feature_major(w["mla_kvnorm_0"]),
        wa2=np.concatenate([w["rw_w2_0"], w["rw_a2_0"]]), g2=w["rw_g2_0"], wuq=uq(), wukv=ukv(),
        foxbf=bf, wf=rows(w_in1[:, 3 * GW:3 * GW + NH]), router=rows(w["router_1"]),
        convw=w["conv_w_2"].reshape(2, 4, 2, P).transpose(3, 0, 2, 1).reshape(P, -1),
        convb=feature_major(w["conv_b_2"]), gab=feature_major(w["gate_a_b_2"]), gxb=feature_major(w["gate_x_b_2"]),
        lam=feature_major(w["lru_lambda_2"]), gaw=block_diagonal(w["gate_a_w_2"]), gxw=block_diagonal(w["gate_x_w_2"]))
    params = np.concatenate([small[k] for k in PARAMS], 1)
    assert params.shape[1] == sum(PARAMS.values())

    consts = shape_constants()
    const_at, at = {}, 0
    for k, v in consts.items():
        const_at[k] = (at, v.shape[1])
        at += v.shape[1]
    arrays = {
        "x_dram": rows(w["x"][0].T), "const_dram": np.concatenate(list(consts.values()), 1),
        "param_dram": params, "w_dram": stream,
    }
    nc = bacc.Bacc("TRN2", target_bir_lowering=False, num_devices=1)
    arrays = {k: np.ascontiguousarray(v) for k, v in arrays.items()}
    args = [nc.dram_tensor(k, v.shape, F32, kind="ExternalInput").ap() for k, v in arrays.items()]
    out = nc.dram_tensor("out_dram", (P, DC * T), F32, kind="ExternalOutput").ap()
    program(nc, *args, out, const_at)
    r = run_bass_kernel_spmd(nc, [arrays], core_ids=[0])
    y = r.results[0]["out_dram"]
    return np.ascontiguousarray(y.reshape(P, DC, T).transpose(2, 1, 0).reshape(1, T, D))
```
